# Optimizing a Trainium2 kernel written in Bass

```python
import math
import jax
import jax.numpy as jnp
from jax import lax
import numpy as np

D_MODEL = 1024
BATCH = 1
SEQ = 512
DEPTH = 1

MIX_WIDTH = D_MODEL
HEAD_DIM = 64
ATT_WIDTH = MIX_WIDTH // 2
ATT_HEADS = ATT_WIDTH // HEAD_DIM
IDX_HEADS = 4
IDX_DIM = HEAD_DIM
TOPK_MAX = 256
Q_BLOCK = 128
ROPE_THETA = 10000.0
INDEXER_SCALE = (IDX_HEADS ** -0.5) * (IDX_DIM ** -0.5)
SSD_WIDTH = MIX_WIDTH - ATT_WIDTH
SSD_HEAD_DIM = 64
SSD_HEADS = SSD_WIDTH // SSD_HEAD_DIM
SSD_GROUPS = 2
D_STATE = 64
CONV_WIDTH = 4
CONV_CH = SSD_WIDTH + 2 * SSD_GROUPS * D_STATE
CHUNK = 128
N_GROUPS_MOE = 4
EXPERTS_PER_GROUP = 4
N_EXPERTS = N_GROUPS_MOE * EXPERTS_PER_GROUP
TOP_K_IN_GROUP = 2
EXPERT_FF = 256
ALPHA = (2 * DEPTH) ** 0.25
BETA = (8 * DEPTH) ** -0.25
LN_EPS = 1e-5
IN_SPLIT_SIZES = (ATT_WIDTH, HEAD_DIM, HEAD_DIM, IDX_HEADS * IDX_DIM, IDX_DIM, IDX_HEADS, SSD_WIDTH, CONV_CH, SSD_HEADS)
IN_WIDTH = sum(IN_SPLIT_SIZES)
IN_SPLIT_POINTS = tuple(int(v) for v in np.cumsum(IN_SPLIT_SIZES)[:-1])


def layer_norm(x, g, b):
    xf = x.astype(jnp.float32)
    mu = jnp.mean(xf, -1, keepdims=True)
    var = jnp.mean(jnp.square(xf - mu), -1, keepdims=True)
    return ((xf - mu) * lax.rsqrt(var + LN_EPS)).astype(x.dtype) * g + b

def rope_tables(seq_len):
    inv = ROPE_THETA ** (-jnp.arange(0, HEAD_DIM, 2, dtype=jnp.float32) / HEAD_DIM)
    ang = jnp.arange(seq_len, dtype=jnp.float32)[:, None] * inv[None, :]
    return jnp.cos(ang), jnp.sin(ang)

def apply_rope(x, cos, sin):
    half = x.shape[-1] // 2
    x1, x2 = x[..., :half], x[..., half:]
    cos = cos.astype(x.dtype)
    sin = sin.astype(x.dtype)
    return jnp.concatenate([x1 * cos - x2 * sin, x1 * sin + x2 * cos], -1)

def dsa_attention(q, k, v, iq, ik, iw, topk):
    bsz, s, h, dh = q.shape
    n_blocks = s // Q_BLOCK
    key_pos = jnp.arange(s)

    def block(i):
        t0 = i * Q_BLOCK
        qb = lax.dynamic_slice_in_dim(q, t0, Q_BLOCK, 1)
        iqb = lax.dynamic_slice_in_dim(iq, t0, Q_BLOCK, 1)
        iwb = lax.dynamic_slice_in_dim(iw, t0, Q_BLOCK, 1)
        qpos = t0 + jnp.arange(Q_BLOCK)
        causal = key_pos[None, :] <= qpos[:, None]
        sc = jax.nn.relu(jnp.einsum('bthd,bsd->bths', iqb, ik))
        sc = jnp.einsum('bths,bth->bts', sc, iwb).astype(jnp.float32)
        sc = jnp.where(causal[None], sc, -jnp.inf)
        _, sel = lax.top_k(sc, topk)
        valid = sel <= qpos[None, :, None]
        k_sel = jax.vmap(lambda a, idx: a[idx])(k, sel)
        v_sel = jax.vmap(lambda a, idx: a[idx])(v, sel)
        logits = jnp.einsum('bthd,btkd->bthk', qb, k_sel).astype(jnp.float32) * (dh ** -0.5)
        logits = jnp.where(valid[:, :, None, :], logits, -jnp.inf)
        p = jax.nn.softmax(logits, -1).astype(v.dtype)
        return jnp.einsum('bthk,btkd->bthd', p, v_sel)

    out = lax.map(block, jnp.arange(n_blocks))
    return jnp.moveaxis(out, 0, 1).reshape(bsz, s, h * dh)

def causal_depthwise_conv(u, w, b):
    out = lax.conv_general_dilated(
        u, w[:, None, :].astype(u.dtype), window_strides=(1,),
        padding=[(CONV_WIDTH - 1, 0)], dimension_numbers=('NWC', 'WIO', 'NWC'),
        feature_group_count=u.shape[-1])
    return out + b

def segsum(a):
    t = a.shape[-1]
    ar = jnp.broadcast_to(a[..., :, None], a.shape + (t,))
    strict = jnp.tril(jnp.ones((t, t), dtype=bool), -1)
    cs = jnp.cumsum(jnp.where(strict, ar, 0.0), axis=-2)
    return jnp.where(jnp.tril(jnp.ones((t, t), dtype=bool)), cs, -jnp.inf)

def ssd_chunked(xdt, adt, bm, cm):
    b, s, h, p = xdt.shape
    n = bm.shape[-1]
    c = s // CHUNK
    X = xdt.reshape(b, c, CHUNK, h, p)
    Bc = bm.reshape(b, c, CHUNK, h, n)
    Cc = cm.reshape(b, c, CHUNK, h, n)
    A = adt.reshape(b, c, CHUNK, h).transpose(0, 3, 1, 2)
    a_cum = jnp.cumsum(A, -1)
    Lmat = jnp.exp(segsum(A))
    y_diag = jnp.einsum('bclhn,bcshn,bhcls,bcshp->bclhp', Cc, Bc, Lmat, X)
    decay_states = jnp.exp(a_cum[..., -1:] - a_cum)
    chunk_states = jnp.einsum('bclhn,bhcl,bclhp->bchpn', Bc, decay_states, X)
    chunk_decay = jnp.exp(a_cum[..., -1])

    def step(carry, inp):
        st, dec = inp
        return carry * dec[..., None, None] + st, carry

    init = jnp.zeros((b, h, p, n), X.dtype)
    _, prev = lax.scan(step, init, (jnp.moveaxis(chunk_states, 1, 0), jnp.moveaxis(chunk_decay, 2, 0)))
    prev = jnp.moveaxis(prev, 0, 1)
    y_off = jnp.einsum('bclhn,bchpn,bhcl->bclhp', Cc, prev, jnp.exp(a_cum))
    return (y_diag + y_off).reshape(b, s, h, p)

def ssd_mixer(z, xbc, dt_raw, conv_w, conv_b, dt_bias, a_log, d_skip, norm_w):
    bsz, s, _ = xbc.shape
    f32 = jnp.float32
    xbc = jax.nn.silu(causal_depthwise_conv(xbc, conv_w, conv_b))
    gn = SSD_GROUPS * D_STATE
    xs = xbc[..., :SSD_WIDTH].reshape(bsz, s, SSD_HEADS, SSD_HEAD_DIM).astype(f32)
    bm = xbc[..., SSD_WIDTH:SSD_WIDTH + gn].reshape(bsz, s, SSD_GROUPS, D_STATE)
    cm = xbc[..., SSD_WIDTH + gn:].reshape(bsz, s, SSD_GROUPS, D_STATE)
    rep = SSD_HEADS // SSD_GROUPS
    bm = jnp.repeat(bm, rep, axis=2).astype(f32)
    cm = jnp.repeat(cm, rep, axis=2).astype(f32)
    dt = jax.nn.softplus(dt_raw.astype(f32) + dt_bias.astype(f32))
    a = -jnp.exp(a_log.astype(f32))
    y = ssd_chunked(xs * dt[..., None], dt * a, bm, cm)
    y = y + d_skip.astype(f32)[:, None] * xs
    y = y.reshape(bsz, s, SSD_WIDTH) * jax.nn.silu(z.astype(f32))
    y = y * lax.rsqrt(jnp.mean(jnp.square(y), -1, keepdims=True) + LN_EPS)
    return y.astype(z.dtype) * norm_w

def hier_moe(h, w_rg, b_rg, w_re, b_re, w_gate, w_up, w_down):
    bsz, s, _ = h.shape
    f32 = jnp.float32
    p_group = jax.nn.softmax((h @ w_rg + b_rg).astype(f32), -1)
    g_idx = jnp.argmax(p_group, -1)
    g_prob = jnp.max(p_group, -1)
    e_logits = (h @ w_re + b_re).astype(f32).reshape(bsz, s, N_GROUPS_MOE, EXPERTS_PER_GROUP)
    e_in_group = jnp.take_along_axis(e_logits, g_idx[..., None, None], axis=2)[..., 0, :]
    top_logits, top_idx = lax.top_k(e_in_group, TOP_K_IN_GROUP)
    top_w = jax.nn.softmax(top_logits, -1) * g_prob[..., None]
    expert_id = g_idx[..., None] * EXPERTS_PER_GROUP + top_idx
    gates = jnp.sum(jax.nn.one_hot(expert_id, N_EXPERTS, dtype=f32) * top_w[..., None], axis=-2).astype(h.dtype)
    y = jnp.zeros_like(h)
    for e in range(N_EXPERTS):
        hid = jax.nn.silu(h @ w_gate[e]) * (h @ w_up[e])
        y = y + gates[..., e:e + 1] * (hid @ w_down[e])
    return y

def first_inputs(seed: int = 0) -> dict:
    key = jax.random.key(seed)
    ks = jax.random.split(key, 21)
    f32 = jnp.float32

    def nrm(k, shape, scale):
        return jax.random.normal(k, shape, f32) * scale

    x = nrm(ks[0], (BATCH, SEQ, D_MODEL), 1.0)
    w_in = nrm(ks[1], (DEPTH, D_MODEL, IN_WIDTH), D_MODEL ** -0.5)
    conv_w = nrm(ks[2], (DEPTH, CONV_WIDTH, CONV_CH), CONV_WIDTH ** -0.5)
    conv_b = nrm(ks[3], (DEPTH, CONV_CH), 0.02)
    dt0 = jnp.exp(jax.random.uniform(ks[4], (DEPTH, SSD_HEADS), f32, math.log(1e-3), math.log(1e-1)))
    dt_bias = dt0 + jnp.log(-jnp.expm1(-dt0))
    a_log = jnp.log(jax.random.uniform(ks[5], (DEPTH, SSD_HEADS), f32, 1.0, 16.0))
    d_skip = 1.0 + nrm(ks[6], (DEPTH, SSD_HEADS), 0.1)
    ssd_norm_w = 1.0 + nrm(ks[7], (DEPTH, SSD_WIDTH), 0.05)
    w_out = nrm(ks[8], (DEPTH, MIX_WIDTH, D_MODEL), (MIX_WIDTH ** -0.5) * BETA)
    ln1_g = 1.0 + nrm(ks[9], (DEPTH, D_MODEL), 0.05)
    ln1_b = nrm(ks[10], (DEPTH, D_MODEL), 0.02)
    w_route_group = nrm(ks[11], (DEPTH, D_MODEL, N_GROUPS_MOE), D_MODEL ** -0.5)
    b_route_group = nrm(ks[12], (DEPTH, N_GROUPS_MOE), 0.01)
    w_route_expert = nrm(ks[13], (DEPTH, D_MODEL, N_EXPERTS), D_MODEL ** -0.5)
    b_route_expert = nrm(ks[14], (DEPTH, N_EXPERTS), 0.01)
    w_gate = nrm(ks[15], (DEPTH, N_EXPERTS, D_MODEL, EXPERT_FF), D_MODEL ** -0.5)
    w_up = nrm(ks[16], (DEPTH, N_EXPERTS, D_MODEL, EXPERT_FF), D_MODEL ** -0.5)
    w_down = nrm(ks[17], (DEPTH, N_EXPERTS, EXPERT_FF, D_MODEL), (EXPERT_FF ** -0.5) * BETA)
    ln2_g = 1.0 + nrm(ks[18], (DEPTH, D_MODEL), 0.05)
    ln2_b = nrm(ks[19], (DEPTH, D_MODEL), 0.02)
    return {'x': x, 'w_in': w_in, 'conv_w': conv_w, 'conv_b': conv_b, 'dt_bias': dt_bias,
            'a_log': a_log, 'd_skip': d_skip, 'ssd_norm_w': ssd_norm_w, 'w_out': w_out,
            'ln1_g': ln1_g, 'ln1_b': ln1_b, 'w_route_group': w_route_group,
            'b_route_group': b_route_group, 'w_route_expert': w_route_expert,
            'b_route_expert': b_route_expert, 'w_gate': w_gate, 'w_up': w_up,
            'w_down': w_down, 'ln2_g': ln2_g, 'ln2_b': ln2_b}

def first_block(x, w_in, conv_w, conv_b, dt_bias, a_log, d_skip, ssd_norm_w, w_out, ln1_g, ln1_b,
              w_route_group, b_route_group, w_route_expert, b_route_expert, w_gate, w_up,
              w_down, ln2_g, ln2_b):
    bsz, s, _ = x.shape
    topk = min(TOPK_MAX, s // 4)
    cos, sin = rope_tables(s)
    cos_h, sin_h = cos[:, None, :], sin[:, None, :]
    for l in range(DEPTH):
        proj = jnp.einsum('bsd,de->bse', x, w_in[l])
        q, k, v, iq, ik, iw, z, xbc, dt_raw = jnp.split(proj, IN_SPLIT_POINTS, axis=-1)
        q = apply_rope(q.reshape(bsz, s, ATT_HEADS, HEAD_DIM), cos_h, sin_h)
        k = apply_rope(k, cos, sin)
        iq = apply_rope(iq.reshape(bsz, s, IDX_HEADS, IDX_DIM), cos_h, sin_h)
        ik = apply_rope(ik, cos, sin)
        att = dsa_attention(q, k, v, iq, ik, iw * INDEXER_SCALE, topk)
        ssd = ssd_mixer(z, xbc, dt_raw, conv_w[l], conv_b[l], dt_bias[l], a_log[l],
                        d_skip[l], ssd_norm_w[l])
        mixed = jnp.einsum('bse,ed->bsd', jnp.concatenate([att, ssd], -1), w_out[l])
        x = layer_norm(ALPHA * x + mixed, ln1_g[l], ln1_b[l])
        ffn = hier_moe(x, w_route_group[l], b_route_group[l], w_route_expert[l],
                       b_route_expert[l], w_gate[l], w_up[l], w_down[l])
        x = layer_norm(ALPHA * x + ffn, ln2_g[l], ln2_b[l])
    return x


BLOCK = 128
EPS = 1e-6

MLA_HEADS = 8
MLA_NOPE = 64
MLA_ROPE = 32
MLA_V = 64
MLA_KV_RANK = 256

DIL_PATTERNS = ((128, 1), (512, 4), (2048, 16))
N_DIL_GROUPS = 3
DIL_HEADS = 8
DIL_HEAD_DIM = 64

N_EXPERT_GROUPS = 4
EXPERTS_PER_GROUP_2 = 8
N_EXPERTS_2 = N_EXPERT_GROUPS * EXPERTS_PER_GROUP_2
TOP_K_EXPERT = 2
D_FF_EXPERT = 256

MLA_Q_COLS = MLA_HEADS * (MLA_NOPE + MLA_ROPE)
DIL_COLS = 3 * N_DIL_GROUPS * DIL_HEADS * DIL_HEAD_DIM
GATE_COLS = 2 * D_MODEL
IN_COLS = MLA_Q_COLS + MLA_KV_RANK + MLA_ROPE + DIL_COLS + GATE_COLS


def rms_norm(x, g):
    xf = x.astype(jnp.float32)
    y = xf * lax.rsqrt(jnp.mean(xf * xf, axis=-1, keepdims=True) + EPS)
    return (y * g.astype(jnp.float32)).astype(x.dtype)

def alibi_slopes(n):
    return jnp.exp2(-8.0 * (jnp.arange(n, dtype=jnp.float32) + 1.0) / n)

def rope(t, positions):
    half = t.shape[-1] // 2
    freqs = ROPE_THETA ** (-jnp.arange(half, dtype=jnp.float32) / half)
    ang = positions.astype(jnp.float32)[:, :, None] * freqs
    cos = jnp.cos(ang)[:, :, None, :]
    sin = jnp.sin(ang)[:, :, None, :]
    t1 = t[..., :half].astype(jnp.float32)
    t2 = t[..., half:].astype(jnp.float32)
    return jnp.concatenate([t1 * cos - t2 * sin, t2 * cos + t1 * sin], axis=-1).astype(t.dtype)

def causal_block_attention(q, k, v, scale):
    B, S, H, dq = q.shape
    nb = S // BLOCK
    q_blocks = jnp.moveaxis(q.reshape(B, nb, BLOCK, H, dq), 1, 0)
    kpos = jnp.arange(S)

    def one_block(args):
        qb, bi = args
        s = jnp.einsum('bqhd,bkhd->bhqk', qb, k).astype(jnp.float32) * scale
        qpos = bi * BLOCK + jnp.arange(BLOCK)
        s = jnp.where(kpos[None, :] <= qpos[:, None], s, -jnp.inf)
        p = jax.nn.softmax(s, axis=-1)
        return jnp.einsum('bhqk,bkhd->bqhd', p.astype(v.dtype), v)

    o = lax.map(one_block, (q_blocks, jnp.arange(nb)))
    return jnp.moveaxis(o, 0, 1).reshape(B, S, H, v.shape[-1])

def banded_attention(q, k, v, n_back, stride, slopes, scale):
    assert n_back <= BLOCK
    N, L, H, dh = q.shape
    nb = -(-L // BLOCK)
    Lp = nb * BLOCK
    qb = jnp.pad(q, ((0, 0), (0, Lp - L), (0, 0), (0, 0))).reshape(N, nb, BLOCK, H, dh)

    def key_blocks(t):
        tp = jnp.pad(t, ((0, 0), (BLOCK, Lp - L), (0, 0), (0, 0)))
        prev = tp[:, :Lp].reshape(N, nb, BLOCK, H, dh)
        cur = tp[:, BLOCK:].reshape(N, nb, BLOCK, H, dh)
        return jnp.concatenate([prev, cur], axis=2)

    kb = key_blocks(k)
    vb = key_blocks(v)
    s = jnp.einsum('nbqhd,nbkhd->nbhqk', qb, kb).astype(jnp.float32) * scale
    i = jnp.arange(BLOCK)[:, None]
    j = jnp.arange(2 * BLOCK)[None, :]
    delta = i + BLOCK - j
    kpos = jnp.arange(nb)[:, None, None] * BLOCK - BLOCK + j[None]
    valid = (delta >= 0) & (delta <= n_back) & (kpos >= 0)
    bias = -slopes[:, None, None] * (delta * stride).astype(jnp.float32)
    s = jnp.where(valid[None, :, None], s + bias, -jnp.inf)
    m = jnp.max(s, axis=-1, keepdims=True)
    p = jnp.exp(s - m)
    den = jnp.sum(p, axis=-1, keepdims=True)
    o = jnp.einsum('nbhqk,nbkhd->nbqhd', (p / den).astype(v.dtype), vb)
    o = o.reshape(N, Lp, H, dh)[:, :L]
    lse = jnp.transpose((m + jnp.log(den))[..., 0], (0, 1, 3, 2)).reshape(N, Lp, H)[:, :L]
    return o, lse

def mla_branch(q_cols, ckv, k_rope, positions, norm_ckv, w_ukv, q_norm, k_norm):
    B, S, _ = q_cols.shape
    q = q_cols.reshape(B, S, MLA_HEADS, MLA_NOPE + MLA_ROPE)
    kv = (rms_norm(ckv, norm_ckv) @ w_ukv).reshape(B, S, MLA_HEADS, MLA_NOPE + MLA_V)
    k_nope, v = kv[..., :MLA_NOPE], kv[..., MLA_NOPE:]
    k = jnp.concatenate([k_nope, jnp.broadcast_to(k_rope[:, :, None, :], (B, S, MLA_HEADS, MLA_ROPE))], axis=-1)
    q = rms_norm(q, q_norm)
    k = rms_norm(k, k_norm)
    q = jnp.concatenate([q[..., :MLA_NOPE], rope(q[..., MLA_NOPE:], positions)], axis=-1)
    k = jnp.concatenate([k[..., :MLA_NOPE], rope(k[..., MLA_NOPE:], positions)], axis=-1)
    o = causal_block_attention(q, k, v, (MLA_NOPE + MLA_ROPE) ** -0.5)
    return o.reshape(B, S, MLA_HEADS * MLA_V)

def dilated_branch(qkv_cols, q_norm, k_norm):
    B, S, _ = qkv_cols.shape
    H, dh = DIL_HEADS, DIL_HEAD_DIM
    qkv = qkv_cols.reshape(B, S, 3, N_DIL_GROUPS, H, dh)
    q = rms_norm(qkv[:, :, 0], q_norm[:, None, :])
    k = rms_norm(qkv[:, :, 1], k_norm[:, None, :])
    v = qkv[:, :, 2]
    slopes = alibi_slopes(H)
    outs, lses = [], []
    for g, (window, dil) in enumerate(DIL_PATTERNS):
        L = S // dil
        def fold(t):
            return t[:, :, g].reshape(B, L, dil, H, dh).transpose(0, 2, 1, 3, 4).reshape(B * dil, L, H, dh)
        o, lse = banded_attention(fold(q), fold(k), fold(v), window // dil, dil, slopes, dh ** -0.5)
        outs.append(o.reshape(B, dil, L, H, dh).transpose(0, 2, 1, 3, 4).reshape(B, S, H, dh))
        lses.append(lse.reshape(B, dil, L, H).transpose(0, 2, 1, 3).reshape(B, S, H))
    w = jax.nn.softmax(jnp.stack(lses, axis=0), axis=0)
    o = jnp.sum(w[..., None] * jnp.stack(outs, axis=0).astype(jnp.float32), axis=0)
    return o.astype(qkv_cols.dtype).reshape(B, S, H * dh)

def hier_moe_2(h, w_rg, b_rg, w_re, b_re, w_gate, w_up, w_down):
    B, S, D = h.shape
    T = B * S
    hf = h.reshape(T, D)
    gp = jax.nn.softmax((hf @ w_rg + b_rg).astype(jnp.float32), axis=-1)
    g_p, g_i = lax.top_k(gp, 1)
    g_p, g_i = g_p[:, 0], g_i[:, 0]
    el = (hf @ w_re + b_re).astype(jnp.float32).reshape(T, N_EXPERT_GROUPS, EXPERTS_PER_GROUP_2)
    el_sel = el[jnp.arange(T), g_i]
    ep = jax.nn.softmax(el_sel, axis=-1)
    e_p, e_i = lax.top_k(ep, TOP_K_EXPERT)
    e_p = e_p / jnp.sum(e_p, axis=-1, keepdims=True)
    weights = g_p[:, None] * e_p
    expert_idx = g_i[:, None] * EXPERTS_PER_GROUP_2 + e_i
    combine = jnp.sum(jax.nn.one_hot(expert_idx, N_EXPERTS_2, dtype=jnp.float32) * weights[..., None], axis=1)
    combine = combine.astype(hf.dtype)
    y = jnp.zeros_like(hf)
    for e in range(N_EXPERTS_2):
        he = jax.nn.silu(hf @ w_gate[e]) * (hf @ w_up[e])
        y = y + combine[:, e:e + 1] * (he @ w_down[e])
    return y.reshape(B, S, D)

def second_inputs(seed: int = 0) -> dict:
    key = jax.random.key(seed)
    ks = jax.random.split(key, 24)

    def nrm(k, shape, fan_in):
        return jax.random.normal(k, shape, jnp.float32) * (fan_in ** -0.5)

    def gain(k, shape):
        return 1.0 + 0.02 * jax.random.normal(k, shape, jnp.float32)

    def bias(k, shape, scale):
        return scale * jax.random.normal(k, shape, jnp.float32)

    Ld = DEPTH
    return {
        'x': jax.random.normal(ks[0], (BATCH, SEQ, D_MODEL), jnp.float32),
        'positions': jnp.broadcast_to(jnp.arange(SEQ, dtype=jnp.int32), (BATCH, SEQ)),
        'norm_attn': gain(ks[1], (Ld, D_MODEL)),
        'w_in': nrm(ks[2], (Ld, D_MODEL, IN_COLS), D_MODEL),
        'b_gate': bias(ks[3], (Ld, 2, D_MODEL), 0.02),
        'norm_ckv': gain(ks[4], (Ld, MLA_KV_RANK)),
        'w_ukv': nrm(ks[5], (Ld, MLA_KV_RANK, MLA_HEADS * (MLA_NOPE + MLA_V)), MLA_KV_RANK),
        'q_norm_mla': gain(ks[6], (Ld, MLA_NOPE + MLA_ROPE)),
        'k_norm_mla': gain(ks[7], (Ld, MLA_NOPE + MLA_ROPE)),
        'q_norm_dil': gain(ks[8], (Ld, N_DIL_GROUPS, DIL_HEAD_DIM)),
        'k_norm_dil': gain(ks[9], (Ld, N_DIL_GROUPS, DIL_HEAD_DIM)),
        'w_o_mla': nrm(ks[10], (Ld, MLA_HEADS * MLA_V, D_MODEL), MLA_HEADS * MLA_V),
        'w_o_dil': nrm(ks[11], (Ld, DIL_HEADS * DIL_HEAD_DIM, D_MODEL), DIL_HEADS * DIL_HEAD_DIM),
        'w_out': nrm(ks[12], (Ld, D_MODEL, D_MODEL), D_MODEL),
        'norm_ffn': gain(ks[13], (Ld, D_MODEL)),
        'w_router_group': nrm(ks[14], (Ld, D_MODEL, N_EXPERT_GROUPS), D_MODEL),
        'b_router_group': bias(ks[15], (Ld, N_EXPERT_GROUPS), 0.01),
        'w_router_expert': nrm(ks[16], (Ld, D_MODEL, N_EXPERTS_2), D_MODEL),
        'b_router_expert': bias(ks[17], (Ld, N_EXPERTS_2), 0.01),
        'w_gate': nrm(ks[18], (Ld, N_EXPERTS_2, D_MODEL, D_FF_EXPERT), D_MODEL),
        'w_up': nrm(ks[19], (Ld, N_EXPERTS_2, D_MODEL, D_FF_EXPERT), D_MODEL),
        'w_down': nrm(ks[20], (Ld, N_EXPERTS_2, D_FF_EXPERT, D_MODEL), D_FF_EXPERT),
    }

def second_block(x, positions, norm_attn, w_in, b_gate, norm_ckv, w_ukv, q_norm_mla, k_norm_mla,
              q_norm_dil, k_norm_dil, w_o_mla, w_o_dil, w_out, norm_ffn, w_router_group,
              b_router_group, w_router_expert, b_router_expert, w_gate, w_up, w_down):
    B, S, D = x.shape
    splits = [MLA_Q_COLS, MLA_Q_COLS + MLA_KV_RANK, MLA_Q_COLS + MLA_KV_RANK + MLA_ROPE,
              MLA_Q_COLS + MLA_KV_RANK + MLA_ROPE + DIL_COLS]
    for l in range(DEPTH):
        h = rms_norm(x, norm_attn[l])
        proj = h @ w_in[l]
        q_mla, ckv, k_rope, qkv_dil, gate_pre = jnp.split(proj, splits, axis=-1)
        o_mla = mla_branch(q_mla, ckv, k_rope, positions, norm_ckv[l], w_ukv[l],
                           q_norm_mla[l], k_norm_mla[l])
        o_dil = dilated_branch(qkv_dil, q_norm_dil[l], k_norm_dil[l])
        gates = jax.nn.sigmoid(gate_pre.reshape(B, S, 2, D) + b_gate[l])
        merged = gates[:, :, 0] * (o_mla @ w_o_mla[l]) + gates[:, :, 1] * (o_dil @ w_o_dil[l])
        x = x + merged @ w_out[l]
        h2 = rms_norm(x, norm_ffn[l])
        x = x + hier_moe_2(h2, w_router_group[l], b_router_group[l], w_router_expert[l],
                         b_router_expert[l], w_gate[l], w_up[l], w_down[l])
    return x


def setup_inputs(seed=0):
    out = dict(first_inputs(seed))
    for name, value in second_inputs(seed + 1).items():
        if name != "x":
            out[name + "_2"] = value
    return out


def reference(
    x, w_in, conv_w, conv_b, dt_bias, a_log, d_skip, ssd_norm_w, w_out, ln1_g, ln1_b,
    w_route_group, b_route_group, w_route_expert, b_route_expert, w_gate, w_up, w_down, ln2_g,
    ln2_b, positions_2, norm_attn_2, w_in_2, b_gate_2, norm_ckv_2, w_ukv_2, q_norm_mla_2,
    k_norm_mla_2, q_norm_dil_2, k_norm_dil_2, w_o_mla_2, w_o_dil_2, w_out_2, norm_ffn_2,
    w_router_group_2, b_router_group_2, w_router_expert_2, b_router_expert_2, w_gate_2, w_up_2,
    w_down_2,
):
    x = first_block(
        x, w_in, conv_w, conv_b, dt_bias, a_log, d_skip, ssd_norm_w, w_out, ln1_g, ln1_b,
        w_route_group, b_route_group, w_route_expert, b_route_expert, w_gate, w_up, w_down,
        ln2_g, ln2_b,
    )
    return second_block(
        x, positions_2, norm_attn_2, w_in_2, b_gate_2, norm_ckv_2, w_ukv_2, q_norm_mla_2,
        k_norm_mla_2, q_norm_dil_2, k_norm_dil_2, w_o_mla_2, w_o_dil_2, w_out_2, norm_ffn_2,
        w_router_group_2, b_router_group_2, w_router_expert_2, b_router_expert_2, w_gate_2,
        w_up_2, w_down_2,
    )


_drawn_inputs = setup_inputs


def setup_inputs(seed=0):
    import zlib

    import numpy as np

    out = dict(_drawn_inputs(seed))
    spreads = {}
    factors = {'conv_b': 2.947,
     'b_route_group': 4.511,
     'b_route_expert': 4.594,
     'norm_attn_2': 4.921,
     'b_gate_2': 14.94,
     'norm_ckv_2': 3.734,
     'q_norm_mla_2': 5.187,
     'k_norm_mla_2': 4.442,
     'q_norm_dil_2': 4.383,
     'k_norm_dil_2': 5.154,
     'b_router_group_2': 19.601,
     'b_router_expert_2': 30.57,
     'norm_ffn_2': 6.447}
    for name, (base, spread) in spreads.items():
        noise = np.random.default_rng([zlib.crc32(name.encode()), seed]).standard_normal(out[name].shape)
        drawn = base * np.exp(spread * noise) if base else spread * noise
        out[name] = jnp.asarray(drawn.astype(out[name].dtype))
    for name, factor in factors.items():
        out[name] = (out[name] * factor).astype(out[name].dtype)
    return out
```

```python
from contextlib import ExitStack

import numpy as np
import concourse.bass as bass
from concourse import mybir

F32 = mybir.dt.float32
BF16 = mybir.dt.bfloat16
I32 = mybir.dt.int32
U32 = mybir.dt.uint32
ALU = mybir.AluOpType
ACT = mybir.ActivationFunctionType
AX = mybir.AxisListType.X

P = 128
SEQ = 512
TT = SEQ // P
DM = 1024
KD = DM // P
HD = 64
NEG = -1.0e30
H1 = 8
IDX_HEADS = 4
INDEXER_SCALE = (IDX_HEADS ** -0.5) * (HD ** -0.5)
TOPK = min(256, SEQ // 4)
SSD_HEADS = 8
CONV_W = 4
ALPHA = 2.0 ** 0.25
LN_EPS = 1e-5
NAT1 = 512 + 64 + 4 + 8
EPS = 1e-6
MLA_D = 96
MLA_COLS = 8 * MLA_D + 256 + 32
DIL = ((128, 1), (512, 4), (2048, 16))
FF = 256
E1, G1 = 16, 4
E2, G2 = 32, 4


def most_tiles(experts):
    return (2 * SEQ + (P - 1) * experts) // P


NT1, NT2 = most_tiles(E1), most_tiles(E2)

VECS = [("dt_bias", 8), ("a_log", 8), ("d_skip", 8), ("ssd_norm_w", 512), ("ln1_g", DM), ("ln1_b", DM),
        ("b1", G1 + E1), ("ln2_g", DM), ("ln2_b", DM), ("norm_attn", DM), ("norm_ckv", 256),
        ("q_norm_mla", 96), ("k_norm_mla", 96), ("q_norm_dil", 192), ("k_norm_dil", 192),
        ("b_gate", 2 * DM), ("norm_ffn", DM), ("b2", G2 + E2)]
VEC_AT = {}
_at = 0
for _n, _w in VECS:
    VEC_AT[_n] = (_at, _w)
    _at += _w
NVEC = _at

CONSTS = [("ident", 128), ("upto", 128), ("after", 128), ("before", 128), ("ones", 128), ("rot", 128),
          ("cos", SEQ), ("sin", SEQ), ("iota", 128), ("down", 128), ("tok", TT), ("freq", 16)]
CONST_AT = {}
_at = 0
for _n, _w in CONSTS:
    CONST_AT[_n] = (_at, _w)
    _at += _w
NCONST = _at
CONSTS_B = [("ident_b", 128), ("causal_b", 128), ("slope_b", 8 * 128), ("dlo_b", 3 * SEQ), ("dhi_b", 3 * 256)]
CONST_B_AT = {}
_at = 0
for _n, _w in CONSTS_B:
    CONST_B_AT[_n] = (_at, _w)
    _at += _w
NCONST_B = _at


def constants():
    k = np.arange(P)
    c = {}
    c["ident"] = np.eye(P)
    c["upto"] = k[:, None] <= k[None, :]
    c["after"] = k[:, None] > k[None, :]
    c["before"] = k[:, None] < k[None, :]
    c["ones"] = np.ones((P, P))
    rot = np.zeros((P, P))
    for m in range(P):
        if m % HD < HD // 2:
            rot[m + HD // 2, m] = -1
        else:
            rot[m - HD // 2, m] = 1
    c["rot"] = rot
    inv = (np.float32(10000.0) ** (-np.arange(0, HD, 2, dtype=np.float32) / np.float32(HD))).astype(np.float32)
    ang = np.arange(SEQ, dtype=np.float32)[:, None] * inv[None, :]
    c["cos"] = np.tile(np.cos(ang).T, (4, 1))
    c["sin"] = np.tile(np.sin(ang).T, (4, 1))
    c["iota"] = np.broadcast_to(k[None, :], (P, P))
    c["down"] = np.broadcast_to(P - k[None, :], (P, P))
    c["tok"] = k[:, None] + P * np.arange(TT)[None, :]
    c["freq"] = np.broadcast_to(
        (np.float32(10000.0) ** (-np.arange(16, dtype=np.float32) / np.float32(16))).astype(np.float32)[None], (P, 16))
    f = np.concatenate([np.asarray(c[n], np.float32).reshape(P, w) for n, w in CONSTS], 1)
    b = {}
    b["ident_b"] = np.eye(P)
    b["causal_b"] = np.where(k[None, :] <= k[:, None], 0.0, NEG)
    b["slope_b"] = np.stack([np.eye(P) * 2.0 ** -(h + 1) for h in range(8)], 1)
    x = np.arange(SEQ)[None, :]
    delta = k[:, None] + SEQ - P - x
    lo, hi = [], []
    for window, dil in DIL:
        ok = (delta >= 0) & (delta <= window) & (delta % dil == 0)
        high = np.where(x < 256, 256, 0)
        lo.append(np.where(ok, -(delta - high), NEG))
        hi.append(np.where(ok, -high, 0)[:, :256])
    b["dlo_b"] = np.stack(lo, 1)
    b["dhi_b"] = np.stack(hi, 1)
    fb = np.concatenate([np.asarray(b[n], np.float32).reshape(P, w) for n, w in CONSTS_B], 1)
    return np.ascontiguousarray(f), (fb.view(np.uint32) >> 16).astype(np.uint16)


class Chain:

    def __init__(self, eng, sem, start=0):
        self.eng, self.sem, self.n = eng, sem, start

    def __call__(self, ins):
        ins.then_inc(self.sem, 1)
        self.n = self.n + 1
        self.eng.wait_ge(self.sem, self.n)


class Core:

    def __init__(self, nc, ctx, d):
        self.nc, self.ctx, self.d = nc, ctx, d
        self.uid = 0
        self.held = ExitStack()
        self.held_sems = []
        self.gathered = [0] * 6
        self.gather_sems = [ctx.enter_context(nc.semaphore(f"gathered{i}")) for i in range(6)]

    def sem(self, name):
        self.uid += 1
        sem = self.held.enter_context(self.nc.semaphore(f"{name}_{self.uid}"))
        self.held_sems.append(sem)
        return sem

    def recycle_semaphores(self):
        sems = self.held_sems
        with self.nc.Block() as block:
            @block.gpsimd
            def _(pool):
                for sem in sems:
                    pool.sem_clear(sem)
        self.held.close()
        self.held, self.held_sems = ExitStack(), []

    def sb(self, ctx, name, shape, dt=F32):
        return ctx.enter_context(self.nc.sbuf_tensor(name, shape, dt))

    def ps(self, ctx, name, shape=(P, 512), dt=F32):
        return ctx.enter_context(self.nc.psum_tensor(name, list(shape), dt))

    def c(self, name):
        a, w = CONST_AT[name]
        return self.consts[:, a:a + w]

    def cb(self, name):
        a, w = CONST_B_AT[name]
        return self.consts_b[:, a:a + w]

    def vec(self, name):
        a, w = VEC_AT[name]
        return self.d["vecs"][:, a:a + w]


def bc(ap, axis, n):
    shape = list(ap.shape)
    shape.insert(axis, n)
    return ap.unsqueeze(axis).broadcast_to(shape)


def transpose_tiles(k, name, src, dst, blocks):
    nc = k.nc
    with ExitStack() as s:
        bank = k.ps(s, f"{name}_bank", (P, 4, 512))
        turned = k.sem(f"{name}_turned")
        copied = [k.sem(f"{name}_copied_{e}") for e in ("vector", "scalar")]
        with nc.Block() as block:
            @block.tensor
            def _(pe):
                for b in range(blocks):
                    if b >= 4:
                        pe.wait_ge(copied[b % 2], (b - 4) // 2 + 1)
                    for tt in range(TT):
                        a = src(tt, b)
                        ins = pe.transpose(bank[0:a.shape[1], b % 4, tt * P:(tt + 1) * P], a, k.c("ident"))
                    ins.then_inc(turned, 1)

            @block.vector
            def _(dve):
                for b in range(0, blocks, 2):
                    dve.wait_ge(turned, b + 1)
                    w = dst(b).shape[0]
                    dve.tensor_copy(dst(b), bank[0:w, b % 4, :]).then_inc(copied[0], 1)

            @block.scalar
            def _(act):
                for b in range(1, blocks, 2):
                    act.wait_ge(turned, b + 1)
                    w = dst(b).shape[0]
                    act.activation(dst(b), bank[0:w, b % 4, :], ACT.Copy).then_inc(copied[1], 1)


CONV_BLOCKS = 6
ROPE_BLOCKS = 8


def load_block1(k, ctx):
    nc, d = k.nc, k.d
    k.consts = k.sb(k.ctx, "consts", [P, NCONST])
    k.consts_b = k.sb(k.ctx, "consts_b", [P, NCONST_B], BF16)
    k.x1 = k.sb(k.ctx, "x_res", [P, TT, DM])
    k.xT = k.sb(k.ctx, "xT", [P, KD, SEQ])
    k.v = k.sb(ctx, "v1", [P, TT, 76])
    k.ropeT = k.sb(ctx, "ropeT", [P, ROPE_BLOCKS, SEQ])
    k.sz = k.sb(ctx, "silu_z", [P, TT, 512])
    k.xbcT = k.sb(ctx, "xbcT", [P, CONV_BLOCKS, SEQ])
    k.convw = k.sb(ctx, "convw", [P, CONV_BLOCKS, CONV_W + 1])


def project1(k, ctx):
    nc, d = k.nc, k.d
    NB = ROPE_BLOCKS + CONV_BLOCKS
    with ExitStack() as s:
        w_t = k.sb(s, "w_t", [P, 4, KD * P])
        w_n = k.sb(s, "w_n", [P, KD, NAT1])
        raw = k.sb(s, "raw", [P, 2, SEQ])
        padded = k.sb(s, "padded", [P, 2, SEQ + CONV_W - 1])
        part = k.sb(s, "part", [P, 2, SEQ])
        acc = k.sb(s, "conv_acc", [P, 2, SEQ])
        main = [k.ps(s, f"proj_main{i}") for i in range(4)]
        turned = [k.ps(s, f"proj_rot{i}") for i in range(2)]
        consts_in, x_in, wn_in, small_in = k.sem("consts_in"), k.sem("x_in"), k.sem("wn_in"), k.sem("small_in")
        wt_in = [k.sem(f"wt_in{i}") for i in range(4)]
        proj_done, main_free = k.sem("proj_done"), k.sem("main_free")
        raw_ready, rot_done, roped = k.sem("raw_ready"), k.sem("rot_done"), k.sem("roped")
        pad_zero, conv_done, conv_silu, dve_step = (k.sem("pad_zero"), k.sem("conv_done"), k.sem("conv_silu"),
                                                    k.sem("dve_step"))
        k.vecs_in = k.sem("x_nat_in")
        NN = 2 * TT

        with nc.Block() as block:
            @block.sync
            def _(sp):
                sp.dma_start(k.xT[:], d["xT"]).then_inc(x_in, 16)
                sp.dma_start(w_t[:, 0], d["w_in_t"][0]).then_inc(wt_in[0], 16)
                sp.dma_start(k.consts[:], d["consts"]).then_inc(consts_in, 16)
                sp.dma_start(k.convw[:], d["convw"]).then_inc(small_in, 16)
                sp.dma_start(k.consts_b[:], d["consts_b"]).then_inc(small_in, 16)
                for b in range(1, NB):
                    if b >= 4:
                        sp.wait_ge(proj_done, b - 3)
                    sp.dma_start(w_t[:, b % 4], d["w_in_t"][b]).then_inc(wt_in[b % 4], 16)
                    if b == 4:
                        sp.dma_start(w_n[:], d["w_in_n"]).then_inc(wn_in, 16)
                sp.dma_start(k.x1[:], d["x_nat"]).then_inc(k.vecs_in, 16)
                sp.wait_ge(k.vecs_in, 16)
                sp.wait_ge(small_in, 32)

            @block.tensor
            def _(pe):
                pe.wait_ge(x_in, 16)
                for b in range(NB + 1):
                    if b < NB:
                        pe.wait_ge(wt_in[b % 4], 16 * (b // 4 + 1))
                        if b >= 4:
                            pe.wait_ge(main_free, b - 3)
                        for c in range(KD):
                            ins = pe.matmul(main[b % 4][:], w_t[:, b % 4, c * P:(c + 1) * P], k.xT[:, c, :],
                                            start=(c == 0), stop=(c == KD - 1))
                        ins.then_inc(proj_done, 1)
                    r = b - 1
                    if 0 <= r < ROPE_BLOCKS:
                        if r == 0:
                            pe.wait_ge(consts_in, 16)
                        pe.wait_ge(raw_ready, r + 1)
                        if r >= 2:
                            pe.wait_ge(roped, r - 1)
                        pe.matmul(turned[r % 2][:], k.c("rot"), raw[:, r % 2, :], start=True,
                                  stop=True).then_inc(rot_done, 1)
                pe.wait_ge(wn_in, 16)
                for n in range(NN):
                    b = NB + n
                    pe.wait_ge(main_free, b - 3)
                    tt, lo, w = n // 2, 512 * (n % 2), (512, NAT1 - 512)[n % 2]
                    for c in range(KD):
                        ins = pe.matmul(main[b % 4][:, 0:w], k.xT[:, c, tt * P:(tt + 1) * P],
                                        w_n[:, c, lo:lo + w], start=(c == 0), stop=(c == KD - 1))
                    ins.then_inc(proj_done, 1)

            @block.scalar
            def _(act):
                act.wait_ge(pad_zero, 1)
                for b in range(NB + NN):
                    act.wait_ge(proj_done, b + 1)
                    if b < ROPE_BLOCKS:
                        if b >= 2:
                            act.wait_ge(roped, b - 1)
                        act.activation(raw[:, b % 2, :], main[b % 4][:], ACT.Copy,
                                       scale=(HD ** -0.5 if b < 4 else 1.0)).then_inc(raw_ready, 1)
                        act.wait_ge(raw_ready, b + 1)
                        act.sem_inc(main_free, 1)
                    elif b < NB:
                        r = b - ROPE_BLOCKS
                        if r >= 2:
                            act.wait_ge(conv_done, r - 1)
                        act.activation(padded[:, r % 2, CONV_W - 1:], main[b % 4][:],
                                       ACT.Copy).then_inc(main_free, 1)
                        if r >= 1:
                            act.wait_ge(conv_done, r)
                            act.activation(k.xbcT[:, r - 1, :], acc[:, (r - 1) % 2, :], ACT.Silu,
                                           bias=k.convw[:, r - 1, CONV_W:CONV_W + 1]).then_inc(conv_silu, 1)
                    else:
                        n = b - NB
                        if n == 0:
                            r = CONV_BLOCKS
                            act.wait_ge(conv_done, r)
                            act.activation(k.xbcT[:, r - 1, :], acc[:, (r - 1) % 2, :], ACT.Silu,
                                           bias=k.convw[:, r - 1, CONV_W:CONV_W + 1]).then_inc(conv_silu, 1)
                        tt = n // 2
                        if n % 2 == 0:
                            act.activation(k.sz[:, tt, :], main[b % 4][:], ACT.Silu).then_inc(main_free, 1)
                        else:
                            act.activation(k.v[:, tt, :], main[b % 4][:, 0:76], ACT.Copy).then_inc(main_free, 1)

            @block.vector
            def _(dve):
                step = Chain(dve, dve_step)
                dve.memset(padded[:, :, 0:CONV_W - 1], 0.0).then_inc(pad_zero, 1)
                dve.wait_ge(consts_in, 16)
                for r in range(ROPE_BLOCKS):
                    dve.wait_ge(raw_ready, r + 1)
                    dve.tensor_tensor(part[:, 0, :], raw[:, r % 2, :], k.c("cos"), ALU.mult).then_inc(dve_step, 1)
                    dve.wait_ge(rot_done, r + 1)
                    dve.tensor_tensor(part[:, 1, :], turned[r % 2][:], k.c("sin"), ALU.mult).then_inc(dve_step, 1)
                    step.n += 2
                    dve.wait_ge(dve_step, step.n)
                    dve.tensor_tensor(k.ropeT[:, r, :], part[:, 0, :], part[:, 1, :], ALU.add).then_inc(roped, 1)
                    dve.wait_ge(roped, r + 1)
                dve.wait_ge(small_in, 32)
                for r in range(CONV_BLOCKS):
                    dve.wait_ge(main_free, ROPE_BLOCKS + r + 1)
                    if r >= 2:
                        dve.wait_ge(conv_silu, r - 1)
                    a, u = acc[:, r % 2, :], padded[:, r % 2, :]
                    step(dve.tensor_scalar(a, u[:, 0:SEQ], k.convw[:, r, 0:1], None, ALU.mult))
                    for j in range(1, CONV_W):
                        ins = dve.scalar_tensor_tensor(a, u[:, j:j + SEQ], k.convw[:, r, j:j + 1], a,
                                                       ALU.mult, ALU.add)
                        if j < CONV_W - 1:
                            step(ins)
                    ins.then_inc(conv_done, 1)


def select_keys(k, ctx):
    nc = k.nc
    TAKEN, FLOOR = -3.0e38, -1.0e35
    k.key_bias = k.sb(ctx, "key_bias", [P, TT, SEQ], BF16)
    tiles = [tt for tt in range(TT) if (tt + 1) * P > TOPK]
    with ExitStack() as s:
        relu = k.sb(s, "relu", [P, 2, SEQ])
        score = k.sb(s, "score", [P, TT, SEQ])
        iw = k.sb(s, "iw", [P, TT, IDX_HEADS])
        best = k.sb(s, "best", [P, 8])
        bank = [k.ps(s, f"idx_bank{i}") for i in range(2)]
        dots, relued, used, scored, dve_step, iw_ready = (
            k.sem("idx_dots"), k.sem("idx_relued"), k.sem("idx_used"), k.sem("idx_scored"), k.sem("idx_step"),
            k.sem("iw_ready"))
        units = [(tt, h) for tt in tiles for h in range(IDX_HEADS)]
        with nc.Block() as block:
            @block.tensor
            def _(pe):
                for u, (tt, h) in enumerate(units):
                    if u >= 2:
                        pe.wait_ge(relued, u - 1)
                    lo = HD * (h % 2)
                    pe.matmul(bank[u % 2][:, 0:(tt + 1) * P],
                              k.ropeT[lo:lo + HD, 5 + h // 2, tt * P:(tt + 1) * P],
                              k.ropeT[lo:lo + HD, 7, 0:(tt + 1) * P], start=True, stop=True).then_inc(dots, 1)

            @block.scalar
            def _(act):
                for u, (tt, h) in enumerate(units):
                    act.wait_ge(dots, u + 1)
                    if u >= 2:
                        act.wait_ge(used, u - 1)
                    w = (tt + 1) * P
                    act.activation(relu[:, u % 2, 0:w], bank[u % 2][:, 0:w], ACT.Relu).then_inc(relued, 1)

            @block.vector
            def _(dve):
                step = Chain(dve, dve_step)
                step(dve.tensor_scalar(iw[:], k.v[:, :, 64:64 + IDX_HEADS], INDEXER_SCALE, None, ALU.mult))
                for tt in range(TT):
                    if tt not in tiles:
                        if tt:
                            step(dve.memset(k.key_bias[:, tt, 0:tt * P], 0.0))
                        step(dve.tensor_copy(k.key_bias[:, tt, tt * P:(tt + 1) * P], k.cb("causal_b")))
                for u, (tt, h) in enumerate(units):
                    w = (tt + 1) * P
                    dve.wait_ge(relued, u + 1)
                    sc, r = score[:, tt, 0:w], relu[:, u % 2, 0:w]
                    if h == 0:
                        ins = dve.tensor_scalar(sc, r, iw[:, tt, h:h + 1], None, ALU.mult)
                    else:
                        ins = dve.scalar_tensor_tensor(sc, r, iw[:, tt, h:h + 1], sc, ALU.mult, ALU.add)
                    ins.then_inc(used, 1)
                    dve.wait_ge(used, u + 1)
                    if h == IDX_HEADS - 1:
                        diag = score[:, tt, tt * P:w]
                        step(dve.tensor_tensor(diag, diag, k.cb("causal_b"), ALU.add))
                        for _ in range(TOPK // 8):
                            step(dve.max(best[:], sc))
                            step(dve.match_replace(sc, best[:], sc, TAKEN))
                        step(dve.tensor_scalar(k.key_bias[:, tt, 0:w], sc, FLOOR, NEG, ALU.is_gt, ALU.mult))


def attention(k, name, units, out, group=8, natural=True, stats=None):
    nc = k.nc
    n = len(units)
    with ExitStack() as s:
        probs = k.sb(s, f"{name}_probs", [P, 2, SEQ])
        pT = k.sb(s, f"{name}_pT", [P, 2, SEQ])
        own = stats is None
        nmax, den = (k.sb(s, f"{name}_nmax", [P, n]), k.sb(s, f"{name}_den", [P, n])) if own else stats
        rden = k.sb(s, f"{name}_rden", [P, n])
        sbank = [k.ps(s, f"{name}_scores{i}") for i in range(2)]
        tbank = [k.ps(s, f"{name}_pT{i}") for i in range(2)]
        obank = [k.ps(s, f"{name}_out{i}") for i in range(2)]
        scores, maxed, probs_ready, turned, pT_ready, summed, out_free, rden_ready = (
            k.sem(f"{name}_{x}") for x in ("scores", "maxed", "probs", "turned", "pT", "summed", "outfree", "rden"))
        with nc.Block() as block:
            @block.tensor
            def _(pe):
                for st in range(n + 2):
                    if st < n:
                        u = units[st]
                        if st >= 2:
                            pe.wait_ge(probs_ready, st - 1)
                        w = u["keys"].shape[-1]
                        ms = u["masks"]
                        ins = pe.matmul(sbank[st % 2][:, 0:w], u["q"], u["keys"], start=True, stop=True)
                        for m, (lhs, rhs, lo, hi) in enumerate(ms):
                            ins = pe.matmul(sbank[st % 2][:, lo:hi], lhs, rhs, start=False, stop=True,
                                            skip_group_check=True)
                        ins.then_inc(scores, 1)
                    if 1 <= st <= n:
                        j = st - 1
                        pe.wait_ge(probs_ready, j + 1)
                        if j >= 2:
                            pe.wait_ge(pT_ready, j - 1)
                        for b in range(len(units[j]["values"])):
                            ins = pe.transpose(tbank[j % 2][:, b * P:(b + 1) * P],
                                               probs[:, j % 2, b * P:(b + 1) * P], k.c("ident"))
                        ins.then_inc(turned, 1)
                    if st >= 2:
                        j = st - 2
                        g, h = divmod(j, group)
                        pe.wait_ge(pT_ready, j + 1)
                        if h == 0 and g >= 2:
                            pe.wait_ge(out_free, g - 1)
                        vs = units[j]["values"]
                        for b, v in enumerate(vs):
                            ins = pe.matmul(obank[g % 2][:, h * HD:(h + 1) * HD], pT[:, j % 2, b * P:(b + 1) * P],
                                            v, start=(b == 0), stop=(b == len(vs) - 1))
                        ins.then_inc(summed, 1)

            @block.scalar
            def _(act):
                for j, u in enumerate(units):
                    w = u["keys"].shape[-1]
                    act.wait_ge(maxed, j + 1)
                    if j >= 2:
                        act.wait_ge(turned, j - 1)
                    act.activation(probs[:, j % 2, 0:w], sbank[j % 2][:, 0:w], ACT.Exp, bias=nmax[:, j:j + 1],
                                   accum_out=den[:, j:j + 1]).then_inc(probs_ready, 1)

            @block.vector
            def _(dve):
                for st in range(n + 3):
                    if st < n:
                        w = units[st]["keys"].shape[-1]
                        dve.wait_ge(scores, st + 1)
                        dve.reduce_max(nmax[:, st:st + 1], sbank[st % 2][:, 0:w], AX, negate=True).then_inc(maxed, 1)
                    if 1 <= st <= n:
                        j = st - 1
                        w = len(units[j]["values"]) * P
                        dve.wait_ge(turned, j + 1)
                        if j >= 2:
                            dve.wait_ge(summed, j - 1)
                        dve.tensor_copy(pT[:, j % 2, 0:w], tbank[j % 2][:, 0:w]).then_inc(pT_ready, 1)
                    if st >= 3 and (st - 2) % group == 0:
                        g = (st - 2) // group - 1
                        a, b = g * group, (g + 1) * group
                        dve.wait_ge(summed, b)
                        o = obank[g % 2][:].rearrange("p (h d) -> p h d", h=group)
                        if own:
                            dve.reciprocal(rden[:, a:b], den[:, a:b]).then_inc(rden_ready, 1)
                            dve.wait_ge(rden_ready, g + 1)
                            dve.tensor_tensor(out(g), o, bc(rden[:, a:b], 2, HD), ALU.mult).then_inc(out_free, 1)
                        else:
                            dve.tensor_copy(out(g), o).then_inc(out_free, 1)


def state_space(k, ctx):
    nc, d = k.nc, k.d
    k.y = k.sb(ctx, "ssd_y", [P, TT, 512])
    HW = 4 * HD
    xs = k.sb(ctx, "xs_nat", [P, TT, 5 * P])
    with ExitStack() as s:
        bank = k.ps(s, "xs_bank", (P, 4, 512))
        turned, copied = k.sem("xs_turned"), [k.sem("xs_copied_v"), k.sem("xs_copied_s")]
        with nc.Block() as block:
            @block.tensor
            def _(pe):
                for tt in range(TT):
                    q = 2 * (tt % 2)
                    if tt >= 2:
                        pe.wait_ge(copied[0], tt - 1)
                        pe.wait_ge(copied[1], tt - 1)
                    for b in range(5):
                        ins = pe.transpose(bank[:, q + b // 4, (b % 4) * P:(b % 4 + 1) * P],
                                           k.xbcT[:, b, tt * P:(tt + 1) * P], k.c("ident"))
                    ins.then_inc(turned, 1)

            @block.vector
            def _(dve):
                for tt in range(TT):
                    dve.wait_ge(turned, tt + 1)
                    dve.tensor_copy(xs[:, tt, 0:512], bank[:, 2 * (tt % 2), :]).then_inc(copied[0], 1)

            @block.scalar
            def _(act):
                for tt in range(TT):
                    act.wait_ge(turned, tt + 1)
                    act.activation(xs[:, tt, 512:640], bank[:, 2 * (tt % 2) + 1, 0:P],
                                   ACT.Copy).then_inc(copied[1], 1)
    with ExitStack() as s2:
        k_vec = k.sb(s2, "ssd_vec", [P, 24 + 512])
        t8 = [k.sb(s2, f"ssd_t{i}", [P, TT, 8]) for i in range(8)]
        decay = k.sb(s2, "ssd_decay", [P, 3, TT * 8])
        X = k.sb(s2, "ssd_x", [P, 2, 512])
        Xd = k.sb(s2, "ssd_xd", [P, 2, 512])
        Gm = k.sb(s2, "ssd_gm", [P, 2, 2, P])
        At = k.sb(s2, "ssd_at", [P, 2, P])
        L = k.sb(s2, "ssd_l", [P, 2, P])
        MT = k.sb(s2, "ssd_mt", [P, 2, P])
        St = k.sb(s2, "ssd_state", [P, HW])
        y1 = k.sb(s2, "ssd_y1", [P, 512])
        y2 = k.sb(s2, "ssd_y2", [P, 512])
        yy = k.sb(s2, "ssd_yy", [P, 512])
        ms = k.sb(s2, "ssd_ms", [P, TT, 3])
        b_g = [k.ps(s2, f"ssd_g{i}") for i in range(2)]
        b_seg = [k.ps(s2, f"ssd_seg{i}") for i in range(2)]
        b_y = k.ps(s2, "ssd_ydiag")
        b_sum = b_y
        b_off = [k.ps(s2, f"ssd_yoff{i}") for i in range(2)]
        b_st = k.ps(s2, "ssd_st")
        (vec_in, e_ready, a_ready, sums_ready, decay_ready, x_ready, g_done, gm_ready, at_ready, seg_done, l_ready,
         mt_ready, ydiag_done, yoff_done, st_done, st_ready, y_free, step_d, step_a, sq_ready, rms_ready, lg_ready) = (
            k.sem("ssd_" + x) for x in ("vec_in", "e", "a", "sums", "decay", "x", "g", "gm", "at", "seg", "l", "mt",
                                        "ydiag", "yoff", "stdone", "st", "yfree", "stepd", "stepa", "sq", "rms",
                                        "lg"))
        dtb, al, dsk, nw = (k_vec[:, 0:8], k_vec[:, 8:16], k_vec[:, 16:24], k_vec[:, 24:536])
        pre, ex, dt, a_t, tmp, tmp2, tmp3, A = t8
        dr = k.v[:, :, 68:76]
        NU = TT * SSD_HEADS
        with nc.Block() as block:
            @block.sync
            def _(sp):
                sp.dma_start(k_vec[:, 0:24], k.d["vecs"][:, 0:24]).then_inc(vec_in, 16)
                sp.dma_start(nw, k.vec("ssd_norm_w")).then_inc(vec_in, 16)

            @block.tensor
            def _(pe):
                pe.wait_ge(a_ready, 1)
                Af = A[:].rearrange("p c h -> p (c h)")
                for i, m in enumerate(("after", "ones", "upto")):
                    ins = pe.matmul(b_sum[:, i * 32:(i + 1) * 32], k.c(m), Af, start=True, stop=True)
                ins.then_inc(sums_ready, 1)
                for c in range(TT):
                    tok = slice(c * P, (c + 1) * P)
                    if c >= 1:
                        pe.wait_ge(gm_ready, c)
                    for g in range(2):
                        r = slice(HD * g, HD * (g + 1))
                        ins = pe.matmul(b_g[g][:, 0:P], k.xbcT[r, 4, tok], k.xbcT[r, 5, tok],
                                        start=True, stop=True)
                    ins.then_inc(g_done, 1)
                    if c >= 1:
                        pe.wait_ge(st_ready, c)
                        pe.wait_ge(y_free, c)
                        for g in range(2):
                            r = slice(HD * g, HD * (g + 1))
                            ins = pe.matmul(b_off[g][:, 0:HW], k.xbcT[r, 5, tok], St[r, :],
                                            start=True, stop=True)
                        ins.then_inc(yoff_done, 1)
                    pe.wait_ge(x_ready, c + 1)
                    if c < TT - 1:
                        for g in range(2):
                            ins = pe.matmul(b_st[:, g * HW:(g + 1) * HW], xs[:, c, 512:640],
                                            Xd[:, c % 2, g * HW:(g + 1) * HW], start=True, stop=True)
                        ins.then_inc(st_done, 1)
                    for h in range(SSD_HEADS + 1):
                        if h < SSD_HEADS:
                            u = c * SSD_HEADS + h
                            pe.wait_ge(at_ready, u + 1)
                            if u >= 2:
                                pe.wait_ge(l_ready, u - 1)
                            pe.matmul(b_seg[u % 2][:, 0:P], At[:, u % 2, :], k.c("upto"), start=True,
                                      stop=True).then_inc(seg_done, 1)
                        if h >= 1:
                            u = c * SSD_HEADS + h - 1
                            pe.wait_ge(mt_ready, u + 1)
                            pe.matmul(b_y[:, (h - 1) * HD:h * HD], MT[:, u % 2, :],
                                      X[:, c % 2, (h - 1) * HD:h * HD], start=True, stop=True).then_inc(ydiag_done, 1)

            @block.gpsimd
            def _(pool):
                pool.wait_ge(a_ready, 1)
                for u in range(NU):
                    c, h = divmod(u, SSD_HEADS)
                    if u >= 2:
                        pool.wait_ge(seg_done, u - 1)
                    pool.tensor_scalar(At[:, u % 2, :], k.c("after"), A[:, c, h:h + 1], None,
                                       ALU.mult).then_inc(at_ready, 1)

            @block.scalar
            def _(act):
                act.wait_ge(vec_in, 32)
                act.activation(a_t[:, 0, :], al, ACT.Exp).then_inc(e_ready, 1)
                act.wait_ge(step_d, 3)
                act.activation(ex[:], tmp[:], ACT.Exp).then_inc(e_ready, 1)
                act.wait_ge(step_d, 4)
                act.activation(tmp3[:], tmp2[:], ACT.Ln).then_inc(lg_ready, 1)
                act.wait_ge(sums_ready, 1)
                act.activation(decay[:], b_sum[:, 0:96].rearrange("p (a b) -> p a b", a=3),
                               ACT.Exp).then_inc(decay_ready, 1)
                for u in range(NU):
                    act.wait_ge(seg_done, u + 1)
                    if u >= 2:
                        act.wait_ge(mt_ready, u - 1)
                    act.activation(L[:, u % 2, :], b_seg[u % 2][:, 0:P], ACT.Exp).then_inc(l_ready, 1)
                for c in range(TT):
                    act.wait_ge(sq_ready, c + 1)
                    act.activation(ms[:, c, 1:2], ms[:, c, 0:1], ACT.Sqrt, scale=1.0,
                                   bias=0.0).then_inc(rms_ready, 1)

            @block.vector
            def _(dve):
                step = Chain(dve, step_d)
                dve.wait_ge(vec_in, 32)
                step(dve.tensor_tensor(pre[:], dr, bc(dtb, 1, TT), ALU.add))
                step(dve.tensor_scalar(dt[:], pre[:], -1.0, None, ALU.mult))
                step(dve.tensor_tensor(tmp[:], pre[:], dt[:], ALU.min))
                dve.wait_ge(e_ready, 2)
                step(dve.tensor_scalar(tmp2[:], ex[:], 1.0, None, ALU.add))
                step(dve.tensor_scalar(dt[:], tmp2[:], -1.0, 1e-30, ALU.add, ALU.max))
                step(dve.reciprocal(tmp[:], dt[:]))
                step(dve.tensor_tensor(dt[:], tmp[:], ex[:], ALU.mult))
                dve.wait_ge(lg_ready, 1)
                step(dve.tensor_tensor(tmp3[:], tmp3[:], dt[:], ALU.mult))
                step(dve.tensor_scalar(tmp2[:], tmp2[:], 1.0, None, ALU.is_equal))
                step(dve.tensor_tensor(tmp2[:], tmp2[:], ex[:], ALU.mult))
                step(dve.tensor_tensor(tmp3[:], tmp3[:], tmp2[:], ALU.add))
                step(dve.scalar_tensor_tensor(dt[:], pre[:], 0.0, tmp3[:], ALU.max, ALU.add))
                step(dve.tensor_scalar(a_t[:, 1, :], a_t[:, 0, :], -1.0, None, ALU.mult))
                dve.tensor_tensor(A[:], dt[:], bc(a_t[:, 1, :], 1, TT), ALU.mult).then_inc(a_ready, 1)
                dve.wait_ge(decay_ready, 1)
                h8 = dict(h=8)
                for c in range(TT):
                    cs = slice(c * 8, c * 8 + 8)
                    xc = xs[:, c, 0:512].rearrange("p (h d) -> p h d", **h8)
                    Xc = X[:, c % 2, :].rearrange("p (h d) -> p h d", **h8)
                    Xdc = Xd[:, c % 2, :].rearrange("p (h d) -> p h d", **h8)
                    step(dve.tensor_tensor(Xc, xc, bc(dt[:, c, :], 2, HD), ALU.mult))
                    dve.tensor_tensor(Xdc, Xc, bc(decay[:, 0, cs], 2, HD), ALU.mult).then_inc(x_ready, 1)
                    dve.wait_ge(g_done, c + 1)
                    for g in range(2):
                        ins = dve.tensor_tensor(Gm[:, c % 2, g, :], b_g[g][:, 0:P], k.c("upto"), ALU.mult)
                        if g == 0:
                            step(ins)
                    ins.then_inc(gm_ready, 1)
                    if c < TT - 1:
                        dve.wait_ge(st_done, c + 1)
                        if c >= 1:
                            dve.wait_ge(yoff_done, c)
                            s3 = St[:].rearrange("p (h d) -> p h d", h=4)
                            for g in range(2):
                                r = slice(HD * g, HD * (g + 1))
                                step(dve.tensor_tensor(s3[r], s3[r], bc(decay[r, 1, c * 8 + 4 * g:c * 8 + 4 * g + 4], 2, HD),
                                                       ALU.mult))
                            for g in range(2):
                                r = slice(HD * g, HD * (g + 1))
                                ins = dve.tensor_tensor(St[r, :], St[r, :], b_st[r, g * HW:(g + 1) * HW], ALU.add)
                                if g == 0:
                                    step(ins)
                            ins.then_inc(st_ready, 1)
                        else:
                            for g in range(2):
                                r = slice(HD * g, HD * (g + 1))
                                ins = dve.tensor_copy(St[r, :], b_st[r, g * HW:(g + 1) * HW])
                                if g == 0:
                                    step(ins)
                            ins.then_inc(st_ready, 1)
                    dve.wait_ge(gm_ready, c + 1)
                    for h in range(SSD_HEADS):
                        u = c * SSD_HEADS + h
                        dve.wait_ge(l_ready, u + 1)
                        if u >= 2:
                            dve.wait_ge(ydiag_done, u - 1)
                        dve.tensor_tensor(MT[:, u % 2, :], L[:, u % 2, :], Gm[:, c % 2, h // 4, :],
                                          ALU.mult).then_inc(mt_ready, 1)
                    y13, y23 = (t[:].rearrange("p (h d) -> p h d", **h8) for t in (y1, y2))
                    step(dve.tensor_tensor(y13, xc, bc(dsk, 2, HD), ALU.mult))
                    if c >= 1:
                        dve.wait_ge(yoff_done, c)
                        for g in range(2):
                            hs = slice(4 * g, 4 * g + 4)
                            step(dve.tensor_tensor(y23[:, hs], b_off[g][:, 0:HW].rearrange("p (h d) -> p h d", h=4),
                                                   bc(decay[:, 2, c * 8 + 4 * g:c * 8 + 4 * g + 4], 2, HD), ALU.mult))
                        step(dve.tensor_tensor(y1[:], y1[:], y2[:], ALU.add))
                    dve.wait_ge(ydiag_done, (c + 1) * SSD_HEADS)
                    dve.tensor_tensor(y2[:], y1[:], b_y[:], ALU.add).then_inc(y_free, 1)
                    dve.wait_ge(y_free, c + 1)
                    step(dve.tensor_tensor(k.y[:, c, :], y2[:], k.sz[:, c, :], ALU.mult))
                    step(dve.tensor_tensor(yy[:], k.y[:, c, :], k.y[:, c, :], ALU.mult))
                    step(dve.reduce_sum(ms[:, c, 2:3], yy[:], AX))
                    dve.tensor_scalar(ms[:, c, 0:1], ms[:, c, 2:3], 1.0 / 512, LN_EPS, ALU.mult,
                                      ALU.add).then_inc(sq_ready, 1)
                for c in range(TT):
                    dve.wait_ge(rms_ready, c + 1)
                    step(dve.reciprocal(ms[:, c, 2:3], ms[:, c, 1:2]))
                    step(dve.scalar_tensor_tensor(k.y[:, c, :], k.y[:, c, :], ms[:, c, 2:3], nw, ALU.mult, ALU.mult))


def layer_norm(k, name, x, g, b, extra=None):
    nc = k.nc
    with ExitStack() as s:
        vec = k.sb(s, f"{name}_gb", [P, 2, DM])
        stats = k.sb(s, f"{name}_stats", [P, TT, 2, 6])
        mv = k.sb(s, f"{name}_mv", [P, TT, 2])
        sd = k.sb(s, f"{name}_sd", [P, 3, TT])
        tmp = k.sb(s, f"{name}_tmp", [P, DM])
        vec_in, var_ready, sd_ready, step_d = (k.sem(f"{name}_{n}") for n in ("vecin", "var", "sd", "step"))
        with nc.Block() as block:
            @block.sync
            def _(sp):
                sp.dma_start(vec[:, 0, :], k.vec(g)).then_inc(vec_in, 16)
                sp.dma_start(vec[:, 1, :], k.vec(b)).then_inc(vec_in, 16)

            @block.vector
            def _(dve):
                step = Chain(dve, step_d)
                for tt in range(TT):
                    step(dve.bn_stats(stats[:, tt, 0, :], x[:, tt, 0:512]))
                    step(dve.bn_stats(stats[:, tt, 1, :], x[:, tt, 512:1024]))
                    step(dve.bn_aggr(mv[:, tt, :], stats[:, tt, :, :].rearrange("p a b -> p (a b)")))
                dve.tensor_scalar(sd[:, 0, :], mv[:, :, 1], LN_EPS, None, ALU.add).then_inc(var_ready, 1)
                dve.wait_ge(vec_in, 32)
                dve.wait_ge(sd_ready, 1)
                step(dve.reciprocal(sd[:, 2, :], sd[:, 1, :]))
                for tt in range(TT):
                    step(dve.tensor_scalar(tmp[:], x[:, tt, :], mv[:, tt, 0:1], sd[:, 2, tt:tt + 1], ALU.subtract,
                                           ALU.mult))
                    step(dve.tensor_tensor(tmp[:], tmp[:], vec[:, 0, :], ALU.mult))
                    step(dve.tensor_tensor(x[:, tt, :], tmp[:], vec[:, 1, :], ALU.add))

            @block.scalar
            def _(act):
                act.wait_ge(var_ready, 1)
                act.activation(sd[:, 1, :], sd[:, 0, :], ACT.Sqrt).then_inc(sd_ready, 1)


def rms_rows(k, name, x, out, gain, width=DM, eps=EPS):
    nc = k.nc
    with ExitStack() as s:
        vec = k.sb(s, f"{name}_gain", [P, width])
        sq = k.sb(s, f"{name}_sq", [P, 2, width])
        m = k.sb(s, f"{name}_ms", [P, 4, TT])
        vec_in, summed, sd_ready, ms_ready, step_d = (k.sem(f"{name}_{n}") for n in ("vecin", "sum", "sd", "ms", "step"))
        with nc.Block() as block:
            @block.sync
            def _(sp):
                sp.dma_start(vec[:], k.vec(gain)).then_inc(vec_in, 16)

            @block.scalar
            def _(act):
                for tt in range(TT):
                    act.activation(sq[:, tt % 2, :], x(tt), ACT.Square, accum_out=m[:, 0, tt:tt + 1]).then_inc(summed, 1)
                    act.wait_ge(summed, tt + 1)
                act.wait_ge(ms_ready, 1)
                act.activation(m[:, 2, :], m[:, 1, :], ACT.Sqrt).then_inc(sd_ready, 1)

            @block.vector
            def _(dve):
                step = Chain(dve, step_d)
                dve.wait_ge(summed, TT)
                dve.tensor_scalar(m[:, 1, :], m[:, 0, :], 1.0 / width, eps, ALU.mult, ALU.add).then_inc(ms_ready, 1)
                dve.wait_ge(sd_ready, 1)
                step(dve.reciprocal(m[:, 3, :], m[:, 2, :]))
                dve.wait_ge(vec_in, 16)
                for tt in range(TT):
                    step(dve.scalar_tensor_tensor(out(tt), x(tt), m[:, 3, tt:tt + 1], vec[:], ALU.mult, ALU.mult))


def project(k, name, lhsT, chunks, load, evac, kd=KD, wbuf=2, evac_scalar=None):
    nc = k.nc
    n = len(chunks)
    with ExitStack() as s:
        w = k.sb(s, f"{name}_w", [P, wbuf, kd, max(chunks)])
        banks = [k.ps(s, f"{name}_bank{i}") for i in range(4)]
        w_in = [k.sem(f"{name}_w_in{i}") for i in range(wbuf)]
        done, free, step_d = k.sem(f"{name}_done"), k.sem(f"{name}_free"), k.sem(f"{name}_step")
        with nc.Block() as block:
            @block.sync
            def _(sp):
                for i in range(n):
                    if i >= wbuf:
                        sp.wait_ge(done, TT * (i - wbuf + 1))
                    sp.dma_start(w[:, i % wbuf, :, 0:chunks[i]], load(i)).then_inc(w_in[i % wbuf], 16)

            @block.tensor
            def _(pe):
                for i in range(n):
                    pe.wait_ge(w_in[i % wbuf], 16 * (i // wbuf + 1))
                    for tt in range(TT):
                        j = i * TT + tt
                        if j >= 4:
                            pe.wait_ge(free, j - 3)
                        for c in range(kd):
                            ins = pe.matmul(banks[j % 4][:, 0:chunks[i]], lhsT(tt, c), w[:, i % wbuf, c, 0:chunks[i]],
                                            start=(c == 0), stop=(c == kd - 1))
                        ins.then_inc(done, 1)

            @block.vector
            def _(dve):
                step = Chain(dve, step_d)
                for i in range(n):
                    for tt in range(TT):
                        dve.wait_ge(done, i * TT + tt + 1)
                        evac(dve, step, i, tt, banks[(i * TT + tt) % 4]).then_inc(free, 1)
                        dve.wait_ge(free, i * TT + tt + 1)


def route(k, name, E, G, bias, logits_w, ctx):
    nc = k.nc
    PG, NT, W = E // G, most_tiles(E), G + E
    k.gate = k.sb(ctx, f"{name}_gate", [P, 2, TT])
    k.slot = k.sb(ctx, f"{name}_slot", [P, 2, TT], U32)
    k.tok_of = k.sb(ctx, f"{name}_tok_of", [P, NT], U32)
    k.exp_of = k.sb(ctx, f"{name}_exp_of", [1, NT], I32)
    with ExitStack() as s:
        wr = k.sb(s, f"{name}_wr", [P, KD, W])
        bv = k.sb(s, f"{name}_bv", [P, W])
        lg = k.sb(s, f"{name}_lg", [P, TT, W])
        small = [k.sb(s, f"{name}_small{i}", [P, TT]) for i in range(8)]
        g4 = [k.sb(s, f"{name}_g{i}", [P, TT, G]) for i in range(4)]
        e4 = [k.sb(s, f"{name}_e{i}", [P, TT, PG]) for i in range(6)]
        wide = k.sb(s, f"{name}_wide", [P, TT, G, PG])
        OH = [k.sb(s, f"{name}_oh{i}", [P, TT, G, PG]) for i in range(2)]
        M = k.sb(s, f"{name}_m", [P, TT, E])
        tiles, cum, base, zero = (k.sb(s, f"{name}_{n}", [P, E]) for n in ("tiles", "cum", "base", "zero"))
        rank = k.sb(s, f"{name}_rank", [P, TT, E])
        counts = k.sb(s, f"{name}_counts", [P, E])
        cmp = k.sb(s, f"{name}_cmp", [1, NT, E])
        tef = k.sb(s, f"{name}_tef", [1, NT])
        pos, q, jt, r, slotf = (k.sb(s, f"{name}_{n}", [P, 2, TT]) for n in ("pos", "q", "jt", "r", "slotf"))
        ohr = k.sb(s, f"{name}_ohr", [P, 2 * TT, P])
        ohj = k.sb(s, f"{name}_ohj", [P, 2 * TT, NT])
        lbank, rbank, tbank = (k.ps(s, f"{name}_{n}") for n in ("lbank", "rbank", "tbank"))
        (in_ready, logits_done, step_d, diff_ready, exp_ready, m_ready, rank_done, oh_ready, tok_done) = (
            k.sem(f"{name}_{n}") for n in ("in", "logits", "step", "diff", "exp", "mready", "rank", "oh", "tok"))
        with nc.Block() as block:
            @block.sync
            def _(sp):
                sp.dma_start(wr[:], logits_w).then_inc(in_ready, 16)
                sp.dma_start(bv[:], k.vec(bias)).then_inc(in_ready, 16)

            @block.tensor
            def _(pe):
                pe.wait_ge(in_ready, 32)
                for tt in range(TT):
                    for c in range(KD):
                        ins = pe.matmul(lbank[:, tt * W:(tt + 1) * W], k.xT[:, c, tt * P:(tt + 1) * P], wr[:, c, :],
                                        start=(c == 0), stop=(c == KD - 1))
                ins.then_inc(logits_done, 1)
                pe.wait_ge(m_ready, 1)
                for tt in range(TT):
                    for t in range(tt + 1):
                        pe.matmul(rbank[:, tt * E:(tt + 1) * E], k.c("before" if t == tt else "ones"), M[:, t, :],
                                  start=(t == 0), stop=(t == tt))
                for t in range(TT):
                    ins = pe.matmul(rbank[:, TT * E:(TT + 1) * E], k.c("ones"), M[:, t, :], start=(t == 0),
                                    stop=(t == TT - 1))
                ins.then_inc(rank_done, 1)
                pe.wait_ge(oh_ready, 1)
                for i in range(2 * TT):
                    ins = pe.matmul(tbank[:, 0:NT], ohr[:, i, :], ohj[:, i, :], start=(i == 0), stop=(i == 2 * TT - 1))
                ins.then_inc(tok_done, 1)

            @block.scalar
            def _(act):
                act.wait_ge(diff_ready, 1)
                act.activation(g4[1][:], g4[0][:], ACT.Exp).then_inc(exp_ready, 1)
                act.wait_ge(diff_ready, 2)
                act.activation(small[5][:], small[4][:], ACT.Exp).then_inc(exp_ready, 1)

            @block.vector
            def _(dve):
                step = Chain(dve, step_d)

                def first_best(x, best, down, key, onehot, n):
                    step(dve.reduce_max(best[:], x, AX))
                    step(dve.tensor_tensor(key, x, bc(best[:], 2, n), ALU.is_equal))
                    step(dve.tensor_tensor(key, key, down, ALU.mult))
                    step(dve.reduce_max(small[7][:], key, AX))
                    step(dve.tensor_tensor(onehot, key, bc(small[7][:], 2, n), ALU.is_equal))

                def down(n):
                    a = k.c("down")[:, P - n:P]
                    return bc(a, 1, TT)

                dve.wait_ge(in_ready, 32)
                dve.wait_ge(logits_done, 1)
                step(dve.tensor_tensor(lg[:], lbank[:, 0:TT * W].rearrange("p (t w) -> p t w", t=TT), bc(bv[:], 1, TT),
                                       ALU.add))
                gl = lg[:, :, 0:G]
                first_best(gl, small[0], down(G), g4[2][:], g4[3][:], G)
                dve.tensor_tensor(g4[0][:], gl, bc(small[0][:], 2, G), ALU.subtract).then_inc(diff_ready, 1)
                dve.wait_ge(exp_ready, 1)
                step(dve.reduce_sum(small[1][:], g4[1][:], AX))
                step(dve.reciprocal(small[2][:], small[1][:]))
                step(dve.tensor_tensor(wide[:], lg[:, :, G:W].rearrange("p t (g e) -> p t g e", g=G),
                                       bc(g4[3][:], 3, PG), ALU.mult))
                step(dve.reduce_sum(e4[0][:], wide[:].rearrange("p t g e -> p t e g"), AX))
                first_best(e4[0][:], small[1], down(PG), e4[1][:], e4[2][:], PG)
                step(dve.scalar_tensor_tensor(e4[3][:], e4[2][:], NEG, e4[0][:], ALU.mult, ALU.add))
                first_best(e4[3][:], small[3], down(PG), e4[1][:], e4[4][:], PG)
                dve.tensor_tensor(small[4][:], small[3][:], small[1][:], ALU.subtract).then_inc(diff_ready, 1)
                dve.wait_ge(exp_ready, 2)
                step(dve.tensor_scalar(small[6][:], small[5][:], 1.0, None, ALU.add))
                step(dve.reciprocal(small[0][:], small[6][:]))
                step(dve.tensor_tensor(k.gate[:, 0, :], small[0][:], small[2][:], ALU.mult))
                step(dve.tensor_tensor(k.gate[:, 1, :], k.gate[:, 0, :], small[5][:], ALU.mult))
                for i, oh in enumerate((e4[2], e4[4])):
                    for tt in range(TT):
                        step(dve.tensor_tensor(OH[i][:, tt], bc(g4[3][:, tt, :], 2, PG), bc(oh[:, tt, :], 1, G), ALU.mult))
                flat = [o[:].rearrange("p t g e -> p t (g e)") for o in OH]
                dve.tensor_tensor(M[:], flat[0], flat[1], ALU.add).then_inc(m_ready, 1)
                dve.wait_ge(rank_done, 1)
                step(dve.tensor_copy(rank[:], rbank[:, 0:TT * E].rearrange("p (t e) -> p t e", t=TT)))
                step(dve.tensor_copy(counts[:], rbank[:, TT * E:(TT + 1) * E]))
                step(dve.memset(zero[:], 0.0))
                step(dve.tensor_scalar(tiles[:], counts[:], 0.5, None, ALU.is_gt))
                for j in range(1, TT):
                    step(dve.scalar_tensor_tensor(tiles[:], counts[:], j * P + 0.5, tiles[:], ALU.is_gt, ALU.add))
                step(dve.tensor_tensor_scan(cum[:], tiles[:], zero[:], 0.0, ALU.add, ALU.add))
                step(dve.tensor_tensor(base[:], cum[:], tiles[:], ALU.subtract))
                for i in range(2):
                    step(dve.tensor_tensor(M[:], flat[i], rank[:], ALU.mult))
                    step(dve.reduce_sum(pos[:, i, :], M[:], AX))
                    step(dve.tensor_tensor(M[:], flat[i], bc(base[:], 1, TT), ALU.mult))
                    step(dve.reduce_sum(jt[:, i, :], M[:], AX))
                step(dve.scalar_tensor_tensor(slotf[:], jt[:], float(P), pos[:], ALU.mult, ALU.add))
                step(dve.tensor_copy(k.slot[:], slotf[:]))
                step(dve.tensor_scalar(q[:], pos[:], P - 0.5, None, ALU.is_gt))
                for j in range(2, TT):
                    step(dve.scalar_tensor_tensor(q[:], pos[:], j * P - 0.5, q[:], ALU.is_gt, ALU.add))
                step(dve.tensor_tensor(jt[:], jt[:], q[:], ALU.add))
                step(dve.scalar_tensor_tensor(r[:], q[:], -float(P), pos[:], ALU.mult, ALU.add))
                for i in range(2):
                    for tt in range(TT):
                        step(dve.tensor_scalar(ohr[:, i * TT + tt, :], k.c("iota"), r[:, i, tt:tt + 1], None,
                                               ALU.is_equal))
                        ins = dve.tensor_scalar(ohj[:, i * TT + tt, :], k.c("iota")[:, 0:NT], jt[:, i, tt:tt + 1],
                                                k.c("tok")[:, tt:tt + 1], ALU.is_equal, ALU.mult)
                        if (i, tt) != (1, TT - 1):
                            step(ins)
                ins.then_inc(oh_ready, 1)
                step(dve.tensor_tensor(cmp[:], bc(k.c("iota")[0:1, 0:NT], 2, E), bc(base[0:1, :], 1, NT), ALU.is_ge))
                step(dve.reduce_sum(tef[:], cmp[:], AX))
                step(dve.tensor_scalar(k.exp_of[:], tef[:], -1.0, None, ALU.add))
                dve.wait_ge(tok_done, 1)
                step(dve.tensor_copy(k.tok_of[:], tbank[:, 0:NT]))


def experts(k, name, E, rows, w_gu, w_dn, out_rows, x_store):
    nc = k.nc
    NT = most_tiles(E)
    GU, DN = KD * 2 * FF, 2 * DM
    with ExitStack() as s:
        w1 = [k.sb(s, f"{name}_w1_{i}", [P, GU]) for i in range(2)]
        w2 = [k.sb(s, f"{name}_w2_{i}", [P, DN]) for i in range(2)]
        xg = [k.sb(s, f"{name}_xg{i}", [P, DM]) for i in range(2)]
        idx = [k.sb(s, f"{name}_idx{i}", [P, 1], U32) for i in range(2)]
        xT = [k.sb(s, f"{name}_xT{i}", [P, DM]) for i in range(2)]
        sg = k.sb(s, f"{name}_sg", [P, FF])
        hid = k.sb(s, f"{name}_hid", [P, FF])
        hT = k.sb(s, f"{name}_hT", [P, FF])
        y = [k.sb(s, f"{name}_y{i}", [P, DM]) for i in range(2)]
        xbank = k.ps(s, f"{name}_xbank", (P, 1024))
        gbank = [k.ps(s, f"{name}_gbank{i}") for i in range(2)]
        hbank = k.ps(s, f"{name}_hbank")
        ybank = k.ps(s, f"{name}_ybank", (P, 1024))
        w1_in, w2_in, y_out = ([k.sem(f"{name}_{n}{b}") for b in range(2)] for n in ("w1", "w2", "yout"))
        x_in, x_base = k.gather_sems[0:2], k.gathered[0:2]
        (stored, idx_ready, idx_seen, x_turned, xT_v, xT_s, gu_done, silu_ready, hid_ready, h_turned,
         hT_ready, y_done, y_v, y_s) = (k.sem(f"{name}_{n}") for n in (
             "stored", "idx", "idx_seen", "x_turned", "xT_v", "xT_s", "gu", "silu", "hid", "h_turned",
             "hT", "y_done", "y_v", "y_s"))

        with nc.Block() as block:
            @block.sync
            def _(sp):
                for tt in range(TT):
                    sp.dma_start(rows[tt * P:(tt + 1) * P, :], x_store(tt)).then_inc(stored, 16)

                def tile(i, b, first=False):
                    t = 2 * i + b
                    e = sp.value_load(k.exp_of[0:1, bass.ds(t, 1)], min_val=0, max_val=E - 1)
                    if not first:
                        sp.wait_ge(gu_done, t - 1)
                    sp.dma_start(w1[b][:], w_gu[bass.ds(e, 1)].rearrange("a p n -> (a p) n")).then_inc(w1_in[b], 16)
                    if not first:
                        sp.wait_ge(y_done, t - 1)
                    sp.dma_start(w2[b][:], w_dn[bass.ds(e, 1)].rearrange("a p n -> (a p) n")).then_inc(w2_in[b], 16)

                tile(0, 0, True)
                tile(0, 1, True)
                with sp.Fori(1, NT // 2) as i:
                    for b in range(2):
                        tile(i, b)
                if NT % 2:
                    tile(NT // 2, 0)
                sp.wait_ge(y_out[0], 16 * ((NT + 1) // 2))
                sp.wait_ge(y_out[1], 16 * (NT // 2))

            @block.gpsimd
            def _(pool):
                pool.wait_ge(stored, 16 * TT)

                def tile(i, b, first=False):
                    t = 2 * i + b
                    if not first:
                        pool.wait_ge(x_turned, t - 1)
                    pool.tensor_copy(idx[b][:], k.tok_of[:, bass.ds(t, 1)]).then_inc(idx_ready, 1)
                    pool.wait_ge(idx_ready, t + 1)
                    pool.sem_inc(idx_seen, 1)
                    pool.indirect_dma_start(xg[b][:], None, rows,
                                            bass.IndirectOffsetOnAxis(ap=idx[b][:], axis=0)).then_inc(x_in[b], 16)

                tile(0, 0, True)
                tile(0, 1, True)
                with pool.Fori(1, NT // 2) as i:
                    for b in range(2):
                        tile(i, b)
                if NT % 2:
                    tile(NT // 2, 0)

            @block.tensor
            def _(pe):
                def turn_x(i, b):
                    t = 2 * i + b
                    pe.wait_ge(x_in[b], 16 * i + (x_base[b] + 16))
                    pe.wait_ge(xT_v, t)
                    pe.wait_ge(xT_s, t)
                    for c in range(KD):
                        ins = pe.transpose(xbank[:, c * P:(c + 1) * P], xg[b][:, c * P:(c + 1) * P], k.c("ident"))
                    ins.then_inc(x_turned, 1)

                def tile(i, b, last=False):
                    t = 2 * i + b
                    pe.wait_ge(w1_in[b], 16 * i + 16)
                    pe.wait_ge(xT_v, t + 1)
                    pe.wait_ge(xT_s, t + 1)
                    for c in range(KD):
                        ins = pe.matmul(gbank[b][:], xT[b][:, c * P:(c + 1) * P], w1[b][:, c * 2 * FF:(c + 1) * 2 * FF],
                                        start=(c == 0), stop=(c == KD - 1))
                    ins.then_inc(gu_done, 1)
                    if not last:
                        turn_x(i + b, 1 - b)
                    pe.wait_ge(hid_ready, t + 1)
                    for c in range(2):
                        ins = pe.transpose(hbank[:, c * P:(c + 1) * P], hid[:, c * P:(c + 1) * P], k.c("ident"))
                    ins.then_inc(h_turned, 1)
                    pe.wait_ge(w2_in[b], 16 * i + 16)
                    pe.wait_ge(hT_ready, t + 1)
                    pe.wait_ge(y_v, t)
                    pe.wait_ge(y_s, t)
                    for m in range(2):
                        for c in range(2):
                            ins = pe.matmul(ybank[:, m * 512:(m + 1) * 512], hT[:, c * P:(c + 1) * P],
                                            w2[b][:, c * DM + m * 512:c * DM + (m + 1) * 512], start=(c == 0),
                                            stop=(c == 1))
                    ins.then_inc(y_done, 1)

                pe.wait_ge(x_in[0], x_base[0] + 16)
                for c in range(KD):
                    ins = pe.transpose(xbank[:, c * P:(c + 1) * P], xg[0][:, c * P:(c + 1) * P], k.c("ident"))
                ins.then_inc(x_turned, 1)
                tile(0, 0)
                tile(0, 1)
                with pe.Fori(1, (NT - 1) // 2) as i:
                    for b in range(2):
                        tile(i, b)
                for t in range(2 * ((NT - 1) // 2), NT):
                    tile(t // 2, t % 2, last=(t == NT - 1))

            @block.vector
            def _(dve):
                def copy_x(t, b):
                    dve.wait_ge(x_turned, t + 1)
                    dve.tensor_copy(xT[b][:, 0:512], xbank[:, 0:512]).then_inc(xT_v, 1)

                def tile(i, b, last=False):
                    t = 2 * i + b
                    dve.wait_ge(silu_ready, t + 1)
                    dve.wait_ge(gu_done, t + 1)
                    dve.tensor_tensor(hid[:], sg[:], gbank[b][:, FF:2 * FF], ALU.mult).then_inc(hid_ready, 1)
                    if not last:
                        copy_x(t + 1, 1 - b)
                    dve.wait_ge(h_turned, t + 1)
                    dve.tensor_copy(hT[:], hbank[:, 0:FF]).then_inc(hT_ready, 1)
                    dve.wait_ge(y_done, t + 1)
                    dve.wait_ge(y_out[b], 16 * i)
                    dve.tensor_copy(y[b][:, 0:512], ybank[:, 0:512]).then_inc(y_v, 1)

                copy_x(0, 0)
                tile(0, 0)
                tile(0, 1)
                with dve.Fori(1, (NT - 1) // 2) as i:
                    for b in range(2):
                        tile(i, b)
                for t in range(2 * ((NT - 1) // 2), NT):
                    tile(t // 2, t % 2, last=(t == NT - 1))

            @block.scalar
            def _(act):
                def copy_x(t, b):
                    act.wait_ge(x_turned, t + 1)
                    act.activation(xT[b][:, 512:1024], xbank[:, 512:1024], ACT.Copy).then_inc(xT_s, 1)

                def tile(i, b, last=False):
                    t = 2 * i + b
                    act.wait_ge(gu_done, t + 1)
                    act.wait_ge(hid_ready, t)
                    act.activation(sg[:], gbank[b][:, 0:FF], ACT.Silu).then_inc(silu_ready, 1)
                    if not last:
                        copy_x(t + 1, 1 - b)
                    act.wait_ge(y_done, t + 1)
                    act.wait_ge(y_out[b], 16 * i)
                    act.activation(y[b][:, 512:1024], ybank[:, 512:1024], ACT.Copy).then_inc(y_s, 1)
                    act.wait_ge(y_s, t + 1)
                    act.wait_ge(y_v, t + 1)
                    act.dma_start(out_rows[bass.ds(t * P, P), :], y[b][:]).then_inc(y_out[b], 16)

                copy_x(0, 0)
                tile(0, 0)
                tile(0, 1)
                with act.Fori(1, (NT - 1) // 2) as i:
                    for b in range(2):
                        tile(i, b)
                for t in range(2 * ((NT - 1) // 2), NT):
                    tile(t // 2, t % 2, last=(t == NT - 1))
    for b in range(2):
        k.gathered[b] += 16 * ((NT + 1 - b) // 2)


def combine(k, name, out_rows, x, scale, out=None):
    nc = k.nc
    with ExitStack() as s:
        yr = [k.sb(s, f"{name}_row{i}", [P, DM]) for i in range(4)]
        idx = k.sb(s, f"{name}_cidx", [P, 8], U32)
        row_in, row_base = k.gather_sems[2:6], k.gathered[2:6]
        idx_ready, used, step_d, done, out_done = (k.sem(f"{name}_{n}") for n in ("cidx", "used", "step", "xdone",
                                                                                 "outd"))
        with nc.Block() as block:
            @block.gpsimd
            def _(pool):
                for j in range(2 * TT):
                    tt, i = divmod(j, 2)
                    if j >= 4:
                        pool.wait_ge(used, j - 3)
                    pool.indirect_dma_start(yr[j % 4][:], None, out_rows, bass.IndirectOffsetOnAxis(
                        ap=k.slot[:, i, tt:tt + 1], axis=0)).then_inc(row_in[j % 4], 16)

            @block.vector
            def _(dve):
                step = Chain(dve, step_d)
                for tt in range(TT):
                    if scale != 1.0:
                        step(dve.tensor_scalar(x[:, tt, :], x[:, tt, :], scale, None, ALU.mult))
                    for i in range(2):
                        j = 2 * tt + i
                        dve.wait_ge(row_in[j % 4], row_base[j % 4] + 16 * (j // 4 + 1))
                        dve.scalar_tensor_tensor(x[:, tt, :], yr[j % 4][:], k.gate[:, i, tt:tt + 1], x[:, tt, :],
                                                 ALU.mult, ALU.add).then_inc(used, 1)
                        dve.wait_ge(used, j + 1)

            if out is not None:
                @block.sync
                def _(sp):
                    for tt in range(TT):
                        sp.wait_ge(used, 2 * tt + 2)
                        sp.dma_start(out[tt * P:(tt + 1) * P, :], x[:, tt, :]).then_inc(out_done, 16)
                    sp.wait_ge(out_done, 16 * TT)
    for b in range(4):
        k.gathered[2 + b] += 16 * (2 * TT // 4)


def head_norms(k, name, items, eps=EPS):
    nc = k.nc
    n = len(items)
    with ExitStack() as s:
        H, D = items[0][0].shape[2:]
        sq = k.sb(s, f"{name}_sq", [P, 2, H, D])
        m = k.sb(s, f"{name}_m", [P, n, 4, TT, H])
        summed, squared, ms_ready, sd_ready, step_d = (k.sem(f"{name}_{x}") for x in ("sum", "sq", "ms", "sd", "step"))
        with nc.Block() as block:
            @block.scalar
            def _(act):
                for j in range(n * TT):
                    i, tt = divmod(j, TT)
                    if j >= 2:
                        act.wait_ge(summed, j - 1)
                    act.activation(sq[:, j % 2], items[i][0][:, tt], ACT.Square).then_inc(squared, 1)
                for i in range(n):
                    act.wait_ge(ms_ready, i + 1)
                    act.activation(m[:, i, 2], m[:, i, 1], ACT.Sqrt).then_inc(sd_ready, 1)

            @block.vector
            def _(dve):
                step = Chain(dve, step_d)
                for j in range(n * TT):
                    i, tt = divmod(j, TT)
                    dve.wait_ge(squared, j + 1)
                    dve.reduce_sum(m[:, i, 0, tt], sq[:, j % 2], AX).then_inc(summed, 1)
                for i, (x, gain, scale) in enumerate(items):
                    dve.wait_ge(summed, (i + 1) * TT)
                    dve.tensor_scalar(m[:, i, 1], m[:, i, 0], 1.0 / D / scale ** 2, eps / scale ** 2, ALU.mult,
                                      ALU.add).then_inc(ms_ready, 1)
                for i, (x, gain, scale) in enumerate(items):
                    dve.wait_ge(sd_ready, i + 1)
                    step(dve.reciprocal(m[:, i, 3], m[:, i, 2]))
                    for tt in range(TT):
                        step(dve.tensor_tensor(x[:, tt], x[:, tt], bc(m[:, i, 3, tt], 2, D), ALU.mult))
                        step(dve.tensor_tensor(x[:, tt], x[:, tt], bc(gain, 1, H), ALU.mult))


def copy_evac(dst):
    def evac(dve, step, i, tt, bank):
        o = dst(i, tt)
        return dve.tensor_copy(o, bank[:, 0:o.shape[-1]])
    return evac


def rope_tables(k, cos, sin):
    nc, d = k.nc, k.d
    two_pi = [6.28125, 0.0019340515136718750, 1.2554228305816650e-06]
    two_pi.append(float(2 * np.pi - np.sum(np.array(two_pi, np.float64))))
    MAGIC = 12582912.0
    EDGE = 3.1415925
    with ExitStack() as s:
        pi32 = k.sb(s, "pos_i", [P, TT], I32)
        pos = k.sb(s, "pos_f", [P, TT])
        ang, turns, r, c, over = (k.sb(s, f"ang{i}", [P, TT, 16]) for i in range(5))
        pos_in, red, done, step_d = k.sem("pos_in"), k.sem("angle_red"), k.sem("angle_done"), k.sem("angle_step")
        with nc.Block() as block:
            @block.sync
            def _(sp):
                sp.dma_start(pi32[:], d["positions"]).then_inc(pos_in, 16)

            @block.vector
            def _(dve):
                step = Chain(dve, step_d)
                dve.wait_ge(pos_in, 16)
                step(dve.tensor_copy(pos[:], pi32[:]))
                step(dve.tensor_tensor(ang[:], bc(pos[:], 2, 16), bc(k.c("freq"), 1, TT), ALU.mult))
                step(dve.tensor_scalar(turns[:], ang[:], 1.0 / (2 * np.pi), MAGIC, ALU.mult, ALU.add))
                step(dve.tensor_scalar(turns[:], turns[:], -MAGIC, None, ALU.add))
                for i, part in enumerate(two_pi):
                    step(dve.scalar_tensor_tensor(r[:], turns[:], -part, r[:] if i else ang[:], ALU.mult, ALU.add))
                step(dve.tensor_scalar(c[:], r[:], float(np.pi / 2), None, ALU.add))
                step(dve.tensor_scalar(over[:], c[:], float(np.pi), -2 * float(np.pi), ALU.is_gt, ALU.mult))
                step(dve.tensor_tensor(c[:], c[:], over[:], ALU.add))
                step(dve.tensor_scalar(c[:], c[:], EDGE, -EDGE, ALU.min, ALU.max))
                dve.tensor_scalar(r[:], r[:], EDGE, -EDGE, ALU.min, ALU.max).then_inc(red, 1)

            @block.scalar
            def _(act):
                act.wait_ge(red, 1)
                act.activation(cos[:], c[:], ACT.Sin).then_inc(done, 1)
                act.activation(sin[:], r[:], ACT.Sin).then_inc(done, 1)


def latent_attention(k, ctx):
    nc, d = k.nc, k.d
    k.o_mla = k.sb(ctx, "o_mla", [P, TT, 512])
    with ExitStack() as s:
        kv = k.sb(s, "kv", [P, TT, 1024])
        qT, kT = (k.sb(s, n, [MLA_D, 8, SEQ]) for n in ("mla_qT", "mla_kT"))
        with ExitStack() as s1:
            nat = k.sb(s1, "mla_nat", [P, TT, MLA_COLS])
            kf = k.sb(s1, "mla_k", [P, TT, 8, MLA_D])
            cos, sin = k.sb(s1, "cos2", [P, TT, 16]), k.sb(s1, "sin2", [P, TT, 16])
            ckvT = k.sb(s1, "ckvT", [P, 2, SEQ])
            gains = k.sb(s1, "mla_gains", [P, 2 * MLA_D])
            widths = [384, 384, 288]
            project(k, "mla", lambda tt, c: k.xT[:, c, tt * P:(tt + 1) * P], widths,
                    lambda i: d["w_mla"][:, :, 384 * i:384 * i + widths[i]],
                    copy_evac(lambda i, tt: nat[:, tt, 384 * i:384 * i + widths[i]]))
            rope_tables(k, cos, sin)
            ckv = lambda tt: nat[:, tt, 768:1024]
            rms_rows(k, "ckv", ckv, ckv, "norm_ckv", 256)
            transpose_tiles(k, "ckvT", lambda tt, b: nat[:, tt, 768 + b * P:768 + (b + 1) * P],
                            lambda b: ckvT[:, b, :], 2)
            project(k, "ukv", lambda tt, c: ckvT[:, c, tt * P:(tt + 1) * P], [512, 512],
                    lambda i: d["w_ukv"][:, :, i * 512:(i + 1) * 512],
                    copy_evac(lambda i, tt: kv[:, tt, i * 512:(i + 1) * 512]), kd=2)
            q4 = nat[:, :, 0:768].rearrange("p t (h e) -> p t h e", h=8)
            kv4 = kv[:].rearrange("p t (h e) -> p t h e", h=8)
            gains_in, built = k.sem("gains_in"), k.sem("k_built")
            with nc.Block() as block:
                @block.sync
                def _(sp):
                    a = VEC_AT["q_norm_mla"][0]
                    sp.dma_start(gains[:], k.d["vecs"][:, a:a + 2 * MLA_D]).then_inc(gains_in, 16)
                    sp.wait_ge(gains_in, 16)

                @block.vector
                def _(dve):
                    for tt in range(TT):
                        dve.tensor_copy(kf[:, tt, :, 0:64], kv4[:, tt, :, 0:64]).then_inc(built, 1)
                        dve.tensor_copy(kf[:, tt, :, 64:96], bc(nat[:, tt, 1024:1056], 1, 8)).then_inc(built, 1)
                    dve.wait_ge(built, 2 * TT)
            head_norms(k, "mlanorm", [(q4, gains[:, 0:MLA_D], MLA_D ** -0.5), (kf[:], gains[:, MLA_D:], 1.0)])
            with ExitStack() as s2:
                t = [k.sb(s2, f"rope_t{i}", [P, TT, 8, 16]) for i in range(4)]
                step_d = k.sem("rope2_step")
                with nc.Block() as block:
                    @block.vector
                    def _(dve):
                        step = Chain(dve, step_d)
                        C, S = bc(cos[:], 2, 8), bc(sin[:], 2, 8)
                        for x in (q4, kf[:]):
                            for tt in range(TT):
                                a, b = x[:, tt, :, 64:80], x[:, tt, :, 80:96]
                                for o, v, w in ((0, a, C), (1, b, S), (2, b, C), (3, a, S)):
                                    step(dve.tensor_tensor(t[o][:, tt], v, w[:, tt], ALU.mult))
                                step(dve.tensor_tensor(a, t[0][:, tt], t[1][:, tt], ALU.subtract))
                                step(dve.tensor_tensor(b, t[2][:, tt], t[3][:, tt], ALU.add))
            transpose_tiles(k, "mlaT", lambda tt, b: (q4 if b < 8 else kf[:])[:, tt, b % 8, :],
                            lambda b: (qT if b < 8 else kT)[:, b % 8, :], 16)
        units = []
        for tt in range(TT):
            w = (tt + 1) * P
            for h in range(8):
                units.append(dict(q=qT[:, h, tt * P:w], keys=kT[:, h, 0:w],
                                  masks=[(k.cb("ident_b"), k.cb("causal_b"), tt * P, w)],
                                  values=[kv[:, b, h * P + HD:(h + 1) * P] for b in range(tt + 1)]))
        attention(k, "mlaatt", units, lambda g: k.o_mla[:, g, :].rearrange("p (h d) -> p h d", h=8))


def dilated_attention(k, ctx):
    nc, d = k.nc, k.d
    k.o_dil = k.sb(ctx, "o_dil", [P, TT, 512])
    NG, NU = len(DIL), TT * 8
    with ExitStack() as s:
        o_raw = k.sb(s, "o_raw", [P, NG, TT, 512])
        nmax, den = k.sb(s, "dil_nmax", [P, NG, NU]), k.sb(s, "dil_den", [P, NG, NU])
        gains = k.sb(s, "dil_gains", [P, 2 * NG * HD])
        gains_in = k.sem("dil_gains_in")
        with nc.Block() as block:
            @block.sync
            def _(sp):
                a = VEC_AT["q_norm_dil"][0]
                sp.dma_start(gains[:], k.d["vecs"][:, a:a + 2 * NG * HD]).then_inc(gains_in, 16)
                sp.wait_ge(gains_in, 16)
        dlo = k.cb("dlo_b").rearrange("p (g x) -> p g x", g=NG)
        dhi = k.cb("dhi_b").rearrange("p (g x) -> p g x", g=NG)
        slope = k.cb("slope_b").rearrange("p (h q) -> p h q", h=8)
        for g in range(NG):
            with ExitStack() as s1:
                nat = k.sb(s1, f"dil_nat{g}", [P, 3, TT, 512])
                qkT = k.sb(s1, f"dil_qkT{g}", [P, 8, SEQ])
                project(k, f"dil{g}", lambda tt, c: k.xT[:, c, tt * P:(tt + 1) * P], [512] * 3,
                        lambda i: d["w_dil"][:, :, (3 * i + g) * 512:(3 * i + g + 1) * 512],
                        copy_evac(lambda i, tt: nat[:, i, tt, :]))
                heads = [nat[:, i].rearrange("p t (h e) -> p t h e", h=8) for i in range(2)]
                head_norms(k, f"dilnorm{g}", [(heads[0], gains[:, g * HD:(g + 1) * HD], HD ** -0.5),
                                              (heads[1], gains[:, (NG + g) * HD:(NG + g + 1) * HD], 1.0)])
                transpose_tiles(k, f"dilT{g}", lambda tt, b: nat[:, b // 4, tt, (b % 4) * P:(b % 4 + 1) * P],
                                lambda b: qkT[:, b, :], 8)
                units = []
                for tt in range(TT):
                    lo = max(0, tt - 1) if g == 0 else 0
                    w = (tt + 1 - lo) * P
                    x0 = SEQ - w
                    for h in range(8):
                        r = slice(HD * (h % 2), HD * (h % 2) + HD)
                        masks = [(slope[:, h, :], dlo[:, g, x0:], 0, w)]
                        if x0 < 256:
                            masks.append((slope[:, h, :], dhi[:, g, x0:], 0, 256 - x0))
                        units.append(dict(q=qkT[r, h // 2, tt * P:(tt + 1) * P],
                                          keys=qkT[r, 4 + h // 2, lo * P:(tt + 1) * P], masks=masks,
                                          values=[nat[:, 2, b, h * HD:(h + 1) * HD] for b in range(lo, tt + 1)]))
                attention(k, f"dilatt{g}", units, lambda t: o_raw[:, g, t, :].rearrange("p (h d) -> p h d", h=8),
                          stats=(nmax[:, g, :], den[:, g, :]))
                k.recycle_semaphores()
        with ExitStack() as s1:
            diff, e, part = (k.sb(s1, f"merge_{n}", [P, NG, NU]) for n in ("diff", "e", "part"))
            least, total, inv = (k.sb(s1, f"merge_{n}", [P, NU]) for n in ("least", "total", "inv"))
            tmp = k.sb(s1, "merge_tmp", [P, 512])
            diff_ready, e_ready, step_d = k.sem("merge_diff"), k.sem("merge_e"), k.sem("merge_step")
            with nc.Block() as block:
                @block.scalar
                def _(act):
                    act.wait_ge(diff_ready, 1)
                    act.activation(e[:], diff[:], ACT.Exp).then_inc(e_ready, 1)

                @block.vector
                def _(dve):
                    step = Chain(dve, step_d)
                    step(dve.tensor_tensor(least[:], nmax[:, 0], nmax[:, 1], ALU.min))
                    step(dve.tensor_tensor(least[:], least[:], nmax[:, 2], ALU.min))
                    dve.tensor_tensor(diff[:], bc(least[:], 1, NG), nmax[:], ALU.subtract).then_inc(diff_ready, 1)
                    dve.wait_ge(e_ready, 1)
                    step(dve.tensor_tensor(part[:], e[:], den[:], ALU.mult))
                    step(dve.reduce_sum(total[:], part[:].rearrange("p g u -> p u g"), AX))
                    step(dve.reciprocal(inv[:], total[:]))
                    step(dve.tensor_tensor(e[:], e[:], bc(inv[:], 1, NG), ALU.mult))
                    for tt in range(TT):
                        o = k.o_dil[:, tt, :].rearrange("p (h d) -> p h d", h=8)
                        t3 = tmp[:].rearrange("p (h d) -> p h d", h=8)
                        for g in range(NG):
                            w = bc(e[:, g, tt * 8:tt * 8 + 8], 2, HD)
                            x = o_raw[:, g, tt, :].rearrange("p (h d) -> p h d", h=8)
                            step(dve.tensor_tensor(t3 if g else o, x, w, ALU.mult))
                            if g:
                                step(dve.tensor_tensor(o, o, t3, ALU.add))


def second_block(k):
    nc, d = k.nc, k.d
    k.recycle_semaphores()
    x = lambda tt: k.x1[:, tt, :]
    token_lhs = lambda tt, c: k.xT[:, c, tt * P:(tt + 1) * P]
    with ExitStack() as s:
        h_nat = k.sb(s, "h_nat", [P, TT, DM])
        rms_rows(k, "rms1", x, lambda tt: h_nat[:, tt, :], "norm_attn")
        transpose_tiles(k, "hT", lambda tt, b: h_nat[:, tt, b * P:(b + 1) * P], lambda b: k.xT[:, b, :], KD)
    with ExitStack() as s:
        latent_attention(k, s)
        k.recycle_semaphores()
        dilated_attention(k, s)
        k.recycle_semaphores()
        a = k.sb(s, "branches", [P, 2, TT, DM])
        with ExitStack() as s1:
            oT = k.sb(s1, "oT", [P, 8, SEQ])
            transpose_tiles(k, "oT", lambda tt, b: (k.o_mla if b < 4 else k.o_dil)[:, tt, (b % 4) * P:(b % 4 + 1) * P],
                            lambda b: oT[:, b, :], 8)
            for i, n in enumerate(("w_o_mla", "w_o_dil")):
                project(k, n, lambda tt, c: oT[:, 4 * i + c, tt * P:(tt + 1) * P], [512, 512],
                        lambda j: d[n][:, :, j * 512:(j + 1) * 512],
                        copy_evac(lambda j, tt: a[:, i, tt, j * 512:(j + 1) * 512]), kd=4)
        with ExitStack() as s1:
            pre = k.sb(s1, "gate_pre", [P, TT, 2 * DM])
            bg = k.sb(s1, "gate_bias", [P, 2 * DM])
            bg_in = k.sem("gate_bias_in")
            with nc.Block() as block:
                @block.sync
                def _(sp):
                    sp.dma_start(bg[:], k.vec("b_gate")).then_inc(bg_in, 16)
                    sp.wait_ge(bg_in, 16)

            def add_bias(dve, step, i, tt, bank):
                return dve.tensor_tensor(pre[:, tt, i * 512:(i + 1) * 512], bank[:], bg[:, i * 512:(i + 1) * 512], ALU.add)

            project(k, "gates", token_lhs, [512] * 4, lambda i: d["w_gates"][:, :, i * 512:(i + 1) * 512], add_bias)
            sig, step_d = k.sem("gate_sig"), k.sem("gate_step")
            with nc.Block() as block:
                @block.scalar
                def _(act):
                    for tt in range(TT):
                        act.activation(pre[:, tt, :], pre[:, tt, :], ACT.Sigmoid).then_inc(sig, 1)

                @block.vector
                def _(dve):
                    step = Chain(dve, step_d)
                    for tt in range(TT):
                        dve.wait_ge(sig, tt + 1)
                        for i in range(2):
                            step(dve.tensor_tensor(a[:, i, tt, :], a[:, i, tt, :], pre[:, tt, i * DM:(i + 1) * DM],
                                                   ALU.mult))
                        step(dve.tensor_tensor(a[:, 0, tt, :], a[:, 0, tt, :], a[:, 1, tt, :], ALU.add))
        transpose_tiles(k, "merT", lambda tt, b: a[:, 0, tt, b * P:(b + 1) * P], lambda b: k.xT[:, b, :], KD)

        def add_out(dve, step, i, tt, bank):
            o = k.x1[:, tt, i * 512:(i + 1) * 512]
            return dve.tensor_tensor(o, o, bank[:], ALU.add)

        project(k, "out2", token_lhs, [512] * 2, lambda i: d["w_out2"][:, :, i * 512:(i + 1) * 512], add_out)
    k.recycle_semaphores()
    with ExitStack() as s:
        h2 = k.sb(s, "h2_nat", [P, TT, DM])
        rms_rows(k, "rms2", x, lambda tt: h2[:, tt, :], "norm_ffn")
        transpose_tiles(k, "h2T", lambda tt, b: h2[:, tt, b * P:(b + 1) * P], lambda b: k.xT[:, b, :], KD)
        route(k, "r2", E2, G2, "b2", d["w_route2"], s)
        experts(k, "e2", E2, d["rows"], d["gu2"], d["dn2"], d["slots"], lambda tt: h2[:, tt, :])
        combine(k, "c2", d["slots"], k.x1, 1.0, out=d["out"])


def first_block(k):
    nc, d = k.nc, k.d
    with ExitStack() as s:
        load_block1(k, s)
        project1(k, s)
        select_keys(k, s)
        state_space(k, s)
        att = k.sb(s, "att1", [P, TT, 512])
        units = []
        for tt in range(TT):
            w = (tt + 1) * P
            for h in range(H1):
                r = slice(HD * (h % 2), HD * (h % 2) + HD)
                units.append(dict(q=k.ropeT[r, h // 2, tt * P:w], keys=k.ropeT[r, 4, 0:w],
                                  masks=[(k.cb("ident_b"), k.key_bias[:, tt, 0:w], 0, w)],
                                  values=[k.v[:, b, 0:HD] for b in range(tt + 1)]))
        attention(k, "dsa", units, lambda g: att[:, g, :].rearrange("p (h d) -> p h d", h=8))
        cat = lambda tt, b: att[:, tt, b * P:(b + 1) * P] if b < 4 else k.y[:, tt, (b - 4) * P:(b - 3) * P]
        transpose_tiles(k, "mix1", cat, lambda b: k.xT[:, b, :], KD)

        def add_mixed(dve, step, i, tt, bank):
            x = k.x1[:, tt, i * 512:(i + 1) * 512]
            return dve.scalar_tensor_tensor(x, x, ALPHA, bank[:], ALU.mult, ALU.add)

        project(k, "out1", lambda tt, c: k.xT[:, c, tt * P:(tt + 1) * P], [512, 512],
                lambda i: d["w_out"][:, :, i * 512:(i + 1) * 512], add_mixed)
    layer_norm(k, "ln1", k.x1, "ln1_g", "ln1_b")
    k.recycle_semaphores()
    transpose_tiles(k, "x1T", lambda tt, b: k.x1[:, tt, b * P:(b + 1) * P], lambda b: k.xT[:, b, :], KD)
    with ExitStack() as s:
        route(k, "r1", E1, G1, "b1", d["w_route1"], s)
        experts(k, "e1", E1, d["rows"], d["gu1"], d["dn1"], d["slots"][0:NT1 * P, :], lambda tt: k.x1[:, tt, :])
        combine(k, "c1", d["slots"][0:NT1 * P, :], k.x1, ALPHA)
    layer_norm(k, "ln2", k.x1, "ln2_g", "ln2_b")


def program(nc, d):
    with ExitStack() as ctx:
        k = Core(nc, ctx, d)
        first_block(k)
        second_block(k)


def lay_out(a):
    f = np.float32
    A = {n: np.asarray(v) for n, v in a.items()}
    L = {n: (v[0] if v.ndim > 1 or n in () else v) for n, v in A.items() if n not in ("x", "positions_2")}
    o = {}
    x = A["x"][0]
    o["x_nat"] = x.reshape(TT, P, DM).transpose(1, 0, 2)
    o["xT"] = x.T.reshape(KD, P, SEQ).transpose(1, 0, 2)
    w = L["w_in"]
    rows = lambda m: m.reshape(-1, P, m.shape[1]).transpose(1, 0, 2)
    q, kk, vv, iq, ik, iw, z, xbc, dt = np.split(w, np.cumsum([512, 64, 64, 256, 64, 4, 512, 768]), axis=1)
    cols = np.concatenate([q, kk, kk, iq, ik, ik, xbc], axis=1)
    o["w_in_t"] = cols.reshape(KD, P, -1, P).transpose(2, 1, 0, 3).reshape(-1, P, KD * P)
    o["w_in_n"] = rows(np.concatenate([z, vv, iw, dt], axis=1))
    cw = np.concatenate([L["conv_w"], L["conv_b"][None]], 0)
    o["convw"] = cw.reshape(5, 6, P).transpose(2, 1, 0)
    o["w_out"] = rows(L["w_out"])
    o["w_route1"] = rows(np.concatenate([L["w_route_group"], L["w_route_expert"]], 1))

    def expert(wg, wu, wd):
        E = wg.shape[0]
        gu = np.concatenate([wg, wu], 2).reshape(E, KD, P, 2 * FF).transpose(0, 2, 1, 3).reshape(E, P, -1)
        return gu, wd.reshape(E, 2, P, DM).transpose(0, 2, 1, 3).reshape(E, P, -1)

    o["gu1"], o["dn1"] = expert(L["w_gate"], L["w_up"], L["w_down"])
    o["gu2"], o["dn2"] = expert(L["w_gate_2"], L["w_up_2"], L["w_down_2"])
    v = {"b1": np.concatenate([L["b_route_group"], L["b_route_expert"]]),
         "b2": np.concatenate([L["b_router_group_2"], L["b_router_expert_2"]])}
    for n, width in VECS:
        if n not in v:
            v[n] = L[n] if n in L else L[n + "_2"]
    flat = np.concatenate([np.asarray(v[n]).reshape(-1) for n, _ in VECS])
    o["vecs"] = np.broadcast_to(flat[None], (P, NVEC))
    w2 = L["w_in_2"]
    o["w_mla"] = rows(w2[:, 0:MLA_COLS])
    o["w_dil"] = rows(w2[:, MLA_COLS:MLA_COLS + 9 * 512])
    o["w_gates"] = rows(w2[:, MLA_COLS + 9 * 512:])
    o["w_ukv"] = rows(L["w_ukv_2"])
    o["w_o_mla"], o["w_o_dil"], o["w_out2"] = rows(L["w_o_mla_2"]), rows(L["w_o_dil_2"]), rows(L["w_out_2"])
    o["w_route2"] = rows(np.concatenate([L["w_router_group_2"], L["w_router_expert_2"]], 1))
    o["positions"] = A["positions_2"][0].reshape(TT, P).T.astype(np.int32)
    o["consts"], o["consts_b"] = constants()
    return {n: np.ascontiguousarray(m) for n, m in o.items()}


def kernel(**inputs):
    import concourse.bacc as bacc
    from concourse.bass_utils import run_bass_kernel_spmd
    nc = bacc.Bacc("TRN2", target_bir_lowering=False, num_devices=1)
    arrays = {f"in_{n}": m for n, m in lay_out(inputs).items()}
    d = {n[3:]: nc.dram_tensor(n, m.shape, mybir.dt.from_np(m.dtype), kind="ExternalInput").ap()
         for n, m in arrays.items()}
    d["consts_b"] = d["consts_b"].bitcast(BF16)
    d["rows"] = nc.dram_tensor("token_rows", (SEQ, DM), F32, kind="Internal").ap()
    d["slots"] = nc.dram_tensor("slot_rows", (NT2 * P, DM), F32, kind="Internal").ap()
    d["out"] = nc.dram_tensor("out", (SEQ, DM), F32, kind="ExternalOutput").ap()
    program(nc, d)
    r = run_bass_kernel_spmd(nc, [arrays], core_ids=[0])
    return r.results[0]["out"].reshape(1, SEQ, DM)
```

```python
from contextlib import ExitStack

import numpy as np
import concourse.bass as bass
from concourse import mybir

F32 = mybir.dt.float32
BF16 = mybir.dt.bfloat16
F32R = mybir.dt.float32r
I32 = mybir.dt.int32
U32 = mybir.dt.uint32
ALU = mybir.AluOpType
ACT = mybir.ActivationFunctionType
AX = mybir.AxisListType.X

P = 128
SEQ = 512
TT = SEQ // P
DM = 1024
KD = DM // P
HD = 64
NEG = -1.0e30
H1 = 8
IDX_HEADS = 4
INDEXER_SCALE = (IDX_HEADS ** -0.5) * (HD ** -0.5)
TOPK = min(256, SEQ // 4)
SSD_HEADS = 8
CONV_W = 4
ALPHA = 2.0 ** 0.25
LN_EPS = 1e-5
NAT1 = 512 + 64 + 4 + 8
EPS = 1e-6
MLA_D = 96
MLA_COLS = 8 * MLA_D + 256 + 32
DIL = ((128, 1), (512, 4), (2048, 16))
FF = 256
E1, G1 = 16, 4
E2, G2 = 32, 4


S1, S2 = 96, 64


def most_tiles(experts, slots):
    return (2 * SEQ + (slots - 1) * experts) // slots


SLOTS1, SLOTS2 = S1 * most_tiles(E1, S1), S2 * most_tiles(E2, S2)

VECS = [("dt_bias", 8), ("a_log", 8), ("d_skip", 8), ("ssd_norm_w", 512), ("ln1_g", DM), ("ln1_b", DM),
        ("b1", G1 + E1), ("ln2_g", DM), ("ln2_b", DM), ("norm_attn", DM), ("norm_ckv", 256),
        ("q_norm_mla", 96), ("k_norm_mla", 96), ("q_norm_dil", 192), ("k_norm_dil", 192),
        ("b_gate", 2 * DM), ("norm_ffn", DM), ("b2", G2 + E2)]
VEC_AT = {}
_at = 0
for _n, _w in VECS:
    VEC_AT[_n] = (_at, _w)
    _at += _w
NVEC = _at

CONSTS = [("ident", 128), ("upto", 128), ("after", 128), ("before", 128), ("ones", 128), ("rot", 128),
          ("cos", SEQ), ("sin", SEQ), ("iota", 128), ("down", 128), ("tok", TT), ("freq", 16)]
CONST_AT = {}
_at = 0
for _n, _w in CONSTS:
    CONST_AT[_n] = (_at, _w)
    _at += _w
NCONST = _at
CONSTS_B = [("ident_b", 128), ("causal_b", 128), ("slope_b", 8 * 128), ("slope4_b", 8 * 128),
            ("delta_b", 256), ("dfold_b", 2 * 128)]
CONST_B_AT = {}
_at = 0
for _n, _w in CONSTS_B:
    CONST_B_AT[_n] = (_at, _w)
    _at += _w
NCONST_B = _at


def constants():
    k = np.arange(P)
    c = {}
    c["ident"] = np.eye(P)
    c["upto"] = k[:, None] <= k[None, :]
    c["after"] = k[:, None] > k[None, :]
    c["before"] = k[:, None] < k[None, :]
    c["ones"] = np.ones((P, P))
    rot = np.zeros((P, P))
    for m in range(P):
        if m % HD < HD // 2:
            rot[m + HD // 2, m] = -1
        else:
            rot[m - HD // 2, m] = 1
    c["rot"] = rot
    inv = (np.float32(10000.0) ** (-np.arange(0, HD, 2, dtype=np.float32) / np.float32(HD))).astype(np.float32)
    ang = np.arange(SEQ, dtype=np.float32)[:, None] * inv[None, :]
    c["cos"] = np.tile(np.cos(ang).T, (4, 1))
    c["sin"] = np.tile(np.sin(ang).T, (4, 1))
    c["iota"] = np.broadcast_to(k[None, :], (P, P))
    c["down"] = np.broadcast_to(P - k[None, :], (P, P))
    c["tok"] = k[:, None] + P * np.arange(TT)[None, :]
    c["freq"] = np.broadcast_to(
        (np.float32(10000.0) ** (-np.arange(16, dtype=np.float32) / np.float32(16))).astype(np.float32)[None], (P, 16))
    f = np.concatenate([np.asarray(c[n], np.float32).reshape(P, w) for n, w in CONSTS], 1)
    b = {}
    b["ident_b"] = np.eye(P)
    b["causal_b"] = np.where(k[None, :] <= k[:, None], 0.0, NEG)
    b["slope_b"] = np.stack([np.eye(P) * 2.0 ** -(h + 1) for h in range(8)], 1)
    b["slope4_b"] = 4 * b["slope_b"]
    delta = k[:, None] + P - np.arange(2 * P)[None, :]
    b["delta_b"] = np.where((delta >= 0) & (delta <= DIL[0][0]), -delta, NEG)
    own = k[:, None] - k[None, :]
    b["dfold_b"] = np.stack([np.where((own >= 0) & (own % (dil // 4) == 0), -own, NEG) for _, dil in DIL[1:]], 1)
    fb = np.concatenate([np.asarray(b[n], np.float32).reshape(P, w) for n, w in CONSTS_B], 1)
    return np.ascontiguousarray(f), (fb.view(np.uint32) >> 16).astype(np.uint16)


class Chain:

    def __init__(self, eng, sem, start=0):
        self.eng, self.sem, self.n = eng, sem, start

    def __call__(self, ins):
        ins.then_inc(self.sem, 1)
        self.n = self.n + 1
        self.eng.wait_ge(self.sem, self.n)


class Core:

    def __init__(self, nc, ctx, d):
        self.nc, self.ctx, self.d = nc, ctx, d
        self.uid = 0
        self.held = ExitStack()
        self.held_sems = []
        self.gathered = [0] * 8
        self.w_in = [ctx.enter_context(nc.semaphore(f"weights_in{i}")) for i in range(2)]
        self.chunks_loaded = 0
        self.gather_sems = [ctx.enter_context(nc.semaphore(f"gathered{i}")) for i in range(8)]

    def sem(self, name):
        self.uid += 1
        sem = self.held.enter_context(self.nc.semaphore(f"{name}_{self.uid}"))
        self.held_sems.append(sem)
        return sem

    def recycle_semaphores(self):
        sems = self.held_sems
        with self.nc.Block() as block:
            @block.gpsimd
            def _(pool):
                for sem in sems:
                    pool.sem_clear(sem)
        self.held.close()
        self.held, self.held_sems = ExitStack(), []

    def sb(self, ctx, name, shape, dt=F32):
        return ctx.enter_context(self.nc.sbuf_tensor(name, shape, dt))

    def ps(self, ctx, name, shape=(P, 512), dt=F32):
        return ctx.enter_context(self.nc.psum_tensor(name, list(shape), dt))

    def weight_buffers(self, ctx, name):
        self.w = self.sb(ctx, f"{name}_w", [P, 2, KD, 512])
        self.w_ring = [self.sb(ctx, f"{name}_w_{x}", [P, 4, 512], F32R) for x in ("hi", "lo")]

    def load_chunk(self, sp, chunk):
        slot = self.chunks_loaded % 2
        kd, width = chunk.shape[1:]
        sp.dma_start(self.w[:, slot, 0:kd, 0:width], chunk).then_inc(self.w_in[slot], 16)
        self.chunks_loaded += 1

    def xs_lhs(self, tt, c):
        return tuple(x[:, c, tt * P:(tt + 1) * P] for x in (self.xh, self.xl))

    def c(self, name):
        a, w = CONST_AT[name]
        return self.consts[:, a:a + w]

    def cb(self, name):
        a, w = CONST_B_AT[name]
        return self.consts_b[:, a:a + w]

    def vec(self, name):
        a, w = VEC_AT[name]
        return self.d["vecs"][:, a:a + w]


def bc(ap, axis, n):
    shape = list(ap.shape)
    shape.insert(axis, n)
    return ap.unsqueeze(axis).broadcast_to(shape)


def three_passes(pe, out, lhs, rhs, first, last):
    pe.matmul(out, lhs[0], rhs[0], start=first, stop=False)
    pe.matmul(out, lhs[0], rhs[1], start=False, stop=False)
    return pe.matmul(out, lhs[1], rhs[0], start=False, stop=last)


def transpose_split(k, name, src, dst, blocks):
    nc = k.nc
    with ExitStack() as s:
        bank = [k.ps(s, f"{name}_bank{i}") for i in range(4)]
        turned, hi_ready, lo_ready = (k.sem(f"{name}_{n}") for n in ("turned", "hi", "lo"))
        with nc.Block() as block:
            @block.tensor
            def _(pe):
                for b in range(blocks):
                    if b >= 4:
                        pe.wait_ge(lo_ready, b - 3)
                    for tt in range(TT):
                        a = src(tt, b)
                        ins = pe.transpose(bank[b % 4][0:a.shape[1], tt * P:(tt + 1) * P], a, k.c("ident"))
                    ins.then_inc(turned, 1)

            @block.scalar
            def _(act):
                for b in range(blocks):
                    act.wait_ge(turned, b + 1)
                    hi, lo = dst(b)
                    act.activation(hi, bank[b % 4][0:hi.shape[0], :], ACT.Copy).then_inc(hi_ready, 1)

            @block.vector
            def _(dve):
                for b in range(blocks):
                    hi, lo = dst(b)
                    dve.wait_ge(hi_ready, b + 1)
                    dve.tensor_tensor(lo, bank[b % 4][0:hi.shape[0], :], hi.bitcast(F32),
                                      ALU.subtract).then_inc(lo_ready, 1)


def transpose_tiles(k, name, src, dst, blocks):
    nc = k.nc
    with ExitStack() as s:
        bank = k.ps(s, f"{name}_bank", (P, 4, 512))
        turned = k.sem(f"{name}_turned")
        copied = [k.sem(f"{name}_copied_{e}") for e in ("vector", "scalar")]
        with nc.Block() as block:
            @block.tensor
            def _(pe):
                for b in range(blocks):
                    if b >= 4:
                        pe.wait_ge(copied[b % 2], (b - 4) // 2 + 1)
                    for tt in range(TT):
                        a = src(tt, b)
                        ins = pe.transpose(bank[0:a.shape[1], b % 4, tt * P:(tt + 1) * P], a, k.c("ident"))
                    ins.then_inc(turned, 1)

            @block.vector
            def _(dve):
                for b in range(0, blocks, 2):
                    dve.wait_ge(turned, b + 1)
                    w = dst(b).shape[0]
                    dve.tensor_copy(dst(b), bank[0:w, b % 4, :]).then_inc(copied[0], 1)

            @block.scalar
            def _(act):
                for b in range(1, blocks, 2):
                    act.wait_ge(turned, b + 1)
                    w = dst(b).shape[0]
                    act.activation(dst(b), bank[0:w, b % 4, :], ACT.Copy).then_inc(copied[1], 1)


def columns(w, width, count=None):
    n = w.shape[2]
    return [w[:, :, i:min(i + width, n)] for i in range(0, n, width)][:count]


CONV_BLOCKS = 6
ROPE_BLOCKS = 8


def load_block1(k, ctx):
    nc, d = k.nc, k.d
    k.consts = k.sb(k.ctx, "consts", [P, NCONST])
    k.consts_b = k.sb(k.ctx, "consts_b", [P, NCONST_B], BF16)
    k.x1 = k.sb(k.ctx, "x_res", [P, TT, DM])
    k.xh, k.xl = (k.sb(k.ctx, n, [P, KD, SEQ], F32R) for n in ("xT_hi", "xT_lo"))
    k.v = k.sb(ctx, "v1", [P, TT, 76])
    k.ropeT = k.sb(ctx, "ropeT", [P, ROPE_BLOCKS, SEQ])
    k.sz = k.sb(ctx, "z", [P, TT, 512])
    k.xbcT = k.sb(ctx, "xbcT", [P, CONV_BLOCKS, SEQ])
    k.convw = k.sb(ctx, "convw", [P, CONV_BLOCKS, CONV_W + 1])


def project1(k, ctx):
    nc, d = k.nc, k.d
    NB = ROPE_BLOCKS + CONV_BLOCKS
    with ExitStack() as s:
        xT = k.sb(s, "xT", [P, KD, SEQ])
        w_t = k.sb(s, "w_t", [P, 2, KD * P])
        w_h, w_l = (k.sb(s, n, [P, 2, KD * P], F32R) for n in ("w_t_hi", "w_t_lo"))
        raw = k.sb(s, "raw", [P, 2, SEQ])
        padded = k.sb(s, "padded", [P, 2, SEQ + CONV_W - 1])
        part = k.sb(s, "part", [P, 2, SEQ])
        acc = k.sb(s, "conv_acc", [P, 2, SEQ])
        main = [k.ps(s, f"proj_main{i}") for i in range(4)]
        turned = [k.ps(s, f"proj_rot{i}") for i in range(2)]
        consts_in, small_in = k.sem("consts_in"), k.sem("small_in")
        x_in = [k.sem(f"x_in{i}") for i in range(4)]
        wt_in = [k.sem(f"wt_in{i}") for i in range(2)]
        xh_ready, xl_ready, wh_ready, wl_ready = k.sem("xh"), k.sem("xl"), k.sem("wh"), k.sem("wl")
        proj_done, main_free = k.sem("proj_done"), k.sem("main_free")
        raw_ready, rot_done, roped = k.sem("raw_ready"), k.sem("rot_done"), k.sem("roped")
        pad_zero, conv_done, conv_silu, dve_step = (k.sem("pad_zero"), k.sem("conv_done"), k.sem("conv_silu"),
                                                    k.sem("dve_step"))
        k.vecs_in = k.sem("x_nat_in")

        with nc.Block() as block:
            @block.sync
            def _(sp):
                sp.dma_start(w_t[:, 0], d["w_in_t"][0]).then_inc(wt_in[0], 16)
                for c in range(4):
                    sp.dma_start(xT[:, 2 * c:2 * c + 2], d["xT"][:, 2 * c:2 * c + 2]).then_inc(x_in[c], 16)
                sp.dma_start(w_t[:, 1], d["w_in_t"][1]).then_inc(wt_in[1], 16)
                sp.dma_start(k.consts[:], d["consts"]).then_inc(consts_in, 16)
                sp.dma_start(k.convw[:], d["convw"]).then_inc(small_in, 16)
                sp.dma_start(k.consts_b[:], d["consts_b"]).then_inc(small_in, 16)
                for b in range(2, NB):
                    sp.wait_ge(wl_ready, b - 1)
                    sp.dma_start(w_t[:, b % 2], d["w_in_t"][b]).then_inc(wt_in[b % 2], 16)
                for chunk in columns(d["w_in_n"], 512):
                    k.load_chunk(sp, chunk)
                sp.dma_start(k.x1[:], d["x_nat"]).then_inc(k.vecs_in, 16)
                sp.wait_ge(k.vecs_in, 16)
                sp.wait_ge(small_in, 32)

            @block.tensor
            def _(pe):
                for b in range(NB + 1):
                    if b < NB:
                        pe.wait_ge(wl_ready, b + 1)
                        if b >= 4:
                            pe.wait_ge(main_free, b - 3)
                        for c in range(KD):
                            if b == 0:
                                pe.wait_ge(xl_ready, c + 1)
                            f = slice(c * P, (c + 1) * P)
                            ins = three_passes(pe, main[b % 4][:], (w_h[:, b % 2, f], w_l[:, b % 2, f]),
                                               (k.xh[:, c, :], k.xl[:, c, :]), c == 0, c == KD - 1)
                        ins.then_inc(proj_done, 1)
                    r = b - 1
                    if 0 <= r < ROPE_BLOCKS:
                        if r == 0:
                            pe.wait_ge(consts_in, 16)
                        pe.wait_ge(raw_ready, r + 1)
                        if r >= 2:
                            pe.wait_ge(roped, r - 1)
                        pe.matmul(turned[r % 2][:], k.c("rot"), raw[:, r % 2, :], start=True,
                                  stop=True).then_inc(rot_done, 1)

            @block.gpsimd
            def _(pool):
                def split_w(b):
                    pool.wait_ge(wh_ready, b + 1)
                    pool.tensor_tensor(w_l[:, b % 2], w_t[:, b % 2], w_h[:, b % 2].bitcast(F32),
                                       ALU.subtract).then_inc(wl_ready, 1)

                split_w(0)
                for c in range(KD):
                    pool.wait_ge(xh_ready, c + 1)
                    pool.tensor_tensor(k.xl[:, c], xT[:, c], k.xh[:, c].bitcast(F32), ALU.subtract).then_inc(xl_ready, 1)
                for b in range(1, NB):
                    split_w(b)

            @block.scalar
            def _(act):
                def split_w(b):
                    act.wait_ge(wt_in[b % 2], 16 * (b // 2 + 1))
                    if b >= 2:
                        act.wait_ge(proj_done, b - 1)
                    act.activation(w_h[:, b % 2], w_t[:, b % 2], ACT.Copy).then_inc(wh_ready, 1)

                def silu_conv(r):
                    act.wait_ge(conv_done, r + 1)
                    act.activation(k.xbcT[:, r, :], acc[:, r % 2, :], ACT.Silu,
                                   bias=k.convw[:, r, CONV_W:CONV_W + 1]).then_inc(conv_silu, 1)

                split_w(0)
                for c in range(KD):
                    act.wait_ge(x_in[c // 2], 16)
                    act.activation(k.xh[:, c], xT[:, c], ACT.Copy).then_inc(xh_ready, 1)
                split_w(1)
                act.wait_ge(pad_zero, 1)
                for b in range(NB):
                    act.wait_ge(proj_done, b + 1)
                    if b + 2 < NB:
                        split_w(b + 2)
                    if b < ROPE_BLOCKS:
                        if b >= 2:
                            act.wait_ge(roped, b - 1)
                        act.activation(raw[:, b % 2, :], main[b % 4][:], ACT.Copy,
                                       scale=(HD ** -0.5 if b < 4 else 1.0)).then_inc(raw_ready, 1)
                        act.wait_ge(raw_ready, b + 1)
                        act.sem_inc(main_free, 1)
                    elif b < NB:
                        r = b - ROPE_BLOCKS
                        if r >= 2:
                            act.wait_ge(conv_done, r - 1)
                        act.activation(padded[:, r % 2, CONV_W - 1:], main[b % 4][:],
                                       ACT.Copy).then_inc(main_free, 1)
                        if r >= 1:
                            silu_conv(r - 1)
                silu_conv(CONV_BLOCKS - 1)

            @block.vector
            def _(dve):
                step = Chain(dve, dve_step)
                dve.memset(padded[:, :, 0:CONV_W - 1], 0.0).then_inc(pad_zero, 1)
                dve.wait_ge(consts_in, 16)
                for r in range(ROPE_BLOCKS):
                    dve.wait_ge(raw_ready, r + 1)
                    dve.tensor_tensor(part[:, 0, :], raw[:, r % 2, :], k.c("cos"), ALU.mult).then_inc(dve_step, 1)
                    dve.wait_ge(rot_done, r + 1)
                    dve.tensor_tensor(part[:, 1, :], turned[r % 2][:], k.c("sin"), ALU.mult).then_inc(dve_step, 1)
                    step.n += 2
                    dve.wait_ge(dve_step, step.n)
                    dve.tensor_tensor(k.ropeT[:, r, :], part[:, 0, :], part[:, 1, :], ALU.add).then_inc(roped, 1)
                    dve.wait_ge(roped, r + 1)
                dve.wait_ge(small_in, 32)
                for r in range(CONV_BLOCKS):
                    dve.wait_ge(main_free, ROPE_BLOCKS + r + 1)
                    if r >= 2:
                        dve.wait_ge(conv_silu, r - 1)
                    a, u = acc[:, r % 2, :], padded[:, r % 2, :]
                    step(dve.tensor_scalar(a, u[:, 0:SEQ], k.convw[:, r, 0:1], None, ALU.mult))
                    for j in range(1, CONV_W):
                        ins = dve.scalar_tensor_tensor(a, u[:, j:j + SEQ], k.convw[:, r, j:j + 1], a,
                                                       ALU.mult, ALU.add)
                        if j < CONV_W - 1:
                            step(ins)
                    ins.then_inc(conv_done, 1)
    project(k, "nat1", k.xs_lhs, columns(d["w_in_n"], 512), copy_evac(lambda i, tt: (k.sz, k.v)[i][:, tt, :]),
            ahead=2, then=columns(d["w_out"], 512))


def select_keys(k, ctx):
    nc = k.nc
    TAKEN, FLOOR = -3.0e38, -1.0e35
    k.key_bias = k.sb(ctx, "key_bias", [P, TT, SEQ], BF16)
    tiles = [tt for tt in range(TT) if (tt + 1) * P > TOPK]
    with ExitStack() as s:
        relu = k.sb(s, "relu", [P, 2, SEQ])
        score = k.sb(s, "score", [P, TT, SEQ])
        iw = k.sb(s, "iw", [P, TT, IDX_HEADS])
        best = k.sb(s, "best", [P, 8])
        bank = [k.ps(s, f"idx_bank{i}") for i in range(2)]
        dots, relued, used, scored, dve_step, iw_ready = (
            k.sem("idx_dots"), k.sem("idx_relued"), k.sem("idx_used"), k.sem("idx_scored"), k.sem("idx_step"),
            k.sem("iw_ready"))
        units = [(tt, h) for tt in tiles for h in range(IDX_HEADS)]
        with nc.Block() as block:
            @block.tensor
            def _(pe):
                for u, (tt, h) in enumerate(units):
                    if u >= 2:
                        pe.wait_ge(relued, u - 1)
                    lo = HD * (h % 2)
                    pe.matmul(bank[u % 2][:, 0:(tt + 1) * P],
                              k.ropeT[lo:lo + HD, 5 + h // 2, tt * P:(tt + 1) * P],
                              k.ropeT[lo:lo + HD, 7, 0:(tt + 1) * P], start=True, stop=True).then_inc(dots, 1)

            @block.scalar
            def _(act):
                for u, (tt, h) in enumerate(units):
                    act.wait_ge(dots, u + 1)
                    if u >= 2:
                        act.wait_ge(used, u - 1)
                    w = (tt + 1) * P
                    act.activation(relu[:, u % 2, 0:w], bank[u % 2][:, 0:w], ACT.Relu).then_inc(relued, 1)

            @block.vector
            def _(dve):
                step = Chain(dve, dve_step)
                step(dve.tensor_scalar(iw[:], k.v[:, :, 64:64 + IDX_HEADS], INDEXER_SCALE, None, ALU.mult))
                for tt in range(TT):
                    if tt not in tiles:
                        if tt:
                            step(dve.memset(k.key_bias[:, tt, 0:tt * P], 0.0))
                        step(dve.tensor_copy(k.key_bias[:, tt, tt * P:(tt + 1) * P], k.cb("causal_b")))
                for u, (tt, h) in enumerate(units):
                    w = (tt + 1) * P
                    dve.wait_ge(relued, u + 1)
                    sc, r = score[:, tt, 0:w], relu[:, u % 2, 0:w]
                    if h == 0:
                        ins = dve.tensor_scalar(sc, r, iw[:, tt, h:h + 1], None, ALU.mult)
                    else:
                        ins = dve.scalar_tensor_tensor(sc, r, iw[:, tt, h:h + 1], sc, ALU.mult, ALU.add)
                    ins.then_inc(used, 1)
                    dve.wait_ge(used, u + 1)
                    if h == IDX_HEADS - 1:
                        diag = score[:, tt, tt * P:w]
                        step(dve.tensor_tensor(diag, diag, k.cb("causal_b"), ALU.add))
                        for _ in range(TOPK // 8):
                            step(dve.max(best[:], sc))
                            step(dve.match_replace(sc, best[:], sc, TAKEN))
                        step(dve.tensor_scalar(k.key_bias[:, tt, 0:w], sc, FLOOR, NEG, ALU.is_gt, ALU.mult))


def attention(k, name, units, out, group=8, stats=None, sync=None):
    nc = k.nc
    n = len(units)
    with ExitStack() as s:
        probs = k.sb(s, f"{name}_probs", [P, 2, SEQ])
        pT = k.sb(s, f"{name}_pT", [P, 2, SEQ])
        own = stats is None
        if own:
            nmax_t, den_t = k.sb(s, f"{name}_nmax", [P, n]), k.sb(s, f"{name}_den", [P, n])
            nmax, den = (lambda j, t=t: t[:, j:j + 1] for t in (nmax_t, den_t))
        else:
            nmax, den = stats
        rden = k.sb(s, f"{name}_rden", [P, n])
        sbank = [k.ps(s, f"{name}_scores{i}") for i in range(2)]
        tbank = [k.ps(s, f"{name}_pT{i}") for i in range(2)]
        obank = [k.ps(s, f"{name}_out{i}") for i in range(2)]
        scores, maxed, probs_ready, turned, pT_ready, summed, out_free, rden_ready = (
            k.sem(f"{name}_{x}") for x in ("scores", "maxed", "probs", "turned", "pT", "summed", "outfree", "rden"))
        with nc.Block() as block:
            if sync is not None:
                @block.sync
                def _(sp):
                    sync(sp, out_free)

            @block.tensor
            def _(pe):
                for st in range(n + 2):
                    if st < n:
                        u = units[st]
                        if st >= 2:
                            pe.wait_ge(probs_ready, st - 1)
                        w = u["keys"].shape[-1]
                        ms = u["masks"]
                        ins = pe.matmul(sbank[st % 2][:, 0:w], u["q"], u["keys"], start=True, stop=True)
                        for m, (lhs, rhs, lo, hi) in enumerate(ms):
                            ins = pe.matmul(sbank[st % 2][:, lo:hi], lhs, rhs, start=False, stop=True,
                                            skip_group_check=True)
                        ins.then_inc(scores, 1)
                    if 1 <= st <= n:
                        j = st - 1
                        pe.wait_ge(probs_ready, j + 1)
                        if j >= 2:
                            pe.wait_ge(pT_ready, j - 1)
                        for b in range(len(units[j]["values"])):
                            ins = pe.transpose(tbank[j % 2][:, b * P:(b + 1) * P],
                                               probs[:, j % 2, b * P:(b + 1) * P], k.c("ident"))
                        ins.then_inc(turned, 1)
                    if st >= 2:
                        j = st - 2
                        g, h = divmod(j, group)
                        pe.wait_ge(pT_ready, j + 1)
                        if h == 0 and g >= 2:
                            pe.wait_ge(out_free, g - 1)
                        vs = units[j]["values"]
                        for b, v in enumerate(vs):
                            ins = pe.matmul(obank[g % 2][:, h * HD:(h + 1) * HD], pT[:, j % 2, b * P:(b + 1) * P],
                                            v, start=(b == 0), stop=(b == len(vs) - 1))
                        ins.then_inc(summed, 1)

            @block.scalar
            def _(act):
                for j, u in enumerate(units):
                    w = u["keys"].shape[-1]
                    act.wait_ge(maxed, j + 1)
                    if j >= 2:
                        act.wait_ge(turned, j - 1)
                    act.activation(probs[:, j % 2, 0:w], sbank[j % 2][:, 0:w], ACT.Exp, bias=nmax(j),
                                   accum_out=den(j)).then_inc(probs_ready, 1)

            @block.vector
            def _(dve):
                for st in range(n + 3):
                    if st < n:
                        w = units[st]["keys"].shape[-1]
                        dve.wait_ge(scores, st + 1)
                        dve.reduce_max(nmax(st), sbank[st % 2][:, 0:w], AX, negate=True).then_inc(maxed, 1)
                    if 1 <= st <= n:
                        j = st - 1
                        w = len(units[j]["values"]) * P
                        dve.wait_ge(turned, j + 1)
                        if j >= 2:
                            dve.wait_ge(summed, j - 1)
                        dve.tensor_copy(pT[:, j % 2, 0:w], tbank[j % 2][:, 0:w]).then_inc(pT_ready, 1)
                    if st >= 3 and (st - 2) % group == 0:
                        g = (st - 2) // group - 1
                        a, b = g * group, (g + 1) * group
                        dve.wait_ge(summed, b)
                        o = obank[g % 2][:].rearrange("p (h d) -> p h d", h=group)
                        if own:
                            dve.reciprocal(rden[:, a:b], den_t[:, a:b]).then_inc(rden_ready, 1)
                            dve.wait_ge(rden_ready, g + 1)
                            dve.tensor_tensor(out(g), o, bc(rden[:, a:b], 2, HD), ALU.mult).then_inc(out_free, 1)
                        else:
                            dve.tensor_copy(out(g), o).then_inc(out_free, 1)


def state_space(k, ctx):
    nc, d = k.nc, k.d
    k.y = k.sb(ctx, "ssd_y", [P, TT, 512])
    HW = 4 * HD
    xs = k.sb(ctx, "xs_nat", [P, TT, 5 * P])
    with ExitStack() as s:
        bank = k.ps(s, "xs_bank", (P, 4, 512))
        turned, copied = k.sem("xs_turned"), [k.sem("xs_copied_v"), k.sem("xs_copied_s")]
        with nc.Block() as block:
            @block.tensor
            def _(pe):
                for tt in range(TT):
                    q = 2 * (tt % 2)
                    if tt >= 2:
                        pe.wait_ge(copied[0], tt - 1)
                        pe.wait_ge(copied[1], tt - 1)
                    for b in range(5):
                        ins = pe.transpose(bank[:, q + b // 4, (b % 4) * P:(b % 4 + 1) * P],
                                           k.xbcT[:, b, tt * P:(tt + 1) * P], k.c("ident"))
                    ins.then_inc(turned, 1)

            @block.vector
            def _(dve):
                for tt in range(TT):
                    dve.wait_ge(turned, tt + 1)
                    dve.tensor_copy(xs[:, tt, 0:512], bank[:, 2 * (tt % 2), :]).then_inc(copied[0], 1)

            @block.scalar
            def _(act):
                for tt in range(TT):
                    act.wait_ge(turned, tt + 1)
                    act.activation(xs[:, tt, 512:640], bank[:, 2 * (tt % 2) + 1, 0:P],
                                   ACT.Copy).then_inc(copied[1], 1)
    with ExitStack() as s2:
        k_vec = k.sb(s2, "ssd_vec", [P, 24 + 512])
        t8 = [k.sb(s2, f"ssd_t{i}", [P, TT, 8]) for i in range(8)]
        decay = k.sb(s2, "ssd_decay", [P, 3, TT * 8])
        X = k.sb(s2, "ssd_x", [P, 2, 512])
        Xd = k.sb(s2, "ssd_xd", [P, 2, 512])
        Gm = k.sb(s2, "ssd_gm", [P, 2, 2, P])
        At = k.sb(s2, "ssd_at", [P, 2, P])
        L = k.sb(s2, "ssd_l", [P, 2, P])
        MT = k.sb(s2, "ssd_mt", [P, 2, P])
        St = k.sb(s2, "ssd_state", [P, HW])
        y1 = k.sb(s2, "ssd_y1", [P, 512])
        y2 = k.sb(s2, "ssd_y2", [P, 512])
        yy = k.sb(s2, "ssd_yy", [P, 512])
        ms = k.sb(s2, "ssd_ms", [P, TT, 3])
        b_g = [k.ps(s2, f"ssd_g{i}") for i in range(2)]
        b_seg = [k.ps(s2, f"ssd_seg{i}") for i in range(2)]
        b_y = k.ps(s2, "ssd_ydiag")
        b_sum = b_y
        b_off = [k.ps(s2, f"ssd_yoff{i}") for i in range(2)]
        b_st = k.ps(s2, "ssd_st")
        (vec_in, e_ready, a_ready, sums_ready, decay_ready, x_ready, g_done, gm_ready, at_ready, seg_done, l_ready,
         mt_ready, ydiag_done, yoff_done, st_done, st_ready, y_free, step_d, step_a, sq_ready, rms_ready, lg_ready) = (
            k.sem("ssd_" + x) for x in ("vec_in", "e", "a", "sums", "decay", "x", "g", "gm", "at", "seg", "l", "mt",
                                        "ydiag", "yoff", "stdone", "st", "yfree", "stepd", "stepa", "sq", "rms",
                                        "lg"))
        z_ready = k.sem("ssd_z")
        dtb, al, dsk, nw = (k_vec[:, 0:8], k_vec[:, 8:16], k_vec[:, 16:24], k_vec[:, 24:536])
        pre, ex, dt, a_t, tmp, tmp2, tmp3, A = t8
        dr = k.v[:, :, 68:76]
        NU = TT * SSD_HEADS
        with nc.Block() as block:
            @block.sync
            def _(sp):
                sp.dma_start(k_vec[:, 0:24], k.d["vecs"][:, 0:24]).then_inc(vec_in, 16)
                sp.dma_start(nw, k.vec("ssd_norm_w")).then_inc(vec_in, 16)

            @block.tensor
            def _(pe):
                pe.wait_ge(a_ready, 1)
                Af = A[:].rearrange("p c h -> p (c h)")
                for i, m in enumerate(("after", "ones", "upto")):
                    ins = pe.matmul(b_sum[:, i * 32:(i + 1) * 32], k.c(m), Af, start=True, stop=True)
                ins.then_inc(sums_ready, 1)
                for c in range(TT):
                    tok = slice(c * P, (c + 1) * P)
                    if c >= 1:
                        pe.wait_ge(gm_ready, c)
                    for g in range(2):
                        r = slice(HD * g, HD * (g + 1))
                        ins = pe.matmul(b_g[g][:, 0:P], k.xbcT[r, 4, tok], k.xbcT[r, 5, tok],
                                        start=True, stop=True)
                    ins.then_inc(g_done, 1)
                    if c >= 1:
                        pe.wait_ge(st_ready, c)
                        pe.wait_ge(y_free, c)
                        for g in range(2):
                            r = slice(HD * g, HD * (g + 1))
                            ins = pe.matmul(b_off[g][:, 0:HW], k.xbcT[r, 5, tok], St[r, :],
                                            start=True, stop=True)
                        ins.then_inc(yoff_done, 1)
                    pe.wait_ge(x_ready, c + 1)
                    if c < TT - 1:
                        for g in range(2):
                            ins = pe.matmul(b_st[:, g * HW:(g + 1) * HW], xs[:, c, 512:640],
                                            Xd[:, c % 2, g * HW:(g + 1) * HW], start=True, stop=True)
                        ins.then_inc(st_done, 1)
                    for h in range(SSD_HEADS + 1):
                        if h < SSD_HEADS:
                            u = c * SSD_HEADS + h
                            pe.wait_ge(at_ready, u + 1)
                            if u >= 2:
                                pe.wait_ge(l_ready, u - 1)
                            pe.matmul(b_seg[u % 2][:, 0:P], At[:, u % 2, :], k.c("upto"), start=True,
                                      stop=True).then_inc(seg_done, 1)
                        if h >= 1:
                            u = c * SSD_HEADS + h - 1
                            pe.wait_ge(mt_ready, u + 1)
                            pe.matmul(b_y[:, (h - 1) * HD:h * HD], MT[:, u % 2, :],
                                      X[:, c % 2, (h - 1) * HD:h * HD], start=True, stop=True).then_inc(ydiag_done, 1)

            @block.gpsimd
            def _(pool):
                pool.wait_ge(a_ready, 1)
                for u in range(NU):
                    c, h = divmod(u, SSD_HEADS)
                    if u >= 2:
                        pool.wait_ge(seg_done, u - 1)
                    pool.tensor_scalar(At[:, u % 2, :], k.c("after"), A[:, c, h:h + 1], None,
                                       ALU.mult).then_inc(at_ready, 1)

            @block.scalar
            def _(act):
                for c in range(TT):
                    act.activation(k.sz[:, c, :], k.sz[:, c, :], ACT.Silu).then_inc(z_ready, 1)
                act.wait_ge(vec_in, 32)
                act.activation(a_t[:, 0, :], al, ACT.Exp).then_inc(e_ready, 1)
                act.wait_ge(step_d, 3)
                act.activation(ex[:], tmp[:], ACT.Exp).then_inc(e_ready, 1)
                act.wait_ge(step_d, 4)
                act.activation(tmp3[:], tmp2[:], ACT.Ln).then_inc(lg_ready, 1)
                act.wait_ge(sums_ready, 1)
                act.activation(decay[:], b_sum[:, 0:96].rearrange("p (a b) -> p a b", a=3),
                               ACT.Exp).then_inc(decay_ready, 1)
                for u in range(NU):
                    act.wait_ge(seg_done, u + 1)
                    if u >= 2:
                        act.wait_ge(mt_ready, u - 1)
                    act.activation(L[:, u % 2, :], b_seg[u % 2][:, 0:P], ACT.Exp).then_inc(l_ready, 1)
                for c in range(TT):
                    act.wait_ge(sq_ready, c + 1)
                    act.activation(ms[:, c, 1:2], ms[:, c, 0:1], ACT.Sqrt, scale=1.0,
                                   bias=0.0).then_inc(rms_ready, 1)

            @block.vector
            def _(dve):
                step = Chain(dve, step_d)
                dve.wait_ge(vec_in, 32)
                step(dve.tensor_tensor(pre[:], dr, bc(dtb, 1, TT), ALU.add))
                step(dve.tensor_scalar(dt[:], pre[:], -1.0, None, ALU.mult))
                step(dve.tensor_tensor(tmp[:], pre[:], dt[:], ALU.min))
                dve.wait_ge(e_ready, 2)
                step(dve.tensor_scalar(tmp2[:], ex[:], 1.0, None, ALU.add))
                step(dve.tensor_scalar(dt[:], tmp2[:], -1.0, 1e-30, ALU.add, ALU.max))
                step(dve.reciprocal(tmp[:], dt[:]))
                step(dve.tensor_tensor(dt[:], tmp[:], ex[:], ALU.mult))
                dve.wait_ge(lg_ready, 1)
                step(dve.tensor_tensor(tmp3[:], tmp3[:], dt[:], ALU.mult))
                step(dve.tensor_scalar(tmp2[:], tmp2[:], 1.0, None, ALU.is_equal))
                step(dve.tensor_tensor(tmp2[:], tmp2[:], ex[:], ALU.mult))
                step(dve.tensor_tensor(tmp3[:], tmp3[:], tmp2[:], ALU.add))
                step(dve.scalar_tensor_tensor(dt[:], pre[:], 0.0, tmp3[:], ALU.max, ALU.add))
                step(dve.tensor_scalar(a_t[:, 1, :], a_t[:, 0, :], -1.0, None, ALU.mult))
                dve.tensor_tensor(A[:], dt[:], bc(a_t[:, 1, :], 1, TT), ALU.mult).then_inc(a_ready, 1)
                dve.wait_ge(decay_ready, 1)
                h8 = dict(h=8)
                for c in range(TT):
                    cs = slice(c * 8, c * 8 + 8)
                    xc = xs[:, c, 0:512].rearrange("p (h d) -> p h d", **h8)
                    Xc = X[:, c % 2, :].rearrange("p (h d) -> p h d", **h8)
                    Xdc = Xd[:, c % 2, :].rearrange("p (h d) -> p h d", **h8)
                    step(dve.tensor_tensor(Xc, xc, bc(dt[:, c, :], 2, HD), ALU.mult))
                    dve.tensor_tensor(Xdc, Xc, bc(decay[:, 0, cs], 2, HD), ALU.mult).then_inc(x_ready, 1)
                    dve.wait_ge(g_done, c + 1)
                    for g in range(2):
                        ins = dve.tensor_tensor(Gm[:, c % 2, g, :], b_g[g][:, 0:P], k.c("upto"), ALU.mult)
                        if g == 0:
                            step(ins)
                    ins.then_inc(gm_ready, 1)
                    if c < TT - 1:
                        dve.wait_ge(st_done, c + 1)
                        if c >= 1:
                            dve.wait_ge(yoff_done, c)
                            s3 = St[:].rearrange("p (h d) -> p h d", h=4)
                            for g in range(2):
                                r = slice(HD * g, HD * (g + 1))
                                step(dve.tensor_tensor(s3[r], s3[r], bc(decay[r, 1, c * 8 + 4 * g:c * 8 + 4 * g + 4], 2, HD),
                                                       ALU.mult))
                            for g in range(2):
                                r = slice(HD * g, HD * (g + 1))
                                ins = dve.tensor_tensor(St[r, :], St[r, :], b_st[r, g * HW:(g + 1) * HW], ALU.add)
                                if g == 0:
                                    step(ins)
                            ins.then_inc(st_ready, 1)
                        else:
                            for g in range(2):
                                r = slice(HD * g, HD * (g + 1))
                                ins = dve.tensor_copy(St[r, :], b_st[r, g * HW:(g + 1) * HW])
                                if g == 0:
                                    step(ins)
                            ins.then_inc(st_ready, 1)
                    dve.wait_ge(gm_ready, c + 1)
                    for h in range(SSD_HEADS):
                        u = c * SSD_HEADS + h
                        dve.wait_ge(l_ready, u + 1)
                        if u >= 2:
                            dve.wait_ge(ydiag_done, u - 1)
                        dve.tensor_tensor(MT[:, u % 2, :], L[:, u % 2, :], Gm[:, c % 2, h // 4, :],
                                          ALU.mult).then_inc(mt_ready, 1)
                    y13, y23 = (t[:].rearrange("p (h d) -> p h d", **h8) for t in (y1, y2))
                    step(dve.tensor_tensor(y13, xc, bc(dsk, 2, HD), ALU.mult))
                    if c >= 1:
                        dve.wait_ge(yoff_done, c)
                        for g in range(2):
                            hs = slice(4 * g, 4 * g + 4)
                            step(dve.tensor_tensor(y23[:, hs], b_off[g][:, 0:HW].rearrange("p (h d) -> p h d", h=4),
                                                   bc(decay[:, 2, c * 8 + 4 * g:c * 8 + 4 * g + 4], 2, HD), ALU.mult))
                        step(dve.tensor_tensor(y1[:], y1[:], y2[:], ALU.add))
                    dve.wait_ge(ydiag_done, (c + 1) * SSD_HEADS)
                    dve.tensor_tensor(y2[:], y1[:], b_y[:], ALU.add).then_inc(y_free, 1)
                    dve.wait_ge(y_free, c + 1)
                    dve.wait_ge(z_ready, c + 1)
                    step(dve.tensor_tensor(k.y[:, c, :], y2[:], k.sz[:, c, :], ALU.mult))
                    step(dve.tensor_tensor(yy[:], k.y[:, c, :], k.y[:, c, :], ALU.mult))
                    step(dve.reduce_sum(ms[:, c, 2:3], yy[:], AX))
                    dve.tensor_scalar(ms[:, c, 0:1], ms[:, c, 2:3], 1.0 / 512, LN_EPS, ALU.mult,
                                      ALU.add).then_inc(sq_ready, 1)
                for c in range(TT):
                    dve.wait_ge(rms_ready, c + 1)
                    step(dve.reciprocal(ms[:, c, 2:3], ms[:, c, 1:2]))
                    step(dve.scalar_tensor_tensor(k.y[:, c, :], k.y[:, c, :], ms[:, c, 2:3], nw, ALU.mult, ALU.mult))


def layer_norm(k, name, x, g, b, extra=None):
    nc = k.nc
    with ExitStack() as s:
        vec = k.sb(s, f"{name}_gb", [P, 2, DM])
        stats = k.sb(s, f"{name}_stats", [P, TT, 2, 6])
        mv = k.sb(s, f"{name}_mv", [P, TT, 2])
        sd = k.sb(s, f"{name}_sd", [P, 3, TT])
        tmp = k.sb(s, f"{name}_tmp", [P, DM])
        vec_in, var_ready, sd_ready, step_d = (k.sem(f"{name}_{n}") for n in ("vecin", "var", "sd", "step"))
        with nc.Block() as block:
            @block.sync
            def _(sp):
                sp.dma_start(vec[:, 0, :], k.vec(g)).then_inc(vec_in, 16)
                sp.dma_start(vec[:, 1, :], k.vec(b)).then_inc(vec_in, 16)

            @block.vector
            def _(dve):
                step = Chain(dve, step_d)
                for tt in range(TT):
                    step(dve.bn_stats(stats[:, tt, 0, :], x[:, tt, 0:512]))
                    step(dve.bn_stats(stats[:, tt, 1, :], x[:, tt, 512:1024]))
                    step(dve.bn_aggr(mv[:, tt, :], stats[:, tt, :, :].rearrange("p a b -> p (a b)")))
                dve.tensor_scalar(sd[:, 0, :], mv[:, :, 1], LN_EPS, None, ALU.add).then_inc(var_ready, 1)
                dve.wait_ge(vec_in, 32)
                dve.wait_ge(sd_ready, 1)
                step(dve.reciprocal(sd[:, 2, :], sd[:, 1, :]))
                for tt in range(TT):
                    step(dve.tensor_scalar(tmp[:], x[:, tt, :], mv[:, tt, 0:1], sd[:, 2, tt:tt + 1], ALU.subtract,
                                           ALU.mult))
                    step(dve.tensor_tensor(tmp[:], tmp[:], vec[:, 0, :], ALU.mult))
                    step(dve.tensor_tensor(x[:, tt, :], tmp[:], vec[:, 1, :], ALU.add))

            @block.scalar
            def _(act):
                act.wait_ge(var_ready, 1)
                act.activation(sd[:, 1, :], sd[:, 0, :], ACT.Sqrt).then_inc(sd_ready, 1)


def rms_rows(k, name, x, out, gain, width=DM, eps=EPS, then=()):
    nc = k.nc
    with ExitStack() as s:
        vec = k.sb(s, f"{name}_gain", [P, width])
        sq = k.sb(s, f"{name}_sq", [P, 2, width])
        m = k.sb(s, f"{name}_ms", [P, 4, TT])
        vec_in, summed, sd_ready, ms_ready, step_d = (k.sem(f"{name}_{n}") for n in ("vecin", "sum", "sd", "ms", "step"))
        with nc.Block() as block:
            @block.sync
            def _(sp):
                sp.dma_start(vec[:], k.vec(gain)).then_inc(vec_in, 16)
                for chunk in then:
                    k.load_chunk(sp, chunk)

            @block.scalar
            def _(act):
                for tt in range(TT):
                    act.activation(sq[:, tt % 2, :], x(tt), ACT.Square, accum_out=m[:, 0, tt:tt + 1]).then_inc(summed, 1)
                    act.wait_ge(summed, tt + 1)
                act.wait_ge(ms_ready, 1)
                act.activation(m[:, 2, :], m[:, 1, :], ACT.Sqrt).then_inc(sd_ready, 1)

            @block.vector
            def _(dve):
                step = Chain(dve, step_d)
                dve.wait_ge(summed, TT)
                dve.tensor_scalar(m[:, 1, :], m[:, 0, :], 1.0 / width, eps, ALU.mult, ALU.add).then_inc(ms_ready, 1)
                dve.wait_ge(sd_ready, 1)
                step(dve.reciprocal(m[:, 3, :], m[:, 2, :]))
                dve.wait_ge(vec_in, 16)
                for tt in range(TT):
                    step(dve.scalar_tensor_tensor(out(tt), x(tt), m[:, 3, tt:tt + 1], vec[:], ALU.mult, ALU.mult))


def project(k, name, lhsT, chunks, evac, ahead=(), then=()):
    nc = k.nc
    n = len(chunks)
    RING = 4
    kd = chunks[0].shape[1]
    width = [c.shape[2] for c in chunks]
    q0 = k.chunks_loaded - ahead
    wh, wl = k.w_ring
    with ExitStack() as s:
        banks = [k.ps(s, f"{name}_bank{i}") for i in range(2 * TT)]
        hi_ready, lo_ready, piece_done, done, free, step_d = (
            k.sem(f"{name}_{x}") for x in ("hi", "lo", "piece", "done", "free", "step"))
        with nc.Block() as block:
            @block.sync
            def _(sp):
                for i, chunk in list(enumerate(list(chunks) + list(then)))[ahead:]:
                    if i >= 2:
                        sp.wait_ge(lo_ready, kd * (i - 1))
                    k.load_chunk(sp, chunk)

            @block.scalar
            def _(act):
                for i in range(n):
                    slot, turn = (q0 + i) % 2, (q0 + i) // 2
                    act.wait_ge(k.w_in[slot], 16 * (turn + 1))
                    for c in range(kd):
                        j = i * kd + c
                        if j >= RING:
                            act.wait_ge(piece_done, j - RING + 1)
                        act.activation(wh[:, j % RING, 0:width[i]], k.w[:, slot, c, 0:width[i]],
                                       ACT.Copy).then_inc(hi_ready, 1)

            @block.gpsimd
            def _(pool):
                for i in range(n):
                    for c in range(kd):
                        j = i * kd + c
                        pool.wait_ge(hi_ready, j + 1)
                        pool.tensor_tensor(wl[:, j % RING, 0:width[i]], k.w[:, (q0 + i) % 2, c, 0:width[i]],
                                           wh[:, j % RING, 0:width[i]].bitcast(F32), ALU.subtract).then_inc(lo_ready, 1)

            @block.tensor
            def _(pe):
                for i in range(n):
                    for c in range(kd):
                        j = i * kd + c
                        pe.wait_ge(lo_ready, j + 1)
                        for tt in range(TT):
                            u = i * TT + tt
                            if c == 0 and i >= 2:
                                pe.wait_ge(free, u - 2 * TT + 1)
                            ins = three_passes(pe, banks[u % (2 * TT)][:, 0:width[i]], lhsT(tt, c),
                                               (wh[:, j % RING, 0:width[i]], wl[:, j % RING, 0:width[i]]),
                                               c == 0, c == kd - 1)
                            if c < kd - 1 and tt == TT - 1:
                                ins.then_inc(piece_done, 1)
                            elif c == kd - 1 and tt < TT - 1:
                                ins.then_inc(done, 1)
                    ins.then_inc(piece_done, 1)

            @block.vector
            def _(dve):
                step = Chain(dve, step_d)
                for i in range(n):
                    for tt in range(TT):
                        if tt < TT - 1:
                            dve.wait_ge(done, i * (TT - 1) + tt + 1)
                        else:
                            dve.wait_ge(piece_done, kd * (i + 1))
                        evac(dve, step, i, tt, banks[(i * TT + tt) % (2 * TT)]).then_inc(free, 1)
                        dve.wait_ge(free, i * TT + tt + 1)


def route(k, name, E, G, S, bias, logits_w, ctx):
    nc = k.nc
    PG, NT, W = E // G, most_tiles(E, S), G + E
    k.gate = k.sb(ctx, f"{name}_gate", [P, 2, TT])
    k.slot = k.sb(ctx, f"{name}_slot", [P, 2, TT], U32)
    k.tok_of = k.sb(ctx, f"{name}_tok_of", [S, NT], U32)
    k.exp_of = k.sb(ctx, f"{name}_exp_of", [1, NT], I32)
    k.used = k.sb(ctx, f"{name}_used", [1, 1], I32)
    with ExitStack() as s:
        wr = k.sb(s, f"{name}_wr", [P, KD, W])
        wrh, wrl = (k.sb(s, f"{name}_wr{x}", [P, KD, W], F32R) for x in ("hi", "lo"))
        wr_ready = k.sem(f"{name}_wr_ready")
        bv = k.sb(s, f"{name}_bv", [P, W])
        lg = k.sb(s, f"{name}_lg", [P, TT, W])
        small = [k.sb(s, f"{name}_small{i}", [P, TT]) for i in range(8)]
        g4 = [k.sb(s, f"{name}_g{i}", [P, TT, G]) for i in range(4)]
        e4 = [k.sb(s, f"{name}_e{i}", [P, TT, PG]) for i in range(6)]
        wide = k.sb(s, f"{name}_wide", [P, TT, G, PG])
        OH = [k.sb(s, f"{name}_oh{i}", [P, TT, G, PG]) for i in range(2)]
        M = k.sb(s, f"{name}_m", [P, TT, E])
        tiles, cum, base, zero = (k.sb(s, f"{name}_{n}", [P, E]) for n in ("tiles", "cum", "base", "zero"))
        rank = k.sb(s, f"{name}_rank", [P, TT, E])
        counts = k.sb(s, f"{name}_counts", [P, E])
        cmp = k.sb(s, f"{name}_cmp", [1, NT, E])
        tef = k.sb(s, f"{name}_tef", [1, NT])
        pos, q, jt, r, slotf = (k.sb(s, f"{name}_{n}", [P, 2, TT]) for n in ("pos", "q", "jt", "r", "slotf"))
        ohr = k.sb(s, f"{name}_ohr", [P, 2 * TT, S])
        ohj = k.sb(s, f"{name}_ohj", [P, 2 * TT, NT])
        lbank, rbank, tbank = (k.ps(s, f"{name}_{n}") for n in ("lbank", "rbank", "tbank"))
        (in_ready, logits_done, step_d, diff_ready, exp_ready, m_ready, rank_done, oh_ready, tok_done) = (
            k.sem(f"{name}_{n}") for n in ("in", "logits", "step", "diff", "exp", "mready", "rank", "oh", "tok"))
        with nc.Block() as block:
            @block.sync
            def _(sp):
                sp.dma_start(wr[:], logits_w).then_inc(in_ready, 16)
                sp.dma_start(bv[:], k.vec(bias)).then_inc(in_ready, 16)

            @block.tensor
            def _(pe):
                pe.wait_ge(in_ready, 32)
                pe.wait_ge(wr_ready, 2)
                for tt in range(TT):
                    for c in range(KD):
                        ins = three_passes(pe, lbank[:, tt * W:(tt + 1) * W], k.xs_lhs(tt, c),
                                           (wrh[:, c, :], wrl[:, c, :]), c == 0, c == KD - 1)
                ins.then_inc(logits_done, 1)
                pe.wait_ge(m_ready, 1)
                for tt in range(TT):
                    for t in range(tt + 1):
                        pe.matmul(rbank[:, tt * E:(tt + 1) * E], k.c("before" if t == tt else "ones"), M[:, t, :],
                                  start=(t == 0), stop=(t == tt))
                for t in range(TT):
                    ins = pe.matmul(rbank[:, TT * E:(TT + 1) * E], k.c("ones"), M[:, t, :], start=(t == 0),
                                    stop=(t == TT - 1))
                ins.then_inc(rank_done, 1)
                pe.wait_ge(oh_ready, 1)
                for i in range(2 * TT):
                    ins = pe.matmul(tbank[0:S, 0:NT], ohr[:, i, :], ohj[:, i, :], start=(i == 0), stop=(i == 2 * TT - 1))
                ins.then_inc(tok_done, 1)

            @block.gpsimd
            def _(pool):
                pool.wait_ge(in_ready, 32)
                pool.tensor_copy(wrh[:], wr[:]).then_inc(wr_ready, 1)
                pool.wait_ge(wr_ready, 1)
                pool.tensor_tensor(wrl[:], wr[:], wrh[:].bitcast(F32), ALU.subtract).then_inc(wr_ready, 1)

            @block.scalar
            def _(act):
                act.wait_ge(diff_ready, 1)
                act.activation(g4[1][:], g4[0][:], ACT.Exp).then_inc(exp_ready, 1)
                act.wait_ge(diff_ready, 2)
                act.activation(small[5][:], small[4][:], ACT.Exp).then_inc(exp_ready, 1)

            @block.vector
            def _(dve):
                step = Chain(dve, step_d)

                def first_best(x, best, down, key, onehot, n):
                    step(dve.reduce_max(best[:], x, AX))
                    step(dve.tensor_tensor(key, x, bc(best[:], 2, n), ALU.is_equal))
                    step(dve.tensor_tensor(key, key, down, ALU.mult))
                    step(dve.reduce_max(small[7][:], key, AX))
                    step(dve.tensor_tensor(onehot, key, bc(small[7][:], 2, n), ALU.is_equal))

                def down(n):
                    a = k.c("down")[:, P - n:P]
                    return bc(a, 1, TT)

                dve.wait_ge(in_ready, 32)
                dve.wait_ge(logits_done, 1)
                step(dve.tensor_tensor(lg[:], lbank[:, 0:TT * W].rearrange("p (t w) -> p t w", t=TT), bc(bv[:], 1, TT),
                                       ALU.add))
                gl = lg[:, :, 0:G]
                first_best(gl, small[0], down(G), g4[2][:], g4[3][:], G)
                dve.tensor_tensor(g4[0][:], gl, bc(small[0][:], 2, G), ALU.subtract).then_inc(diff_ready, 1)
                dve.wait_ge(exp_ready, 1)
                step(dve.reduce_sum(small[1][:], g4[1][:], AX))
                step(dve.reciprocal(small[2][:], small[1][:]))
                step(dve.tensor_tensor(wide[:], lg[:, :, G:W].rearrange("p t (g e) -> p t g e", g=G),
                                       bc(g4[3][:], 3, PG), ALU.mult))
                step(dve.reduce_sum(e4[0][:], wide[:].rearrange("p t g e -> p t e g"), AX))
                first_best(e4[0][:], small[1], down(PG), e4[1][:], e4[2][:], PG)
                step(dve.scalar_tensor_tensor(e4[3][:], e4[2][:], NEG, e4[0][:], ALU.mult, ALU.add))
                first_best(e4[3][:], small[3], down(PG), e4[1][:], e4[4][:], PG)
                dve.tensor_tensor(small[4][:], small[3][:], small[1][:], ALU.subtract).then_inc(diff_ready, 1)
                dve.wait_ge(exp_ready, 2)
                step(dve.tensor_scalar(small[6][:], small[5][:], 1.0, None, ALU.add))
                step(dve.reciprocal(small[0][:], small[6][:]))
                step(dve.tensor_tensor(k.gate[:, 0, :], small[0][:], small[2][:], ALU.mult))
                step(dve.tensor_tensor(k.gate[:, 1, :], k.gate[:, 0, :], small[5][:], ALU.mult))
                for i, oh in enumerate((e4[2], e4[4])):
                    for tt in range(TT):
                        step(dve.tensor_tensor(OH[i][:, tt], bc(g4[3][:, tt, :], 2, PG), bc(oh[:, tt, :], 1, G), ALU.mult))
                flat = [o[:].rearrange("p t g e -> p t (g e)") for o in OH]
                dve.tensor_tensor(M[:], flat[0], flat[1], ALU.add).then_inc(m_ready, 1)
                dve.wait_ge(rank_done, 1)
                step(dve.tensor_copy(rank[:], rbank[:, 0:TT * E].rearrange("p (t e) -> p t e", t=TT)))
                step(dve.tensor_copy(counts[:], rbank[:, TT * E:(TT + 1) * E]))
                step(dve.memset(zero[:], 0.0))
                step(dve.tensor_scalar(tiles[:], counts[:], 0.5, None, ALU.is_gt))
                for j in range(1, -(-SEQ // S)):
                    step(dve.scalar_tensor_tensor(tiles[:], counts[:], j * S + 0.5, tiles[:], ALU.is_gt, ALU.add))
                step(dve.tensor_tensor_scan(cum[:], tiles[:], zero[:], 0.0, ALU.add, ALU.add))
                step(dve.tensor_tensor(base[:], cum[:], tiles[:], ALU.subtract))
                for i in range(2):
                    step(dve.tensor_tensor(M[:], flat[i], rank[:], ALU.mult))
                    step(dve.reduce_sum(pos[:, i, :], M[:], AX))
                    step(dve.tensor_tensor(M[:], flat[i], bc(base[:], 1, TT), ALU.mult))
                    step(dve.reduce_sum(jt[:, i, :], M[:], AX))
                step(dve.scalar_tensor_tensor(slotf[:], jt[:], float(S), pos[:], ALU.mult, ALU.add))
                step(dve.tensor_copy(k.slot[:], slotf[:]))
                step(dve.tensor_scalar(q[:], pos[:], S - 0.5, None, ALU.is_gt))
                for j in range(2, -(-SEQ // S)):
                    step(dve.scalar_tensor_tensor(q[:], pos[:], j * S - 0.5, q[:], ALU.is_gt, ALU.add))
                step(dve.tensor_tensor(jt[:], jt[:], q[:], ALU.add))
                step(dve.scalar_tensor_tensor(r[:], q[:], -float(S), pos[:], ALU.mult, ALU.add))
                for i in range(2):
                    for tt in range(TT):
                        step(dve.tensor_scalar(ohr[:, i * TT + tt, :], k.c("iota")[:, 0:S], r[:, i, tt:tt + 1], None,
                                               ALU.is_equal))
                        ins = dve.tensor_scalar(ohj[:, i * TT + tt, :], k.c("iota")[:, 0:NT], jt[:, i, tt:tt + 1],
                                                k.c("tok")[:, tt:tt + 1], ALU.is_equal, ALU.mult)
                        if (i, tt) != (1, TT - 1):
                            step(ins)
                ins.then_inc(oh_ready, 1)
                step(dve.tensor_tensor(cmp[:], bc(k.c("iota")[0:1, 0:NT], 2, E), bc(base[0:1, :], 1, NT), ALU.is_ge))
                step(dve.reduce_sum(tef[:], cmp[:], AX))
                step(dve.tensor_scalar(k.exp_of[:], tef[:], -1.0, None, ALU.add))
                step(dve.tensor_copy(k.used[:], cum[0:1, E - 1:E]))
                dve.wait_ge(tok_done, 1)
                step(dve.tensor_copy(k.tok_of[:], tbank[0:S, 0:NT]))


def experts(k, name, E, S, x_in, rows, w_gu, w_dn, out_rows, x_store):
    nc = k.nc
    NT = most_tiles(E, S)
    GU, DN = KD * 2 * FF, 2 * DM
    with ExitStack() as s:
        w1 = [k.sb(s, f"{name}_w1_{i}", [P, GU]) for i in range(2)]
        w2 = [k.sb(s, f"{name}_w2_{i}", [P, DN]) for i in range(2)]
        xg = [k.sb(s, f"{name}_xg{i}", [S, DM]) for i in range(2)]
        idx = [k.sb(s, f"{name}_idx{i}", [S, 1], U32) for i in range(2)]
        xT = [k.sb(s, f"{name}_xT{i}", [P, KD * S]) for i in range(2)]
        sg = k.sb(s, f"{name}_sg", [S, FF])
        hid = k.sb(s, f"{name}_hid", [S, FF])
        hT = [k.sb(s, f"{name}_hT{i}", [P, 2 * S]) for i in range(2)]
        y = [k.sb(s, f"{name}_y{i}", [S, DM]) for i in range(2)]
        blank = k.sb(s, f"{name}_blank", [S, DM])
        xbank = [k.ps(s, f"{name}_xbank{i}") for i in range(2)]
        gbank = [k.ps(s, f"{name}_gbank{i}") for i in range(2)]
        hbank = k.ps(s, f"{name}_hbank")
        ybank = k.ps(s, f"{name}_ybank", (P, 1024))
        XH = KD * S // 2
        w1_in, w2_in, y_out = ([k.sem(f"{name}_{n}{b}") for b in range(2)] for n in ("w1", "w2", "yout"))
        (stored, idx_ready, idx_seen, x_turned, xT_v, xT_s, gu_done, silu_ready, hid_ready, h_turned,
         hT_ready, y_done, y_v, y_s, blank_ready, pe_seen) = (k.sem(f"{name}_{n}") for n in (
             "stored", "idx", "idx_seen", "x_turned", "xT_v", "xT_s", "gu", "silu", "hid", "h_turned",
             "hT", "y_done", "y_v", "y_s", "blank", "pe_seen"))

        def every_tile(eng, used, tile, empty=None):
            tile(0, 0)
            tile(0, 1)
            with eng.Fori(1, NT // 2) as i:
                for b in range(2):
                    with eng.If(used > 2 * i + b):
                        tile(i, b)
                    if empty:
                        with eng.If(used < 2 * i + (b + 1)):
                            empty(i, b)
            if NT % 2:
                with eng.If(used > NT - 1):
                    tile(NT // 2, 0)
                if empty:
                    with eng.If(used < NT):
                        empty(NT // 2, 0)

        with nc.Block() as block:
            @block.sync
            def _(sp):
                used = sp.value_load(k.used[0:1, 0:1], min_val=2, max_val=NT)
                for tt in range(TT):
                    sp.dma_start(rows[tt * P:(tt + 1) * P, :], x_store(tt)).then_inc(stored, 16)

                def tile(i, b):
                    t = 2 * i + b
                    first = isinstance(i, int) and i == 0
                    e = sp.value_load(k.exp_of[0:1, bass.ds(t, 1)], min_val=0, max_val=E - 1)
                    if not first:
                        sp.wait_ge(gu_done, t - 1)
                    sp.dma_start(w1[b][:], w_gu[bass.ds(e, 1)].rearrange("a p n -> (a p) n")).then_inc(w1_in[b], 16)
                    if not first:
                        sp.wait_ge(y_done, t - 1)
                    sp.dma_start(w2[b][:], w_dn[bass.ds(e, 1)].rearrange("a p n -> (a p) n")).then_inc(w2_in[b], 16)

                every_tile(sp, used, tile)
                sp.wait_ge(y_out[0], 16 * ((NT + 1) // 2))
                sp.wait_ge(y_out[1], 16 * (NT // 2))

            @block.gpsimd
            def _(pool):
                used = pool.value_load(k.used[0:1, 0:1], min_val=2, max_val=NT)
                pool.wait_ge(stored, 16 * TT)

                def tile(i, b):
                    t = 2 * i + b
                    if not (isinstance(i, int) and i == 0):
                        pool.wait_ge(x_turned, t - 1)
                    pool.tensor_copy(idx[b][:], k.tok_of[:, bass.ds(t, 1)]).then_inc(idx_ready, 1)
                    pool.wait_ge(idx_ready, t + 1)
                    pool.sem_inc(idx_seen, 1)
                    pool.indirect_dma_start(xg[b][:], None, rows,
                                            bass.IndirectOffsetOnAxis(ap=idx[b][:], axis=0)).then_inc(x_in[b], 16)

                every_tile(pool, used, tile)

            @block.tensor
            def _(pe):
                used = pe.value_load(k.used[0:1, 0:1], min_val=2, max_val=NT)

                def turn_x(i, b):
                    t = 2 * i + b
                    pe.wait_ge(x_in[b], 16 * i + 16)
                    pe.wait_ge(xT_v, t)
                    pe.wait_ge(xT_s, t)
                    pe.sem_inc(pe_seen, 1)
                    for c in range(KD):
                        ins = pe.transpose(xbank[c * 2 // KD][:, c * S % XH:c * S % XH + S], xg[b][:, c * P:(c + 1) * P],
                                           k.c("ident")[0:S, 0:S])
                    ins.then_inc(x_turned, 1)

                def down(i, b, t):
                    pe.wait_ge(w2_in[b], 16 * i + 16)
                    pe.wait_ge(hT_ready, t + 1)
                    pe.wait_ge(y_v, t)
                    pe.wait_ge(y_s, t)
                    for m in range(2):
                        for c in range(2):
                            ins = pe.matmul(ybank[0:S, m * 512:(m + 1) * 512], hT[b][:, c * S:(c + 1) * S],
                                            w2[b][:, c * DM + m * 512:c * DM + (m + 1) * 512], start=(c == 0),
                                            stop=(c == 1))
                    ins.then_inc(y_done, 1)

                def tile(i, b):
                    t = 2 * i + b
                    pe.wait_ge(w1_in[b], 16 * i + 16)
                    pe.wait_ge(xT_v, t + 1)
                    pe.wait_ge(xT_s, t + 1)
                    for c in range(KD):
                        ins = pe.matmul(gbank[b][0:S, :], xT[b][:, c * S:(c + 1) * S],
                                        w1[b][:, c * 2 * FF:(c + 1) * 2 * FF], start=(c == 0), stop=(c == KD - 1))
                    ins.then_inc(gu_done, 1)
                    with pe.If(used > t + 1):
                        turn_x(i + b, 1 - b)
                    if not (isinstance(i, int) and t == 0):
                        down(i - (1 - b), 1 - b, t - 1)
                    pe.wait_ge(hid_ready, t + 1)
                    pe.sem_inc(pe_seen, 1)
                    for c in range(2):
                        ins = pe.transpose(hbank[:, c * S:(c + 1) * S], hid[:, c * P:(c + 1) * P],
                                           k.c("ident")[0:S, 0:S])
                    ins.then_inc(h_turned, 1)
                    with pe.If(used < t + 2):
                        down(i, b, t)

                turn_x(0, 0)
                every_tile(pe, used, tile)

            @block.vector
            def _(dve):
                used = dve.value_load(k.used[0:1, 0:1], min_val=2, max_val=NT)

                def copy_x(i, b):
                    dve.wait_ge(x_turned, 2 * i + b + 1)
                    dve.tensor_copy(xT[b][:, 0:XH], xbank[0][:, 0:XH]).then_inc(xT_v, 1)

                def take_y(i, b, t):
                    dve.wait_ge(y_done, t + 1)
                    dve.wait_ge(y_out[b], 16 * i)
                    dve.tensor_copy(y[b][:, 0:512], ybank[0:S, 0:512]).then_inc(y_v, 1)

                def tile(i, b):
                    t = 2 * i + b
                    dve.wait_ge(silu_ready, t + 1)
                    dve.wait_ge(gu_done, t + 1)
                    dve.tensor_tensor(hid[:], sg[:], gbank[b][0:S, FF:2 * FF], ALU.mult).then_inc(hid_ready, 1)
                    with dve.If(used > t + 1):
                        copy_x(i + b, 1 - b)
                    dve.wait_ge(h_turned, t + 1)
                    dve.tensor_copy(hT[b][:], hbank[:, 0:2 * S]).then_inc(hT_ready, 1)
                    if not (isinstance(i, int) and t == 0):
                        take_y(i - (1 - b), 1 - b, t - 1)
                    with dve.If(used < t + 2):
                        take_y(i, b, t)

                dve.memset(blank[:], 0.0).then_inc(blank_ready, 1)
                copy_x(0, 0)
                every_tile(dve, used, tile)

            @block.scalar
            def _(act):
                used = act.value_load(k.used[0:1, 0:1], min_val=2, max_val=NT)

                def copy_x(i, b):
                    act.wait_ge(x_turned, 2 * i + b + 1)
                    act.activation(xT[b][:, XH:2 * XH], xbank[1][:, 0:XH], ACT.Copy).then_inc(xT_s, 1)

                def take_y(i, b, t):
                    act.wait_ge(y_done, t + 1)
                    act.wait_ge(y_out[b], 16 * i)
                    act.activation(y[b][:, 512:1024], ybank[0:S, 512:1024], ACT.Copy).then_inc(y_s, 1)
                    act.wait_ge(y_s, t + 1)
                    act.wait_ge(y_v, t + 1)
                    act.dma_start(out_rows[bass.ds(t * S, S), :], y[b][:]).then_inc(y_out[b], 16)

                def tile(i, b):
                    t = 2 * i + b
                    act.wait_ge(gu_done, t + 1)
                    act.wait_ge(hid_ready, t)
                    act.activation(sg[:], gbank[b][0:S, 0:FF], ACT.Silu).then_inc(silu_ready, 1)
                    with act.If(used > t + 1):
                        copy_x(i + b, 1 - b)
                    if not (isinstance(i, int) and t == 0):
                        take_y(i - (1 - b), 1 - b, t - 1)
                    with act.If(used < t + 2):
                        take_y(i, b, t)

                def empty(i, b):
                    act.dma_start(out_rows[bass.ds((2 * i + b) * S, S), :], blank[:]).then_inc(y_out[b], 16)

                act.wait_ge(blank_ready, 1)
                copy_x(0, 0)
                every_tile(act, used, tile, empty)


def combine(k, name, out_rows, x, scale, out=None):
    nc = k.nc
    with ExitStack() as s:
        yr = [k.sb(s, f"{name}_row{i}", [P, DM]) for i in range(4)]
        idx = k.sb(s, f"{name}_cidx", [P, 8], U32)
        row_in, row_base = k.gather_sems[4:8], list(k.gathered[4:8])
        idx_ready, used, step_d, done, out_done = (k.sem(f"{name}_{n}") for n in ("cidx", "used", "step", "xdone",
                                                                                 "outd"))
        with nc.Block() as block:
            @block.gpsimd
            def _(pool):
                for j in range(2 * TT):
                    tt, i = divmod(j, 2)
                    if j >= 4:
                        pool.wait_ge(used, j - 3)
                    pool.indirect_dma_start(yr[j % 4][:], None, out_rows, bass.IndirectOffsetOnAxis(
                        ap=k.slot[:, i, tt:tt + 1], axis=0)).then_inc(row_in[j % 4], 16)

            @block.vector
            def _(dve):
                step = Chain(dve, step_d)
                for tt in range(TT):
                    if scale != 1.0:
                        step(dve.tensor_scalar(x[:, tt, :], x[:, tt, :], scale, None, ALU.mult))
                    for i in range(2):
                        j = 2 * tt + i
                        dve.wait_ge(row_in[j % 4], row_base[j % 4] + 16 * (j // 4 + 1))
                        dve.scalar_tensor_tensor(x[:, tt, :], yr[j % 4][:], k.gate[:, i, tt:tt + 1], x[:, tt, :],
                                                 ALU.mult, ALU.add).then_inc(used, 1)
                        dve.wait_ge(used, j + 1)

            if out is not None:
                @block.sync
                def _(sp):
                    for tt in range(TT):
                        sp.wait_ge(used, 2 * tt + 2)
                        sp.dma_start(out[tt * P:(tt + 1) * P, :], x[:, tt, :]).then_inc(out_done, 16)
                    sp.wait_ge(out_done, 16 * TT)
    for b in range(4):
        k.gathered[4 + b] += 16 * (2 * TT // 4)


def head_norms(k, name, items, eps=EPS):
    nc = k.nc
    n = len(items)
    with ExitStack() as s:
        H, D = items[0][0].shape[2:]
        sq = k.sb(s, f"{name}_sq", [P, 2, H, D])
        m = k.sb(s, f"{name}_m", [P, n, 4, TT, H])
        summed, squared, ms_ready, sd_ready, step_d = (k.sem(f"{name}_{x}") for x in ("sum", "sq", "ms", "sd", "step"))
        with nc.Block() as block:
            @block.scalar
            def _(act):
                for j in range(n * TT):
                    i, tt = divmod(j, TT)
                    if j >= 2:
                        act.wait_ge(summed, j - 1)
                    act.activation(sq[:, j % 2], items[i][0][:, tt], ACT.Square).then_inc(squared, 1)
                for i in range(n):
                    act.wait_ge(ms_ready, i + 1)
                    act.activation(m[:, i, 2], m[:, i, 1], ACT.Sqrt).then_inc(sd_ready, 1)

            @block.vector
            def _(dve):
                step = Chain(dve, step_d)
                for j in range(n * TT):
                    i, tt = divmod(j, TT)
                    dve.wait_ge(squared, j + 1)
                    dve.reduce_sum(m[:, i, 0, tt], sq[:, j % 2], AX).then_inc(summed, 1)
                for i, (x, gain, scale) in enumerate(items):
                    dve.wait_ge(summed, (i + 1) * TT)
                    dve.tensor_scalar(m[:, i, 1], m[:, i, 0], 1.0 / D / scale ** 2, eps / scale ** 2, ALU.mult,
                                      ALU.add).then_inc(ms_ready, 1)
                for i, (x, gain, scale) in enumerate(items):
                    dve.wait_ge(sd_ready, i + 1)
                    step(dve.reciprocal(m[:, i, 3], m[:, i, 2]))
                    for tt in range(TT):
                        step(dve.tensor_tensor(x[:, tt], x[:, tt], bc(m[:, i, 3, tt], 2, D), ALU.mult))
                        step(dve.tensor_tensor(x[:, tt], x[:, tt], bc(gain, 1, H), ALU.mult))


def copy_evac(dst):
    def evac(dve, step, i, tt, bank):
        o = dst(i, tt)
        return dve.tensor_copy(o, bank[:, 0:o.shape[-1]])
    return evac


def rope_tables(k, cos, sin):
    nc, d = k.nc, k.d
    two_pi = [6.28125, 0.0019340515136718750, 1.2554228305816650e-06]
    two_pi.append(float(2 * np.pi - np.sum(np.array(two_pi, np.float64))))
    MAGIC = 12582912.0
    EDGE = 3.1415925
    with ExitStack() as s:
        pi32 = k.sb(s, "pos_i", [P, TT], I32)
        pos = k.sb(s, "pos_f", [P, TT])
        ang, turns, r, c, over = (k.sb(s, f"ang{i}", [P, TT, 16]) for i in range(5))
        pos_in, red, done, step_d = k.sem("pos_in"), k.sem("angle_red"), k.sem("angle_done"), k.sem("angle_step")
        with nc.Block() as block:
            @block.sync
            def _(sp):
                sp.dma_start(pi32[:], d["positions"]).then_inc(pos_in, 16)

            @block.vector
            def _(dve):
                step = Chain(dve, step_d)
                dve.wait_ge(pos_in, 16)
                step(dve.tensor_copy(pos[:], pi32[:]))
                step(dve.tensor_tensor(ang[:], bc(pos[:], 2, 16), bc(k.c("freq"), 1, TT), ALU.mult))
                step(dve.tensor_scalar(turns[:], ang[:], 1.0 / (2 * np.pi), MAGIC, ALU.mult, ALU.add))
                step(dve.tensor_scalar(turns[:], turns[:], -MAGIC, None, ALU.add))
                for i, part in enumerate(two_pi):
                    step(dve.scalar_tensor_tensor(r[:], turns[:], -part, r[:] if i else ang[:], ALU.mult, ALU.add))
                step(dve.tensor_scalar(c[:], r[:], float(np.pi / 2), None, ALU.add))
                step(dve.tensor_scalar(over[:], c[:], float(np.pi), -2 * float(np.pi), ALU.is_gt, ALU.mult))
                step(dve.tensor_tensor(c[:], c[:], over[:], ALU.add))
                step(dve.tensor_scalar(c[:], c[:], EDGE, -EDGE, ALU.min, ALU.max))
                dve.tensor_scalar(r[:], r[:], EDGE, -EDGE, ALU.min, ALU.max).then_inc(red, 1)

            @block.scalar
            def _(act):
                act.wait_ge(red, 1)
                act.activation(cos[:], c[:], ACT.Sin).then_inc(done, 1)
                act.activation(sin[:], r[:], ACT.Sin).then_inc(done, 1)


def latent_attention(k, ctx):
    nc, d = k.nc, k.d
    k.o_mla = k.sb(ctx, "o_mla", [P, TT, 512])
    with ExitStack() as s:
        kv = k.sb(s, "kv", [P, TT, 1024])
        qT, kT = (k.sb(s, n, [MLA_D, 8, SEQ]) for n in ("mla_qT", "mla_kT"))
        with ExitStack() as s1:
            nat = k.sb(s1, "mla_nat", [P, TT, MLA_COLS])
            kf = k.sb(s1, "mla_k", [P, TT, 8, MLA_D])
            cos, sin = k.sb(s1, "cos2", [P, TT, 16]), k.sb(s1, "sin2", [P, TT, 16])
            gains = k.sb(s1, "mla_gains", [P, 2 * MLA_D])
            project(k, "mla", k.xs_lhs, columns(d["w_mla"], 384),
                    copy_evac(lambda i, tt: nat[:, tt, 384 * i:min(384 * i + 384, MLA_COLS)]), ahead=2,
                    then=columns(d["w_ukv"], 512))
            rope_tables(k, cos, sin)
            ckv = lambda tt: nat[:, tt, 768:1024]
            rms_rows(k, "ckv", ckv, ckv, "norm_ckv", 256)
            with ExitStack() as s2:
                ckvT = [k.sb(s2, f"ckvT_{x}", [P, 2, SEQ], F32R) for x in ("hi", "lo")]
                transpose_split(k, "ckvT", lambda tt, b: nat[:, tt, 768 + b * P:768 + (b + 1) * P],
                                lambda b: tuple(x[:, b, :] for x in ckvT), 2)
                project(k, "ukv", lambda tt, c: tuple(x[:, c, tt * P:(tt + 1) * P] for x in ckvT),
                        columns(d["w_ukv"], 512), copy_evac(lambda i, tt: kv[:, tt, i * 512:(i + 1) * 512]), ahead=2,
                        then=dil_chunks(d, 0)[0:2])
            q4 = nat[:, :, 0:768].rearrange("p t (h e) -> p t h e", h=8)
            kv4 = kv[:].rearrange("p t (h e) -> p t h e", h=8)
            gains_in, built = k.sem("gains_in"), k.sem("k_built")
            with nc.Block() as block:
                @block.sync
                def _(sp):
                    a = VEC_AT["q_norm_mla"][0]
                    sp.dma_start(gains[:], k.d["vecs"][:, a:a + 2 * MLA_D]).then_inc(gains_in, 16)
                    sp.wait_ge(gains_in, 16)

                @block.vector
                def _(dve):
                    for tt in range(TT):
                        dve.tensor_copy(kf[:, tt, :, 0:64], kv4[:, tt, :, 0:64]).then_inc(built, 1)
                        dve.tensor_copy(kf[:, tt, :, 64:96], bc(nat[:, tt, 1024:1056], 1, 8)).then_inc(built, 1)
                    dve.wait_ge(built, 2 * TT)
            head_norms(k, "mlanorm", [(q4, gains[:, 0:MLA_D], MLA_D ** -0.5), (kf[:], gains[:, MLA_D:], 1.0)])
            with ExitStack() as s2:
                t = [k.sb(s2, f"rope_t{i}", [P, TT, 8, 16]) for i in range(4)]
                step_d = k.sem("rope2_step")
                with nc.Block() as block:
                    @block.vector
                    def _(dve):
                        step = Chain(dve, step_d)
                        C, S = bc(cos[:], 2, 8), bc(sin[:], 2, 8)
                        for x in (q4, kf[:]):
                            for tt in range(TT):
                                a, b = x[:, tt, :, 64:80], x[:, tt, :, 80:96]
                                for o, v, w in ((0, a, C), (1, b, S), (2, b, C), (3, a, S)):
                                    step(dve.tensor_tensor(t[o][:, tt], v, w[:, tt], ALU.mult))
                                step(dve.tensor_tensor(a, t[0][:, tt], t[1][:, tt], ALU.subtract))
                                step(dve.tensor_tensor(b, t[2][:, tt], t[3][:, tt], ALU.add))
            transpose_tiles(k, "mlaT", lambda tt, b: (q4 if b < 8 else kf[:])[:, tt, b % 8, :],
                            lambda b: (qT if b < 8 else kT)[:, b % 8, :], 16)
        units = []
        for tt in range(TT):
            w = (tt + 1) * P
            for h in range(8):
                units.append(dict(q=qT[:, h, tt * P:w], keys=kT[:, h, 0:w],
                                  masks=[(k.cb("ident_b"), k.cb("causal_b"), tt * P, w)],
                                  values=[kv[:, b, h * P + HD:(h + 1) * P] for b in range(tt + 1)]))
        attention(k, "mlaatt", units, lambda g: k.o_mla[:, g, :].rearrange("p (h d) -> p h d", h=8))


DIL_ORDER = (1, 2, 0)
FOLD = 4


def dil_chunks(d, turn):
    if turn == len(DIL):
        return columns(d["w_o_mla"], 512)
    return [columns(d["w_dil"], 512)[3 * i + DIL_ORDER[turn]] for i in range(3)]


def dilated_attention(k, ctx):
    nc, d = k.nc, k.d
    k.o_dil = k.sb(ctx, "o_dil", [P, TT, 512])
    NG, NU = len(DIL), TT * 8
    with ExitStack() as s:
        o_raw = k.sb(s, "o_raw", [P, NG, TT, 528])
        folded_out, folded_in = k.sem("folded_out"), k.sem("folded_in")
        gains = k.sb(s, "dil_gains", [P, 2 * NG * HD])
        gains_in = k.sem("dil_gains_in")
        with nc.Block() as block:
            @block.sync
            def _(sp):
                a = VEC_AT["q_norm_dil"][0]
                sp.dma_start(gains[:], k.d["vecs"][:, a:a + 2 * NG * HD]).then_inc(gains_in, 16)
                sp.wait_ge(gains_in, 16)
        dlo = k.cb("delta_b")
        dfold = k.cb("dfold_b").rearrange("p (g x) -> p g x", g=2)
        slope, slope4 = (k.cb(n).rearrange("p (h q) -> p h q", h=8) for n in ("slope_b", "slope4_b"))
        for turn, g in enumerate(DIL_ORDER):
            fold = DIL[g][1] > 1
            with ExitStack() as s1:
                nat = k.sb(s1, f"dil_nat{g}", [P, 3, TT, 512])
                qkT = k.sb(s1, f"dil_qkT{g}", [P, 8, SEQ])
                if fold:
                    lhs = lambda tt, c: tuple(x[:, c, tt::FOLD] for x in (k.xh, k.xl))
                else:
                    lhs = k.xs_lhs
                project(k, f"dil{g}", lhs, dil_chunks(d, turn), copy_evac(lambda i, tt: nat[:, i, tt, :]), ahead=2,
                        then=dil_chunks(d, turn + 1)[0:2])
                heads = [nat[:, i].rearrange("p t (h e) -> p t h e", h=8) for i in range(2)]
                head_norms(k, f"dilnorm{g}", [(heads[0], gains[:, g * HD:(g + 1) * HD], HD ** -0.5),
                                              (heads[1], gains[:, (NG + g) * HD:(NG + g + 1) * HD], 1.0)])
                transpose_tiles(k, f"dilT{g}", lambda tt, b: nat[:, b // 4, tt, (b % 4) * P:(b % 4 + 1) * P],
                                lambda b: qkT[:, b, :], 8)
                units = []
                for tt in range(TT):
                    lo = tt if fold else max(0, tt - 1)
                    for h in range(8):
                        r = slice(HD * (h % 2), HD * (h % 2) + HD)
                        if fold:
                            masks = [(slope4[:, h, :], dfold[:, g - 1, :], 0, P)]
                        else:
                            masks = [(slope[:, h, :], dlo[:, 2 * P - (tt + 1 - lo) * P:], 0, (tt + 1 - lo) * P)]
                        units.append(dict(q=qkT[r, h // 2, tt * P:(tt + 1) * P],
                                          keys=qkT[r, 4 + h // 2, lo * P:(tt + 1) * P], masks=masks,
                                          values=[nat[:, 2, b, h * HD:(h + 1) * HD] for b in range(lo, tt + 1)]))

                def store(sp, out_free, g=g):
                    rows = d["folded"][g - 1].rearrange("(l j) n -> l j n", j=FOLD)
                    for j in range(TT):
                        sp.wait_ge(out_free, j + 1)
                        sp.dma_start(rows[:, j, :], o_raw[:, g, j, :]).then_inc(folded_out, 16)

                attention(k, f"dilatt{g}", units, lambda t: o_raw[:, g, t, 0:512].rearrange("p (h d) -> p h d", h=8),
                          stats=[lambda j, a=a: o_raw[:, g, j // 8, a + j % 8:a + j % 8 + 1] for a in (512, 520)],
                          sync=store if fold else None)
        nmax, den = (o_raw[:, :, :, a:a + 8] for a in (512, 520))
        with ExitStack() as s1:
            diff, e, part = (k.sb(s1, f"merge_{n}", [P, NG, TT, 8]) for n in ("diff", "e", "part"))
            least, total, inv = (k.sb(s1, f"merge_{n}", [P, TT, 8]) for n in ("least", "total", "inv"))
            tmp = k.sb(s1, "merge_tmp", [P, 512])
            diff_ready, e_ready, step_d = k.sem("merge_diff"), k.sem("merge_e"), k.sem("merge_step")
            with nc.Block() as block:
                @block.sync
                def _(sp):
                    sp.wait_ge(folded_out, 2 * TT * 16)
                    for g in (1, 2):
                        sp.dma_start(o_raw[:, g], d["folded"][g - 1].rearrange("(t p) n -> p t n", p=P)).then_inc(
                            folded_in, 16)

                @block.scalar
                def _(act):
                    act.wait_ge(diff_ready, 1)
                    act.activation(e[:], diff[:], ACT.Exp).then_inc(e_ready, 1)

                @block.vector
                def _(dve):
                    step = Chain(dve, step_d)
                    dve.wait_ge(folded_in, 2 * 16)
                    step(dve.tensor_tensor(least[:], nmax[:, 0], nmax[:, 1], ALU.min))
                    step(dve.tensor_tensor(least[:], least[:], nmax[:, 2], ALU.min))
                    for g in range(NG):
                        ins = dve.tensor_tensor(diff[:, g], least[:], nmax[:, g], ALU.subtract)
                        if g < NG - 1:
                            step(ins)
                    ins.then_inc(diff_ready, 1)
                    dve.wait_ge(e_ready, 1)
                    for g in range(NG):
                        step(dve.tensor_tensor(part[:, g], e[:, g], den[:, g], ALU.mult))
                    step(dve.reduce_sum(total[:], part[:].rearrange("p g t h -> p t h g"), AX))
                    step(dve.reciprocal(inv[:], total[:]))
                    for g in range(NG):
                        step(dve.tensor_tensor(e[:, g], e[:, g], inv[:], ALU.mult))
                    for tt in range(TT):
                        o = k.o_dil[:, tt, :].rearrange("p (h d) -> p h d", h=8)
                        t3 = tmp[:].rearrange("p (h d) -> p h d", h=8)
                        for g in range(NG):
                            w = bc(e[:, g, tt, :], 2, HD)
                            x = o_raw[:, g, tt, 0:512].rearrange("p (h d) -> p h d", h=8)
                            step(dve.tensor_tensor(t3 if g else o, x, w, ALU.mult))
                            if g:
                                step(dve.tensor_tensor(o, o, t3, ALU.add))


def second_block(k):
    nc, d = k.nc, k.d
    k.recycle_semaphores()
    x = lambda tt: k.x1[:, tt, :]
    stage = ExitStack()
    k.weight_buffers(stage, "block2")
    with ExitStack() as s:
        h_nat = k.sb(s, "h_nat", [P, TT, DM])
        rms_rows(k, "rms1", x, lambda tt: h_nat[:, tt, :], "norm_attn", then=columns(d["w_mla"], 384, 2))
        transpose_split(k, "hT", lambda tt, b: h_nat[:, tt, b * P:(b + 1) * P], lambda b: (k.xh[:, b, :], k.xl[:, b, :]), KD)
    with ExitStack() as s:
        latent_attention(k, s)
        k.recycle_semaphores()
        dilated_attention(k, s)
        k.recycle_semaphores()
        a = k.sb(s, "branches", [P, 2, TT, DM])
        with ExitStack() as s1:
            oT = [k.sb(s1, f"oT_{x}", [P, 8, SEQ], F32R) for x in ("hi", "lo")]
            transpose_split(k, "oT", lambda tt, b: (k.o_mla if b < 4 else k.o_dil)[:, tt, (b % 4) * P:(b % 4 + 1) * P],
                            lambda b: tuple(x[:, b, :] for x in oT), 8)
            follow = [columns(d["w_o_dil"], 512), columns(d["w_gates"], 512)[0:2]]
            for i, n in enumerate(("w_o_mla", "w_o_dil")):
                project(k, n, lambda tt, c: tuple(x[:, 4 * i + c, tt * P:(tt + 1) * P] for x in oT), columns(d[n], 512),
                        copy_evac(lambda j, tt: a[:, i, tt, j * 512:(j + 1) * 512]), ahead=2, then=follow[i])
        with ExitStack() as s1:
            pre = k.sb(s1, "gate_pre", [P, TT, 2 * DM])
            bg = k.sb(s1, "gate_bias", [P, 2 * DM])
            bg_in = k.sem("gate_bias_in")
            with nc.Block() as block:
                @block.sync
                def _(sp):
                    sp.dma_start(bg[:], k.vec("b_gate")).then_inc(bg_in, 16)
                    sp.wait_ge(bg_in, 16)

            def add_bias(dve, step, i, tt, bank):
                return dve.tensor_tensor(pre[:, tt, i * 512:(i + 1) * 512], bank[:], bg[:, i * 512:(i + 1) * 512], ALU.add)

            project(k, "gates", k.xs_lhs, columns(d["w_gates"], 512), add_bias, ahead=2,
                    then=columns(d["w_out2"], 512))
            sig, step_d = k.sem("gate_sig"), k.sem("gate_step")
            with nc.Block() as block:
                @block.scalar
                def _(act):
                    for tt in range(TT):
                        act.activation(pre[:, tt, :], pre[:, tt, :], ACT.Sigmoid).then_inc(sig, 1)

                @block.vector
                def _(dve):
                    step = Chain(dve, step_d)
                    for tt in range(TT):
                        dve.wait_ge(sig, tt + 1)
                        for i in range(2):
                            step(dve.tensor_tensor(a[:, i, tt, :], a[:, i, tt, :], pre[:, tt, i * DM:(i + 1) * DM],
                                                   ALU.mult))
                        step(dve.tensor_tensor(a[:, 0, tt, :], a[:, 0, tt, :], a[:, 1, tt, :], ALU.add))
        transpose_split(k, "merT", lambda tt, b: a[:, 0, tt, b * P:(b + 1) * P], lambda b: (k.xh[:, b, :], k.xl[:, b, :]), KD)

        def add_out(dve, step, i, tt, bank):
            o = k.x1[:, tt, i * 512:(i + 1) * 512]
            return dve.tensor_tensor(o, o, bank[:], ALU.add)

        project(k, "out2", k.xs_lhs, columns(d["w_out2"], 512), add_out, ahead=2)
    stage.close()
    k.recycle_semaphores()
    with ExitStack() as s:
        h2 = k.sb(s, "h2_nat", [P, TT, DM])
        rms_rows(k, "rms2", x, lambda tt: h2[:, tt, :], "norm_ffn")
        transpose_split(k, "h2T", lambda tt, b: h2[:, tt, b * P:(b + 1) * P], lambda b: (k.xh[:, b, :], k.xl[:, b, :]), KD)
        route(k, "r2", E2, G2, S2, "b2", d["w_route2"], s)
        experts(k, "e2", E2, S2, k.gather_sems[2:4], d["rows"], d["gu2"], d["dn2"], d["slots"][0:SLOTS2, :], lambda tt: h2[:, tt, :])
        combine(k, "c2", d["slots"][0:SLOTS2, :], k.x1, 1.0, out=d["out"])


def first_block(k):
    nc, d = k.nc, k.d
    with ExitStack() as s:
        load_block1(k, s)
        k.weight_buffers(s, "block1")
        project1(k, s)
        select_keys(k, s)
        state_space(k, s)
        att = k.sb(s, "att1", [P, TT, 512])
        units = []
        for tt in range(TT):
            w = (tt + 1) * P
            for h in range(H1):
                r = slice(HD * (h % 2), HD * (h % 2) + HD)
                units.append(dict(q=k.ropeT[r, h // 2, tt * P:w], keys=k.ropeT[r, 4, 0:w],
                                  masks=[(k.cb("ident_b"), k.key_bias[:, tt, 0:w], 0, w)],
                                  values=[k.v[:, b, 0:HD] for b in range(tt + 1)]))
        attention(k, "dsa", units, lambda g: att[:, g, :].rearrange("p (h d) -> p h d", h=8))
        cat = lambda tt, b: att[:, tt, b * P:(b + 1) * P] if b < 4 else k.y[:, tt, (b - 4) * P:(b - 3) * P]
        transpose_split(k, "mix1", cat, lambda b: (k.xh[:, b, :], k.xl[:, b, :]), KD)

        def add_mixed(dve, step, i, tt, bank):
            x = k.x1[:, tt, i * 512:(i + 1) * 512]
            return dve.scalar_tensor_tensor(x, x, ALPHA, bank[:], ALU.mult, ALU.add)

        project(k, "out1", k.xs_lhs, columns(d["w_out"], 512), add_mixed, ahead=2)
    layer_norm(k, "ln1", k.x1, "ln1_g", "ln1_b")
    k.recycle_semaphores()
    transpose_split(k, "x1T", lambda tt, b: k.x1[:, tt, b * P:(b + 1) * P], lambda b: (k.xh[:, b, :], k.xl[:, b, :]), KD)
    with ExitStack() as s:
        route(k, "r1", E1, G1, S1, "b1", d["w_route1"], s)
        experts(k, "e1", E1, S1, k.gather_sems[0:2], d["rows"], d["gu1"], d["dn1"], d["slots"][0:SLOTS1, :], lambda tt: k.x1[:, tt, :])
        combine(k, "c1", d["slots"][0:SLOTS1, :], k.x1, ALPHA)
    layer_norm(k, "ln2", k.x1, "ln2_g", "ln2_b")


def program(nc, d):
    with ExitStack() as ctx:
        k = Core(nc, ctx, d)
        first_block(k)
        second_block(k)


def lay_out(a):
    f = np.float32
    A = {n: np.asarray(v) for n, v in a.items()}
    L = {n: (v[0] if v.ndim > 1 or n in () else v) for n, v in A.items() if n not in ("x", "positions_2")}
    o = {}
    x = A["x"][0]
    o["x_nat"] = x.reshape(TT, P, DM).transpose(1, 0, 2)
    o["xT"] = x.T.reshape(KD, P, SEQ).transpose(1, 0, 2)
    w = L["w_in"]
    rows = lambda m: m.reshape(-1, P, m.shape[1]).transpose(1, 0, 2)
    q, kk, vv, iq, ik, iw, z, xbc, dt = np.split(w, np.cumsum([512, 64, 64, 256, 64, 4, 512, 768]), axis=1)
    cols = np.concatenate([q, kk, kk, iq, ik, ik, xbc], axis=1)
    o["w_in_t"] = cols.reshape(KD, P, -1, P).transpose(2, 1, 0, 3).reshape(-1, P, KD * P)
    o["w_in_n"] = rows(np.concatenate([z, vv, iw, dt], axis=1))
    cw = np.concatenate([L["conv_w"], L["conv_b"][None]], 0)
    o["convw"] = cw.reshape(5, 6, P).transpose(2, 1, 0)
    o["w_out"] = rows(L["w_out"])
    o["w_route1"] = rows(np.concatenate([L["w_route_group"], L["w_route_expert"]], 1))

    def expert(wg, wu, wd):
        E = wg.shape[0]
        gu = np.concatenate([wg, wu], 2).reshape(E, KD, P, 2 * FF).transpose(0, 2, 1, 3).reshape(E, P, -1)
        return gu, wd.reshape(E, 2, P, DM).transpose(0, 2, 1, 3).reshape(E, P, -1)

    o["gu1"], o["dn1"] = expert(L["w_gate"], L["w_up"], L["w_down"])
    o["gu2"], o["dn2"] = expert(L["w_gate_2"], L["w_up_2"], L["w_down_2"])
    v = {"b1": np.concatenate([L["b_route_group"], L["b_route_expert"]]),
         "b2": np.concatenate([L["b_router_group_2"], L["b_router_expert_2"]])}
    for n, width in VECS:
        if n not in v:
            v[n] = L[n] if n in L else L[n + "_2"]
    flat = np.concatenate([np.asarray(v[n]).reshape(-1) for n, _ in VECS])
    o["vecs"] = np.broadcast_to(flat[None], (P, NVEC))
    w2 = L["w_in_2"]
    o["w_mla"] = rows(w2[:, 0:MLA_COLS])
    o["w_dil"] = rows(w2[:, MLA_COLS:MLA_COLS + 9 * 512])
    o["w_gates"] = rows(w2[:, MLA_COLS + 9 * 512:])
    o["w_ukv"] = rows(L["w_ukv_2"])
    o["w_o_mla"], o["w_o_dil"], o["w_out2"] = rows(L["w_o_mla_2"]), rows(L["w_o_dil_2"]), rows(L["w_out_2"])
    o["w_route2"] = rows(np.concatenate([L["w_router_group_2"], L["w_router_expert_2"]], 1))
    o["positions"] = A["positions_2"][0].reshape(TT, P).T.astype(np.int32)
    o["consts"], o["consts_b"] = constants()
    return {n: np.ascontiguousarray(m) for n, m in o.items()}


def kernel(**inputs):
    import concourse.bacc as bacc
    from concourse.bass_utils import run_bass_kernel_spmd
    nc = bacc.Bacc("TRN2", target_bir_lowering=False, num_devices=1)
    arrays = {f"in_{n}": m for n, m in lay_out(inputs).items()}
    d = {n[3:]: nc.dram_tensor(n, m.shape, mybir.dt.from_np(m.dtype), kind="ExternalInput").ap()
         for n, m in arrays.items()}
    d["consts_b"] = d["consts_b"].bitcast(BF16)
    d["rows"] = nc.dram_tensor("token_rows", (SEQ, DM), F32, kind="Internal").ap()
    d["slots"] = nc.dram_tensor("slot_rows", (max(SLOTS1, SLOTS2), DM), F32, kind="Internal").ap()
    d["folded"] = nc.dram_tensor("folded_rows", (2, SEQ, 528), F32, kind="Internal").ap()
    d["out"] = nc.dram_tensor("out", (SEQ, DM), F32, kind="ExternalOutput").ap()
    program(nc, d)
    r = run_bass_kernel_spmd(nc, [arrays], core_ids=[0])
    return r.results[0]["out"].reshape(1, SEQ, DM)
```

```python
from contextlib import ExitStack, nullcontext

import numpy as np
import concourse.bass as bass
from concourse import mybir

F32 = mybir.dt.float32
BF16 = mybir.dt.bfloat16
F32R = mybir.dt.float32r
I32 = mybir.dt.int32
U32 = mybir.dt.uint32
ALU = mybir.AluOpType
ACT = mybir.ActivationFunctionType
AX = mybir.AxisListType.X

P = 128
SEQ = 512
TT = SEQ // P
DM = 1024
KD = DM // P
HD = 64
NEG = -1.0e30
H1 = 8
IDX_HEADS = 4
INDEXER_SCALE = (IDX_HEADS ** -0.5) * (HD ** -0.5)
TOPK = min(256, SEQ // 4)
SSD_HEADS = 8
CONV_W = 4
ALPHA = 2.0 ** 0.25
LN_EPS = 1e-5
EPS = 1e-6
MLA_D = 96
MLA_COLS = 8 * MLA_D + 256 + 32
DIL = ((128, 1), (512, 4), (2048, 16))
FF = 256
E1, G1 = 16, 4
E2, G2 = 32, 4


S1, S2 = 96, 64
W_SLOTS = 4


def most_tiles(experts, slots):
    return experts + 2 * SEQ // slots


SLOTS1, SLOTS2 = S1 * most_tiles(E1, S1), S2 * most_tiles(E2, S2)

VECS = [("dt_bias", 8), ("a_log", 8), ("d_skip", 8), ("ssd_norm_w", 512), ("ln1_g", DM), ("ln1_b", DM),
        ("b1", G1 + E1), ("ln2_g", DM), ("ln2_b", DM), ("norm_attn", DM), ("norm_ckv", 256),
        ("q_norm_mla", 96), ("k_norm_mla", 96), ("q_norm_dil", 192), ("k_norm_dil", 192),
        ("b_gate", 2 * DM), ("norm_ffn", DM), ("b2", G2 + E2)]
VEC_AT = {}
_at = 0
for _n, _w in VECS:
    VEC_AT[_n] = (_at, _w)
    _at += _w
NVEC = _at

CONSTS = [("ident", 128), ("upto", 128), ("after", 128), ("before", 128), ("ones", 128), ("rot", 128),
          ("cos", SEQ), ("sin", SEQ), ("iota", 128), ("down", 128), ("tok", TT), ("freq", 16)]
CONST_AT = {}
_at = 0
for _n, _w in CONSTS:
    CONST_AT[_n] = (_at, _w)
    _at += _w
NCONST = _at
CONSTS_B = [("ident_b", 128), ("causal_b", 128), ("slope_b", 8 * 128), ("slope4_b", 8 * 128),
            ("delta_b", 256), ("dfold_b", 2 * 128)]
CONST_B_AT = {}
_at = 0
for _n, _w in CONSTS_B:
    CONST_B_AT[_n] = (_at, _w)
    _at += _w
NCONST_B = _at


def constants():
    k = np.arange(P)
    c = {}
    c["ident"] = np.eye(P)
    c["upto"] = k[:, None] <= k[None, :]
    c["after"] = k[:, None] > k[None, :]
    c["before"] = k[:, None] < k[None, :]
    c["ones"] = np.ones((P, P))
    rot = np.zeros((P, P))
    for m in range(P):
        if m % HD < HD // 2:
            rot[m + HD // 2, m] = -1
        else:
            rot[m - HD // 2, m] = 1
    c["rot"] = rot
    inv = (np.float32(10000.0) ** (-np.arange(0, HD, 2, dtype=np.float32) / np.float32(HD))).astype(np.float32)
    ang = np.arange(SEQ, dtype=np.float32)[:, None] * inv[None, :]
    c["cos"] = np.tile(np.cos(ang).T, (4, 1))
    c["sin"] = np.tile(np.sin(ang).T, (4, 1))
    c["iota"] = np.broadcast_to(k[None, :], (P, P))
    c["down"] = np.broadcast_to(P - k[None, :], (P, P))
    c["tok"] = k[:, None] + P * np.arange(TT)[None, :]
    c["freq"] = np.broadcast_to(
        (np.float32(10000.0) ** (-np.arange(16, dtype=np.float32) / np.float32(16))).astype(np.float32)[None], (P, 16))
    f = np.concatenate([np.asarray(c[n], np.float32).reshape(P, w) for n, w in CONSTS], 1)
    b = {}
    b["ident_b"] = np.eye(P)
    b["causal_b"] = np.where(k[None, :] <= k[:, None], 0.0, NEG)
    b["slope_b"] = np.stack([np.eye(P) * 2.0 ** -(h + 1) for h in range(8)], 1)
    b["slope4_b"] = 4 * b["slope_b"]
    delta = k[:, None] + P - np.arange(2 * P)[None, :]
    b["delta_b"] = np.where((delta >= 0) & (delta <= DIL[0][0]), -delta, NEG)
    own = k[:, None] - k[None, :]
    b["dfold_b"] = np.stack([np.where((own >= 0) & (own % (dil // 4) == 0), -own, NEG) for _, dil in DIL[1:]], 1)
    fb = np.concatenate([np.asarray(b[n], np.float32).reshape(P, w) for n, w in CONSTS_B], 1)
    return np.ascontiguousarray(f), (fb.view(np.uint32) >> 16).astype(np.uint16)


class Chain:

    def __init__(self, eng, sem, start=0):
        self.eng, self.sem, self.n = eng, sem, start

    def __call__(self, ins):
        ins.then_inc(self.sem, 1)
        self.n = self.n + 1
        self.eng.wait_ge(self.sem, self.n)


class Core:

    def __init__(self, nc, ctx, d):
        self.nc, self.ctx, self.d = nc, ctx, d
        self.uid = 0
        self.held = ExitStack()
        self.held_sems = []
        self.gathered = [0] * (4 + 2 * TT)
        self.w_in = [ctx.enter_context(nc.semaphore(f"weights_in{i}")) for i in range(2)]
        self.chunks_loaded = 0
        self.gather_sems = [ctx.enter_context(nc.semaphore(f"gathered{i}")) for i in range(4 + 2 * TT)]

    def sem(self, name):
        self.uid += 1
        sem = self.held.enter_context(self.nc.semaphore(f"{name}_{self.uid}"))
        self.held_sems.append(sem)
        return sem

    def recycle_semaphores(self):
        sems = self.held_sems
        with self.nc.Block() as block:
            @block.gpsimd
            def _(pool):
                for sem in sems:
                    pool.sem_clear(sem)
        self.held.close()
        self.held, self.held_sems = ExitStack(), []

    def sb(self, ctx, name, shape, dt=F32):
        return ctx.enter_context(self.nc.sbuf_tensor(name, shape, dt))

    def ps(self, ctx, name, shape=(P, 512), dt=F32):
        return ctx.enter_context(self.nc.psum_tensor(name, list(shape), dt))

    def weight_buffers(self, ctx, name):
        self.w = self.sb(ctx, f"{name}_w", [P, 2, KD, 512])
        self.w_ring = [self.sb(ctx, f"{name}_w_{x}", [P, 4, 512], F32R) for x in ("hi", "lo")]

    def load_chunk(self, sp, chunk):
        slot = self.chunks_loaded % 2
        kd, width = chunk.shape[1:]
        sp.dma_start(self.w[:, slot, 0:kd, 0:width], chunk).then_inc(self.w_in[slot], 16)
        self.chunks_loaded += 1

    def xs_lhs(self, tt, c):
        return tuple(x[:, c, tt * P:(tt + 1) * P] for x in (self.xh, self.xl))

    def c(self, name):
        a, w = CONST_AT[name]
        return self.consts[:, a:a + w]

    def cb(self, name):
        a, w = CONST_B_AT[name]
        return self.consts_b[:, a:a + w]

    def vec(self, name):
        a, w = VEC_AT[name]
        return self.d["vecs"][:, a:a + w]


def bc(ap, axis, n):
    shape = list(ap.shape)
    shape.insert(axis, n)
    return ap.unsqueeze(axis).broadcast_to(shape)


def three_passes(pe, out, lhs, rhs, first, last):
    pe.matmul(out, lhs[0], rhs[0], start=first, stop=False)
    pe.matmul(out, lhs[0], rhs[1], start=False, stop=False)
    return pe.matmul(out, lhs[1], rhs[0], start=False, stop=last)


def transpose_split(k, name, src, dst, blocks):
    nc = k.nc
    with ExitStack() as s:
        bank = [k.ps(s, f"{name}_bank{i}") for i in range(4)]
        turned, hi_ready, lo_ready = (k.sem(f"{name}_{n}") for n in ("turned", "hi", "lo"))
        with nc.Block() as block:
            @block.tensor
            def _(pe):
                for b in range(blocks):
                    if b >= 4:
                        pe.wait_ge(lo_ready, b - 3)
                    for tt in range(TT):
                        a = src(tt, b)
                        ins = pe.transpose(bank[b % 4][0:a.shape[1], tt * P:(tt + 1) * P], a, k.c("ident"))
                    ins.then_inc(turned, 1)

            @block.scalar
            def _(act):
                for b in range(blocks):
                    act.wait_ge(turned, b + 1)
                    hi, lo = dst(b)
                    act.activation(hi, bank[b % 4][0:hi.shape[0], :], ACT.Copy).then_inc(hi_ready, 1)

            @block.vector
            def _(dve):
                for b in range(blocks):
                    hi, lo = dst(b)
                    dve.wait_ge(hi_ready, b + 1)
                    dve.tensor_tensor(lo, bank[b % 4][0:hi.shape[0], :], hi.bitcast(F32),
                                      ALU.subtract).then_inc(lo_ready, 1)


def transpose_tiles(k, name, src, dst, blocks):
    nc = k.nc
    with ExitStack() as s:
        bank = k.ps(s, f"{name}_bank", (P, 4, 512))
        turned = k.sem(f"{name}_turned")
        copied = [k.sem(f"{name}_copied_{e}") for e in ("vector", "scalar")]
        with nc.Block() as block:
            @block.tensor
            def _(pe):
                for b in range(blocks):
                    if b >= 4:
                        pe.wait_ge(copied[b % 2], (b - 4) // 2 + 1)
                    for tt in range(TT):
                        a = src(tt, b)
                        ins = pe.transpose(bank[0:a.shape[1], b % 4, tt * P:(tt + 1) * P], a, k.c("ident"))
                    ins.then_inc(turned, 1)

            @block.vector
            def _(dve):
                for b in range(0, blocks, 2):
                    dve.wait_ge(turned, b + 1)
                    w = dst(b).shape[0]
                    dve.tensor_copy(dst(b), bank[0:w, b % 4, :]).then_inc(copied[0], 1)

            @block.scalar
            def _(act):
                for b in range(1, blocks, 2):
                    act.wait_ge(turned, b + 1)
                    w = dst(b).shape[0]
                    act.activation(dst(b), bank[0:w, b % 4, :], ACT.Copy).then_inc(copied[1], 1)


def columns(w, width, count=None):
    n = w.shape[2]
    return [w[:, :, i:min(i + width, n)] for i in range(0, n, width)][:count]


FEW = HD + IDX_HEADS + SSD_HEADS
CONV_BLOCKS = 6
ROPE_BLOCKS = 8


def place_block1(k, ctx):
    k.consts = k.sb(k.ctx, "consts", [P, NCONST])
    k.consts_b = k.sb(k.ctx, "consts_b", [P, NCONST_B], BF16)
    k.x1 = k.sb(k.ctx, "x_res", [P, TT, DM])
    k.xh, k.xl = (k.sb(k.ctx, n, [P, KD, SEQ], F32R) for n in ("xT_hi", "xT_lo"))
    k.row_stats = k.sb(k.ctx, "row_stats", [P, TT, 2, 6])
    k.v = k.sb(ctx, "v1", [P, TT, FEW])
    k.ropeT = k.sb(ctx, "ropeT", [P, ROPE_BLOCKS, SEQ])
    k.sz = k.sb(ctx, "z", [P, TT, 512])
    k.xbcT = k.sb(ctx, "xbcT", [P, CONV_BLOCKS, SEQ])
    k.convw = k.sb(ctx, "convw", [P, CONV_BLOCKS, CONV_W + 1])
    k.blank = k.sb(ctx, "blank", [P, 256])


def project1(k, ctx):
    nc, d = k.nc, k.d
    NB = ROPE_BLOCKS + CONV_BLOCKS + 1
    with ExitStack() as s:
        xT = k.sb(s, "xT", [P, KD, SEQ])
        w_t = k.sb(s, "w_t", [P, 2, KD * P])
        w_h, w_l = (k.sb(s, n, [P, 2, KD * P], F32R) for n in ("w_t_hi", "w_t_lo"))
        raw = k.sb(s, "raw", [P, 2, SEQ])
        padded = k.sb(s, "padded", [P, 2, SEQ + CONV_W - 1])
        part = k.sb(s, "part", [P, 2, SEQ])
        acc = k.sb(s, "conv_acc", [P, 2, SEQ])
        main = [k.ps(s, f"proj_main{i}") for i in range(4)]
        turned = [k.ps(s, f"proj_rot{i}") for i in range(2)]
        consts_in, small_in = k.sem("consts_in"), k.sem("small_in")
        x_in = [k.sem(f"x_in{i}") for i in range(4)]
        wt_in = [k.sem(f"wt_in{i}") for i in range(2)]
        xh_ready, xl_ready, wh_ready, wl_ready = k.sem("xh"), k.sem("xl"), k.sem("wh"), k.sem("wl")
        proj_done, main_free = k.sem("proj_done"), k.sem("main_free")
        raw_ready, rot_done, roped = k.sem("raw_ready"), k.sem("rot_done"), k.sem("roped")
        pad_zero, conv_done, conv_silu, dve_step = (k.sem("pad_zero"), k.sem("conv_done"), k.sem("conv_silu"),
                                                    k.sem("dve_step"))
        x_nat_in = k.sem("x_nat_in")

        with nc.Block() as block:
            @block.sync
            def _(sp):
                sp.dma_start(w_t[:, 0], d["w_in_t"][0]).then_inc(wt_in[0], 16)
                for c in range(4):
                    sp.dma_start(xT[:, 2 * c:2 * c + 2], d["xT"][:, 2 * c:2 * c + 2]).then_inc(x_in[c], 16)
                sp.dma_start(w_t[:, 1], d["w_in_t"][1]).then_inc(wt_in[1], 16)
                sp.dma_start(k.consts[:], d["consts"]).then_inc(consts_in, 16)
                sp.dma_start(k.convw[:], d["convw"]).then_inc(small_in, 16)
                sp.dma_start(k.consts_b[:], d["consts_b"]).then_inc(small_in, 16)
                for b in range(2, NB):
                    sp.wait_ge(wl_ready, b - 1)
                    sp.dma_start(w_t[:, b % 2], d["w_in_t"][b]).then_inc(wt_in[b % 2], 16)
                k.load_chunk(sp, d["w_z"])
                sp.dma_start(k.x1[:], d["x_nat"]).then_inc(x_nat_in, 16)
                sp.wait_ge(x_nat_in, 16)
                sp.wait_ge(small_in, 32)

            @block.tensor
            def _(pe):
                for b in range(NB + 1):
                    if b < NB:
                        pe.wait_ge(wl_ready, b + 1)
                        if b >= 4:
                            pe.wait_ge(main_free, b - 3)
                        for c in range(KD):
                            if b == 0:
                                pe.wait_ge(xl_ready, c + 1)
                            f = slice(c * P, (c + 1) * P)
                            ins = three_passes(pe, main[b % 4][:], (w_h[:, b % 2, f], w_l[:, b % 2, f]),
                                               (k.xh[:, c, :], k.xl[:, c, :]), c == 0, c == KD - 1)
                        ins.then_inc(proj_done, 1)
                    r = b - 1
                    if 0 <= r < ROPE_BLOCKS:
                        if r == 0:
                            pe.wait_ge(consts_in, 16)
                        pe.wait_ge(raw_ready, r + 1)
                        if r >= 2:
                            pe.wait_ge(roped, r - 1)
                        pe.matmul(turned[r % 2][:], k.c("rot"), raw[:, r % 2, :], start=True,
                                  stop=True).then_inc(rot_done, 1)
                pe.wait_ge(raw_ready, ROPE_BLOCKS + 1)
                pe.wait_ge(roped, ROPE_BLOCKS)
                for tt in range(TT):
                    ins = pe.matmul(turned[0][:, tt * FEW:(tt + 1) * FEW], raw[0:FEW, 0, tt * P:(tt + 1) * P],
                                    k.c("ident")[0:FEW, 0:FEW], start=True, stop=True)
                ins.then_inc(rot_done, 1)

            @block.gpsimd
            def _(pool):
                def split_w(b):
                    pool.wait_ge(wh_ready, b + 1)
                    pool.tensor_tensor(w_l[:, b % 2], w_t[:, b % 2], w_h[:, b % 2].bitcast(F32),
                                       ALU.subtract).then_inc(wl_ready, 1)

                split_w(0)
                for c in range(KD):
                    pool.wait_ge(xh_ready, c + 1)
                    pool.tensor_tensor(k.xl[:, c], xT[:, c], k.xh[:, c].bitcast(F32), ALU.subtract).then_inc(xl_ready, 1)
                for b in range(1, NB):
                    split_w(b)

            @block.scalar
            def _(act):
                def split_w(b):
                    act.wait_ge(wt_in[b % 2], 16 * (b // 2 + 1))
                    if b >= 2:
                        act.wait_ge(proj_done, b - 1)
                    act.activation(w_h[:, b % 2], w_t[:, b % 2], ACT.Copy).then_inc(wh_ready, 1)

                def silu_conv(r):
                    act.wait_ge(conv_done, r + 1)
                    act.activation(k.xbcT[:, r, :], acc[:, r % 2, :], ACT.Silu,
                                   bias=k.convw[:, r, CONV_W:CONV_W + 1]).then_inc(conv_silu, 1)

                split_w(0)
                for c in range(KD):
                    act.wait_ge(x_in[c // 2], 16)
                    act.activation(k.xh[:, c], xT[:, c], ACT.Copy).then_inc(xh_ready, 1)
                split_w(1)
                act.wait_ge(pad_zero, 1)
                for b in range(NB):
                    act.wait_ge(proj_done, b + 1)
                    if b + 2 < NB:
                        split_w(b + 2)
                    if b < ROPE_BLOCKS:
                        if b >= 2:
                            act.wait_ge(roped, b - 1)
                        act.activation(raw[:, b % 2, :], main[b % 4][:], ACT.Copy,
                                       scale=(HD ** -0.5 if b < 4 else 1.0)).then_inc(raw_ready, 1)
                        act.wait_ge(raw_ready, b + 1)
                        act.sem_inc(main_free, 1)
                    elif b < NB - 1:
                        r = b - ROPE_BLOCKS
                        if r >= 2:
                            act.wait_ge(conv_done, r - 1)
                        act.activation(padded[:, r % 2, CONV_W - 1:], main[b % 4][:],
                                       ACT.Copy).then_inc(main_free, 1)
                        if r >= 1:
                            silu_conv(r - 1)
                    else:
                        act.wait_ge(roped, ROPE_BLOCKS)
                        act.activation(raw[0:FEW, 0, :], main[b % 4][0:FEW, :], ACT.Copy).then_inc(raw_ready, 1)
                silu_conv(CONV_BLOCKS - 1)

            @block.vector
            def _(dve):
                step = Chain(dve, dve_step)
                dve.memset(k.blank[:], 0.0)
                dve.memset(padded[:, :, 0:CONV_W - 1], 0.0).then_inc(pad_zero, 1)
                dve.wait_ge(consts_in, 16)
                for r in range(ROPE_BLOCKS):
                    dve.wait_ge(raw_ready, r + 1)
                    dve.tensor_tensor(part[:, 0, :], raw[:, r % 2, :], k.c("cos"), ALU.mult).then_inc(dve_step, 1)
                    dve.wait_ge(rot_done, r + 1)
                    dve.tensor_tensor(part[:, 1, :], turned[r % 2][:], k.c("sin"), ALU.mult).then_inc(dve_step, 1)
                    step.n += 2
                    dve.wait_ge(dve_step, step.n)
                    dve.tensor_tensor(k.ropeT[:, r, :], part[:, 0, :], part[:, 1, :], ALU.add).then_inc(roped, 1)
                    dve.wait_ge(roped, r + 1)
                dve.wait_ge(small_in, 32)
                for r in range(CONV_BLOCKS):
                    dve.wait_ge(main_free, ROPE_BLOCKS + r + 1)
                    if r >= 2:
                        dve.wait_ge(conv_silu, r - 1)
                    a, u = acc[:, r % 2, :], padded[:, r % 2, :]
                    step(dve.tensor_scalar(a, u[:, 0:SEQ], k.convw[:, r, 0:1], None, ALU.mult))
                    for j in range(1, CONV_W):
                        ins = dve.scalar_tensor_tensor(a, u[:, j:j + SEQ], k.convw[:, r, j:j + 1], a,
                                                       ALU.mult, ALU.add)
                        if j < CONV_W - 1:
                            step(ins)
                    ins.then_inc(conv_done, 1)
                dve.wait_ge(rot_done, ROPE_BLOCKS + 1)
                step(dve.tensor_copy(k.v[:], turned[0][:, 0:TT * FEW].rearrange("p (t n) -> p t n", t=TT)))


def select_keys(k, ctx):
    nc, d = k.nc, k.d
    TAKEN, FLOOR = -3.0e38, -1.0e35
    k.key_bias = k.sb(ctx, "key_bias", [P, TT, SEQ], BF16)
    tiles = [tt for tt in range(TT) if (tt + 1) * P > TOPK]
    best = k.sb(ctx, "best", [P, TT, 8])
    last_score = k.sb(ctx, "last_score", [P, SEQ])
    s = ExitStack()
    scores = {tt: last_score if tt == TT - 1 else k.sb(s, f"score{tt}", [P, (tt + 1) * P]) for tt in tiles}
    with ExitStack() as s1:
        relu = k.sb(s1, "relu", [P, 4, SEQ])
        iw = k.sb(s1, "iw", [P, TT, IDX_HEADS])
        bank = [k.ps(s1, f"idx_bank{i}") for i in range(4)]
        dots, relued, used, dve_step = (k.sem("idx_dots"), k.sem("idx_relued"), k.sem("idx_used"),
                                        k.sem("idx_step"))
        units = [(tt, h) for tt in tiles for h in range(IDX_HEADS)]
        with nc.Block() as block:
            @block.tensor
            def _(pe):
                for u, (tt, h) in enumerate(units):
                    if u >= 4:
                        pe.wait_ge(relued, u - 3)
                    lo = HD * (h % 2)
                    pe.matmul(bank[u % 4][:, 0:(tt + 1) * P],
                              k.ropeT[lo:lo + HD, 5 + h // 2, tt * P:(tt + 1) * P],
                              k.ropeT[lo:lo + HD, 7, 0:(tt + 1) * P], start=True, stop=True).then_inc(dots, 1)

            @block.scalar
            def _(act):
                for u, (tt, h) in enumerate(units):
                    act.wait_ge(dots, u + 1)
                    if u >= 4:
                        act.wait_ge(used, u - 3)
                    w = (tt + 1) * P
                    act.activation(relu[:, u % 4, 0:w], bank[u % 4][:, 0:w], ACT.Relu).then_inc(relued, 1)

            @block.vector
            def _(dve):
                step = Chain(dve, dve_step)
                step(dve.tensor_scalar(iw[:], k.v[:, :, 64:64 + IDX_HEADS], INDEXER_SCALE, None, ALU.mult))
                for tt in range(TT):
                    if tt not in tiles:
                        if tt:
                            step(dve.memset(k.key_bias[:, tt, 0:tt * P], 0.0))
                        step(dve.tensor_copy(k.key_bias[:, tt, tt * P:(tt + 1) * P], k.cb("causal_b")))
                for u, (tt, h) in enumerate(units):
                    w = (tt + 1) * P
                    dve.wait_ge(relued, u + 1)
                    sc, r = scores[tt][:], relu[:, u % 4, 0:w]
                    if h == 0:
                        ins = dve.tensor_scalar(sc, r, iw[:, tt, h:h + 1], None, ALU.mult)
                    else:
                        ins = dve.scalar_tensor_tensor(sc, r, iw[:, tt, h:h + 1], sc, ALU.mult, ALU.add)
                    ins.then_inc(used, 1)
                    dve.wait_ge(used, u + 1)
                    if h == IDX_HEADS - 1:
                        diag = scores[tt][:, tt * P:w]
                        step(dve.tensor_tensor(diag, diag, k.cb("causal_b"), ALU.add))
    ROUNDS = TOPK // 8

    def one_round(dve, step, tiles):
        for tt in tiles:
            ins = dve.max(best[:, tt], scores[tt][:])
        step(ins)
        for tt in tiles:
            ins = dve.match_replace(scores[tt][:], best[:, tt], scores[tt][:], TAKEN)
        step(ins)

    def biases(dve, tt):
        return dve.tensor_scalar(k.key_bias[:, tt, 0:(tt + 1) * P], scores[tt][:], FLOOR, NEG, ALU.is_gt, ALU.mult)

    def take_best(dve, step):
        for _ in range(ROUNDS):
            one_round(dve, step, tiles[:-1])
        for tt in tiles[:-1]:
            step(biases(dve, tt))

    k.best_rounds = ROUNDS
    k.best_round = lambda dve, step: one_round(dve, step, tiles[-1:])
    k.last_biases = lambda dve: biases(dve, tiles[-1])
    project(k, "z", k.xs_lhs, [d["w_z"]], copy_evac(lambda i, tt: k.sz[:, tt, :]), ahead=1,
            then=columns(d["w_out"], 512), aside=take_best)
    s.close()


def attention(k, name, units, out, group=8, stats=None, sync=None, aside=None):
    nc = k.nc
    n = len(units)
    widest = max(u["keys"].shape[-1] for u in units)
    LAG = 3
    NS, NP = LAG + 1, 4
    with ExitStack() as s:
        probs = k.sb(s, f"{name}_probs", [P, NP, widest])
        pT = k.sb(s, f"{name}_pT", [P, 2, widest])
        own = stats is None
        if own:
            nmax_t, den_t = k.sb(s, f"{name}_nmax", [P, n]), k.sb(s, f"{name}_den", [P, n])
            nmax, den = (lambda j, t=t: t[:, j:j + 1] for t in (nmax_t, den_t))
        else:
            nmax, den = stats
        rden = k.sb(s, f"{name}_rden", [P, n])
        sbank = [k.ps(s, f"{name}_scores{i}") for i in range(NS)]
        tbank = [k.ps(s, f"{name}_pT{i}") for i in range(2)]
        obank = [k.ps(s, f"{name}_out{i}") for i in range(2)]
        scores, maxed, probs_ready, turned, pT_ready, summed, out_free, rden_ready = (
            k.sem(f"{name}_{x}") for x in ("scores", "maxed", "probs", "turned", "pT", "summed", "outfree", "rden"))
        with nc.Block() as block:
            if sync is not None:
                @block.sync
                def _(sp):
                    sync(sp, out_free)

            @block.tensor
            def _(pe):
                for st in range(n + LAG + 1):
                    if st < n:
                        u = units[st]
                        if st >= NS:
                            pe.wait_ge(probs_ready, st - NS + 1)
                        w = u["keys"].shape[-1]
                        ms = u["masks"]
                        if "wait" in u:
                            pe.wait_ge(*u["wait"])
                        ins = pe.matmul(sbank[st % NS][:, 0:w], u["q"], u["keys"], start=True, stop=True)
                        for lhs, rhs, lo, hi in ms:
                            ins = pe.matmul(sbank[st % NS][:, lo:hi], lhs, rhs, start=False, stop=True,
                                            skip_group_check=True)
                        ins.then_inc(scores, 1)
                    if LAG <= st < n + LAG:
                        j = st - LAG
                        pe.wait_ge(probs_ready, j + 1)
                        if j >= 2:
                            pe.wait_ge(pT_ready, j - 1)
                        for b in range(len(units[j]["values"])):
                            ins = pe.transpose(tbank[j % 2][:, b * P:(b + 1) * P],
                                               probs[:, j % NP, b * P:(b + 1) * P], k.c("ident"))
                        ins.then_inc(turned, 1)
                    if st >= LAG + 1:
                        j = st - LAG - 1
                        g, h = divmod(j, group)
                        pe.wait_ge(pT_ready, j + 1)
                        if h == 0 and g >= 2:
                            pe.wait_ge(out_free, g - 1)
                        vs = units[j]["values"]
                        for b, v in enumerate(vs):
                            ins = pe.matmul(obank[g % 2][:, h * HD:(h + 1) * HD], pT[:, j % 2, b * P:(b + 1) * P],
                                            v, start=(b == 0), stop=(b == len(vs) - 1))
                        ins.then_inc(summed, 1)

            @block.scalar
            def _(act):
                for j, u in enumerate(units):
                    w = u["keys"].shape[-1]
                    act.wait_ge(maxed, j + 1)
                    if j >= NP:
                        act.wait_ge(turned, j - NP + 1)
                    act.activation(probs[:, j % NP, 0:w], sbank[j % NS][:, 0:w], ACT.Exp, bias=nmax(j),
                                   accum_out=den(j)).then_inc(probs_ready, 1)

            @block.vector
            def _(dve):
                for st in range(n + LAG + 2):
                    if st < n:
                        w = units[st]["keys"].shape[-1]
                        dve.wait_ge(scores, st + 1)
                        dve.reduce_max(nmax(st), sbank[st % NS][:, 0:w], AX, negate=True).then_inc(maxed, 1)
                    if LAG <= st < n + LAG:
                        j = st - LAG
                        w = len(units[j]["values"]) * P
                        dve.wait_ge(turned, j + 1)
                        if j >= 2:
                            dve.wait_ge(summed, j - 1)
                        dve.tensor_copy(pT[:, j % 2, 0:w], tbank[j % 2][:, 0:w]).then_inc(pT_ready, 1)
                    if aside:
                        aside(dve, st)
                    if st >= LAG + 2 and (st - LAG - 1) % group == 0:
                        g = (st - LAG - 1) // group - 1
                        a, b = g * group, (g + 1) * group
                        dve.wait_ge(summed, b)
                        o = obank[g % 2][:].rearrange("p (h d) -> p h d", h=group)
                        if own:
                            dve.reciprocal(rden[:, a:b], den_t[:, a:b]).then_inc(rden_ready, 1)
                            dve.wait_ge(rden_ready, g + 1)
                            dve.tensor_tensor(out(g), o, bc(rden[:, a:b], 2, HD), ALU.mult).then_inc(out_free, 1)
                        else:
                            dve.tensor_copy(out(g), o).then_inc(out_free, 1)


def state_space(k, ctx):
    nc, d = k.nc, k.d
    k.y = k.sb(ctx, "ssd_y", [P, TT, 512])
    HW = 4 * HD
    xs = k.sb(ctx, "xs_nat", [P, TT, 5 * P])
    with ExitStack() as s:
        bank = k.ps(s, "xs_bank", (P, 4, 512))
        turned, copied = k.sem("xs_turned"), [k.sem("xs_copied_v"), k.sem("xs_copied_s")]
        with nc.Block() as block:
            @block.tensor
            def _(pe):
                for tt in range(TT):
                    q = 2 * (tt % 2)
                    if tt >= 2:
                        pe.wait_ge(copied[0], tt - 1)
                        pe.wait_ge(copied[1], tt - 1)
                    for b in range(5):
                        ins = pe.transpose(bank[:, q + b // 4, (b % 4) * P:(b % 4 + 1) * P],
                                           k.xbcT[:, b, tt * P:(tt + 1) * P], k.c("ident"))
                    ins.then_inc(turned, 1)

            @block.vector
            def _(dve):
                for tt in range(TT):
                    dve.wait_ge(turned, tt + 1)
                    dve.tensor_copy(xs[:, tt, 0:512], bank[:, 2 * (tt % 2), :]).then_inc(copied[0], 1)

            @block.scalar
            def _(act):
                for tt in range(TT):
                    act.wait_ge(turned, tt + 1)
                    act.activation(xs[:, tt, 512:640], bank[:, 2 * (tt % 2) + 1, 0:P],
                                   ACT.Copy).then_inc(copied[1], 1)
    with ExitStack() as s2:
        k_vec = k.sb(s2, "ssd_vec", [P, 24 + 512])
        t8 = [k.sb(s2, f"ssd_t{i}", [P, TT, 8]) for i in range(8)]
        decay = k.sb(s2, "ssd_decay", [P, 3, TT * 8])
        X = k.sb(s2, "ssd_x", [P, 2, 512])
        Xd = k.sb(s2, "ssd_xd", [P, 2, 512])
        Gm = k.sb(s2, "ssd_gm", [P, 2, 2, P])
        At, L, MT = (k.sb(s2, f"ssd_{n}", [P, 2, 4, P]) for n in ("at", "l", "mt"))
        St = k.sb(s2, "ssd_state", [P, HW])
        y1 = k.sb(s2, "ssd_y1", [P, 512])
        y2 = k.sb(s2, "ssd_y2", [P, 512])
        yy = k.sb(s2, "ssd_yy", [P, 512])
        ms = k.sb(s2, "ssd_ms", [P, TT, 3])
        b_g = [k.ps(s2, f"ssd_g{i}") for i in range(2)]
        b_seg = [k.ps(s2, f"ssd_seg{i}") for i in range(2)]
        b_y = k.ps(s2, "ssd_ydiag")
        b_sum = b_y
        b_off = [k.ps(s2, f"ssd_yoff{i}") for i in range(2)]
        b_st = k.ps(s2, "ssd_st")
        (vec_in, e_ready, a_ready, sums_ready, decay_ready, x_ready, g_done, gm_ready, at_ready, seg_done, l_ready,
         mt_ready, ydiag_done, yoff_done, st_done, st_ready, y_free, step_d, step_a, sq_ready, rms_ready, lg_ready) = (
            k.sem("ssd_" + x) for x in ("vec_in", "e", "a", "sums", "decay", "x", "g", "gm", "at", "seg", "l", "mt",
                                        "ydiag", "yoff", "stdone", "st", "yfree", "stepd", "stepa", "sq", "rms",
                                        "lg"))
        z_ready = k.sem("ssd_z")
        dtb, al, dsk, nw = (k_vec[:, 0:8], k_vec[:, 8:16], k_vec[:, 16:24], k_vec[:, 24:536])
        pre, ex, dt, a_t, tmp, tmp2, tmp3, A = t8
        dr = k.v[:, :, 68:76]
        NU = TT * 2
        with nc.Block() as block:
            @block.sync
            def _(sp):
                sp.dma_start(k_vec[:, 0:24], k.d["vecs"][:, 0:24]).then_inc(vec_in, 16)
                sp.dma_start(nw, k.vec("ssd_norm_w")).then_inc(vec_in, 16)

            @block.tensor
            def _(pe):
                pe.wait_ge(a_ready, 1)
                Af = A[:].rearrange("p c h -> p (c h)")
                for i, m in enumerate(("after", "ones", "upto")):
                    ins = pe.matmul(b_sum[:, i * 32:(i + 1) * 32], k.c(m), Af, start=True, stop=True)
                ins.then_inc(sums_ready, 1)
                for c in range(TT):
                    tok = slice(c * P, (c + 1) * P)
                    if c >= 1:
                        pe.wait_ge(gm_ready, c)
                    for g in range(2):
                        r = slice(HD * g, HD * (g + 1))
                        ins = pe.matmul(b_g[g][:, 0:P], k.xbcT[r, 4, tok], k.xbcT[r, 5, tok],
                                        start=True, stop=True)
                    ins.then_inc(g_done, 1)
                    if c >= 1:
                        pe.wait_ge(st_ready, c)
                        pe.wait_ge(y_free, c)
                        for g in range(2):
                            r = slice(HD * g, HD * (g + 1))
                            ins = pe.matmul(b_off[g][:, 0:HW], k.xbcT[r, 5, tok], St[r, :],
                                            start=True, stop=True)
                        ins.then_inc(yoff_done, 1)
                    pe.wait_ge(x_ready, c + 1)
                    if c < TT - 1:
                        for g in range(2):
                            ins = pe.matmul(b_st[:, g * HW:(g + 1) * HW], xs[:, c, 512:640],
                                            Xd[:, c % 2, g * HW:(g + 1) * HW], start=True, stop=True)
                        ins.then_inc(st_done, 1)
                    for g in range(3):
                        if g < 2:
                            u = 2 * c + g
                            pe.wait_ge(at_ready, u + 1)
                            if u >= 2:
                                pe.wait_ge(l_ready, u - 1)
                            for q in range(4):
                                ins = pe.matmul(b_seg[u % 2][:, q * P:(q + 1) * P], At[:, u % 2, q, :], k.c("upto"),
                                                start=True, stop=True)
                            ins.then_inc(seg_done, 1)
                        if g >= 1:
                            u = 2 * c + g - 1
                            pe.wait_ge(mt_ready, u + 1)
                            for q in range(4):
                                cols = slice((4 * (g - 1) + q) * HD, (4 * (g - 1) + q + 1) * HD)
                                ins = pe.matmul(b_y[:, cols], MT[:, u % 2, q, :], X[:, c % 2, cols], start=True, stop=True)
                            ins.then_inc(ydiag_done, 1)

            @block.gpsimd
            def _(pool):
                pool.wait_ge(a_ready, 1)
                for u in range(NU):
                    c, g = divmod(u, 2)
                    if u >= 2:
                        pool.wait_ge(seg_done, u - 1)
                    pool.tensor_tensor(At[:, u % 2], bc(k.c("after"), 1, 4), bc(A[:, c, 4 * g:4 * g + 4], 2, P),
                                       ALU.mult).then_inc(at_ready, 1)

            @block.scalar
            def _(act):
                for c in range(TT):
                    act.activation(k.sz[:, c, :], k.sz[:, c, :], ACT.Silu).then_inc(z_ready, 1)
                act.wait_ge(vec_in, 32)
                act.activation(a_t[:, 0, :], al, ACT.Exp).then_inc(e_ready, 1)
                act.wait_ge(step_d, 3)
                act.activation(ex[:], tmp[:], ACT.Exp).then_inc(e_ready, 1)
                act.wait_ge(step_d, 4)
                act.activation(tmp3[:], tmp2[:], ACT.Ln).then_inc(lg_ready, 1)
                act.wait_ge(sums_ready, 1)
                act.activation(decay[:], b_sum[:, 0:96].rearrange("p (a b) -> p a b", a=3),
                               ACT.Exp).then_inc(decay_ready, 1)
                for u in range(NU):
                    act.wait_ge(seg_done, u + 1)
                    if u >= 2:
                        act.wait_ge(mt_ready, u - 1)
                    act.activation(L[:, u % 2].rearrange("p q l -> p (q l)"), b_seg[u % 2][:], ACT.Exp).then_inc(l_ready, 1)
                for c in range(TT):
                    act.wait_ge(sq_ready, c + 1)
                    act.activation(ms[:, c, 1:2], ms[:, c, 0:1], ACT.Sqrt, scale=1.0,
                                   bias=0.0).then_inc(rms_ready, 1)

            @block.vector
            def _(dve):
                step = Chain(dve, step_d)
                dve.wait_ge(vec_in, 32)
                step(dve.tensor_tensor(pre[:], dr, bc(dtb, 1, TT), ALU.add))
                step(dve.tensor_scalar(dt[:], pre[:], -1.0, None, ALU.mult))
                step(dve.tensor_tensor(tmp[:], pre[:], dt[:], ALU.min))
                dve.wait_ge(e_ready, 2)
                step(dve.tensor_scalar(tmp2[:], ex[:], 1.0, None, ALU.add))
                step(dve.tensor_scalar(dt[:], tmp2[:], -1.0, 1e-30, ALU.add, ALU.max))
                step(dve.reciprocal(tmp[:], dt[:]))
                step(dve.tensor_tensor(dt[:], tmp[:], ex[:], ALU.mult))
                dve.wait_ge(lg_ready, 1)
                step(dve.tensor_tensor(tmp3[:], tmp3[:], dt[:], ALU.mult))
                step(dve.tensor_scalar(tmp2[:], tmp2[:], 1.0, None, ALU.is_equal))
                step(dve.tensor_tensor(tmp2[:], tmp2[:], ex[:], ALU.mult))
                step(dve.tensor_tensor(tmp3[:], tmp3[:], tmp2[:], ALU.add))
                step(dve.scalar_tensor_tensor(dt[:], pre[:], 0.0, tmp3[:], ALU.max, ALU.add))
                step(dve.tensor_scalar(a_t[:, 1, :], a_t[:, 0, :], -1.0, None, ALU.mult))
                dve.tensor_tensor(A[:], dt[:], bc(a_t[:, 1, :], 1, TT), ALU.mult).then_inc(a_ready, 1)
                dve.wait_ge(decay_ready, 1)
                h8 = dict(h=8)
                for c in range(TT):
                    cs = slice(c * 8, c * 8 + 8)
                    xc = xs[:, c, 0:512].rearrange("p (h d) -> p h d", **h8)
                    Xc = X[:, c % 2, :].rearrange("p (h d) -> p h d", **h8)
                    Xdc = Xd[:, c % 2, :].rearrange("p (h d) -> p h d", **h8)
                    step(dve.tensor_tensor(Xc, xc, bc(dt[:, c, :], 2, HD), ALU.mult))
                    dve.tensor_tensor(Xdc, Xc, bc(decay[:, 0, cs], 2, HD), ALU.mult).then_inc(x_ready, 1)
                    dve.wait_ge(g_done, c + 1)
                    for g in range(2):
                        ins = dve.tensor_tensor(Gm[:, c % 2, g, :], b_g[g][:, 0:P], k.c("upto"), ALU.mult)
                        if g == 0:
                            step(ins)
                    ins.then_inc(gm_ready, 1)
                    if c < TT - 1:
                        dve.wait_ge(st_done, c + 1)
                        if c >= 1:
                            dve.wait_ge(yoff_done, c)
                            s3 = St[:].rearrange("p (h d) -> p h d", h=4)
                            for g in range(2):
                                r = slice(HD * g, HD * (g + 1))
                                step(dve.tensor_tensor(s3[r], s3[r], bc(decay[r, 1, c * 8 + 4 * g:c * 8 + 4 * g + 4], 2, HD),
                                                       ALU.mult))
                            for g in range(2):
                                r = slice(HD * g, HD * (g + 1))
                                ins = dve.tensor_tensor(St[r, :], St[r, :], b_st[r, g * HW:(g + 1) * HW], ALU.add)
                                if g == 0:
                                    step(ins)
                            ins.then_inc(st_ready, 1)
                        else:
                            for g in range(2):
                                r = slice(HD * g, HD * (g + 1))
                                ins = dve.tensor_copy(St[r, :], b_st[r, g * HW:(g + 1) * HW])
                                if g == 0:
                                    step(ins)
                            ins.then_inc(st_ready, 1)
                    dve.wait_ge(gm_ready, c + 1)
                    for g in range(2):
                        u = 2 * c + g
                        dve.wait_ge(l_ready, u + 1)
                        if u >= 2:
                            dve.wait_ge(ydiag_done, u - 1)
                        dve.tensor_tensor(MT[:, u % 2], L[:, u % 2], bc(Gm[:, c % 2, g, :], 1, 4),
                                          ALU.mult).then_inc(mt_ready, 1)
                    y13, y23 = (t[:].rearrange("p (h d) -> p h d", **h8) for t in (y1, y2))
                    step(dve.tensor_tensor(y13, xc, bc(dsk, 2, HD), ALU.mult))
                    if c >= 1:
                        dve.wait_ge(yoff_done, c)
                        for g in range(2):
                            hs = slice(4 * g, 4 * g + 4)
                            step(dve.tensor_tensor(y23[:, hs], b_off[g][:, 0:HW].rearrange("p (h d) -> p h d", h=4),
                                                   bc(decay[:, 2, c * 8 + 4 * g:c * 8 + 4 * g + 4], 2, HD), ALU.mult))
                        step(dve.tensor_tensor(y1[:], y1[:], y2[:], ALU.add))
                    dve.wait_ge(ydiag_done, 2 * (c + 1))
                    dve.tensor_tensor(y2[:], y1[:], b_y[:], ALU.add).then_inc(y_free, 1)
                    dve.wait_ge(y_free, c + 1)
                    dve.wait_ge(z_ready, c + 1)
                    step(dve.tensor_tensor(k.y[:, c, :], y2[:], k.sz[:, c, :], ALU.mult))
                    step(dve.tensor_tensor(yy[:], k.y[:, c, :], k.y[:, c, :], ALU.mult))
                    step(dve.reduce_sum(ms[:, c, 2:3], yy[:], AX))
                    dve.tensor_scalar(ms[:, c, 0:1], ms[:, c, 2:3], 1.0 / 512, LN_EPS, ALU.mult,
                                      ALU.add).then_inc(sq_ready, 1)
                for c in range(TT):
                    dve.wait_ge(rms_ready, c + 1)
                    step(dve.reciprocal(ms[:, c, 2:3], ms[:, c, 1:2]))
                    step(dve.scalar_tensor_tensor(k.y[:, c, :], k.y[:, c, :], ms[:, c, 2:3], nw, ALU.mult, ALU.mult))


def row_stats(dve, stats, x, half):
    return dve.bn_stats(stats[:, half, :], x[:, half * 512:(half + 1) * 512])


def layer_norm(k, name, x, g, b, stats, prefetch=None):
    nc = k.nc
    with ExitStack() as s:
        vec = k.sb(s, f"{name}_gb", [P, 2, DM])
        mv = k.sb(s, f"{name}_mv", [P, TT, 2])
        sd = k.sb(s, f"{name}_sd", [P, 3, TT])
        tmp = k.sb(s, f"{name}_tmp", [P, TT, DM])
        vec_in, var_ready, sd_ready, step_d = (k.sem(f"{name}_{n}") for n in ("vecin", "var", "sd", "step"))
        with nc.Block() as block:
            @block.sync
            def _(sp):
                sp.dma_start(vec[:, 0, :], k.vec(g)).then_inc(vec_in, 16)
                sp.dma_start(vec[:, 1, :], k.vec(b)).then_inc(vec_in, 16)
                if prefetch:
                    prefetch(sp)

            @block.vector
            def _(dve):
                step = Chain(dve, step_d)
                for tt in range(TT):
                    step(dve.bn_aggr(mv[:, tt, :], stats[:, tt, :, :].rearrange("p a b -> p (a b)")))
                dve.tensor_scalar(sd[:, 0, :], mv[:, :, 1], LN_EPS, None, ALU.add).then_inc(var_ready, 1)
                dve.wait_ge(vec_in, 32)
                for tt in range(TT):
                    step(dve.scalar_tensor_tensor(tmp[:, tt, :], x[:, tt, :], mv[:, tt, 0:1], vec[:, 0, :],
                                                  ALU.subtract, ALU.mult))
                dve.wait_ge(sd_ready, 1)
                step(dve.reciprocal(sd[:, 2, :], sd[:, 1, :]))
                for tt in range(TT):
                    step(dve.scalar_tensor_tensor(x[:, tt, :], tmp[:, tt, :], sd[:, 2, tt:tt + 1], vec[:, 1, :],
                                                  ALU.mult, ALU.add))

            @block.scalar
            def _(act):
                act.wait_ge(var_ready, 1)
                act.activation(sd[:, 1, :], sd[:, 0, :], ACT.Sqrt).then_inc(sd_ready, 1)


def rms_rows(k, name, x, out, gain, width=DM, eps=EPS, then=(), prefetch=None):
    nc = k.nc
    with ExitStack() as s:
        vec = k.sb(s, f"{name}_gain", [P, width])
        sq = k.sb(s, f"{name}_sq", [P, 2, width])
        m = k.sb(s, f"{name}_ms", [P, 4, TT])
        vec_in, summed, sd_ready, ms_ready, step_d = (k.sem(f"{name}_{n}") for n in ("vecin", "sum", "sd", "ms", "step"))
        with nc.Block() as block:
            @block.sync
            def _(sp):
                sp.dma_start(vec[:], k.vec(gain)).then_inc(vec_in, 16)
                for chunk in then:
                    k.load_chunk(sp, chunk)
                if prefetch:
                    prefetch(sp)

            @block.scalar
            def _(act):
                for tt in range(TT):
                    act.activation(sq[:, tt % 2, :], x(tt), ACT.Square, accum_out=m[:, 0, tt:tt + 1]).then_inc(summed, 1)
                    act.wait_ge(summed, tt + 1)
                act.wait_ge(ms_ready, 1)
                act.activation(m[:, 2, :], m[:, 1, :], ACT.Sqrt).then_inc(sd_ready, 1)

            @block.vector
            def _(dve):
                step = Chain(dve, step_d)
                dve.wait_ge(summed, TT)
                dve.tensor_scalar(m[:, 1, :], m[:, 0, :], 1.0 / width, eps, ALU.mult, ALU.add).then_inc(ms_ready, 1)
                dve.wait_ge(sd_ready, 1)
                step(dve.reciprocal(m[:, 3, :], m[:, 2, :]))
                dve.wait_ge(vec_in, 16)
                for tt in range(TT):
                    step(dve.scalar_tensor_tensor(out(tt), x(tt), m[:, 3, tt:tt + 1], vec[:], ALU.mult, ALU.mult))


def head_rms(k, ctx, name, count, head, then=None):
    H, D = head(0)[0].shape[2:]
    sq = k.sb(ctx, f"{name}_sq", [P, 2, H, D])
    ms, root, total = (k.sb(ctx, f"{name}_{n}", [P, TT, H]) for n in ("ms", "root", "total"))

    def first(dve, step, i):
        x, _, scale = head(i)
        for r in (slice(0, 2), slice(2, 4)):
            step(dve.tensor_tensor(sq[:], x[:, r], x[:, r], ALU.mult))
            step(dve.reduce_sum(total[:, r], sq[:], AX))
        return dve.tensor_scalar(ms[:], total[:], 1.0 / D / scale ** 2, EPS / scale ** 2, ALU.mult, ALU.add)

    def middle(act, i):
        return act.activation(root[:], ms[:], ACT.Sqrt)

    def last(dve, step, i):
        x, gain, _ = head(i)
        step(dve.reciprocal(total[:], root[:]))
        for tt in range(TT):
            step(dve.tensor_tensor(x[:, tt], x[:, tt], bc(total[:, tt], 2, D), ALU.mult))
            step(dve.tensor_tensor(x[:, tt], x[:, tt], bc(gain, 1, H), ALU.mult))
        if then:
            then(dve, step, i)

    return count, first, middle, last


def project(k, name, lhsT, chunks, evac, ahead=0, then=(), after=None, turn=None, aside=None):
    nc = k.nc
    n = len(chunks)
    RING = 4
    kd = chunks[0].shape[1]
    width = [c.shape[2] for c in chunks]
    q0 = k.chunks_loaded - ahead
    wh, wl = k.w_ring
    turns, turn_src, turn_dst = turn or (0, None, None)
    NBANK = 6 if turns else 8
    with ExitStack() as s:
        banks = [k.ps(s, f"{name}_bank{i}") for i in range(NBANK)]
        tbanks = [k.ps(s, f"{name}_tbank{i}") for i in range(8 - NBANK)]
        finished, turned, turn_out, first_done, middle_done = (
            k.sem(f"{name}_{x}") for x in ("finished", "turned", "turn_out", "first", "middle"))
        afters, first, middle, last = after or (0, None, None, None)
        hi_ready, lo_ready, piece_done, done, free, step_d = (
            k.sem(f"{name}_{x}") for x in ("hi", "lo", "piece", "done", "free", "step"))
        with nc.Block() as block:
            @block.sync
            def _(sp):
                for i, chunk in list(enumerate(list(chunks) + list(then)))[ahead:]:
                    if i >= 2:
                        sp.wait_ge(lo_ready, kd * (i - 1))
                    k.load_chunk(sp, chunk)

            def turned_after(j):
                i, c = divmod(j, kd)
                if 1 <= i <= turns and c >= kd - 2:
                    b = (i - 1) * 4 + 2 * (c - kd + 2)
                    return b, b + 1
                return ()

            def take_turned(act, j):
                for b in turned_after(j):
                    act.wait_ge(turned, b + 1)
                    o = turn_dst(b // 4, b % 4)
                    act.activation(o, tbanks[b % 2][0:o.shape[0], :], ACT.Copy).then_inc(turn_out, 1)

            @block.scalar
            def _(act):
                for i in range(n):
                    slot, round_ = (q0 + i) % 2, (q0 + i) // 2
                    act.wait_ge(k.w_in[slot], 16 * (round_ + 1))
                    for c in range(kd):
                        j = i * kd + c
                        if j >= RING:
                            take_turned(act, j - RING)
                            act.wait_ge(piece_done, j - RING + 1)
                        if 1 <= i <= afters and c == kd - 2:
                            act.wait_ge(first_done, i)
                            middle(act, i - 1).then_inc(middle_done, 1)
                        act.activation(wh[:, j % RING, 0:width[i]], k.w[:, slot, c, 0:width[i]],
                                       ACT.Copy).then_inc(hi_ready, 1)
                for j in range(n * kd - RING, n * kd):
                    take_turned(act, j)
                if afters == n:
                    act.wait_ge(first_done, n)
                    middle(act, n - 1).then_inc(middle_done, 1)

            @block.gpsimd
            def _(pool):
                for i in range(n):
                    for c in range(kd):
                        j = i * kd + c
                        pool.wait_ge(hi_ready, j + 1)
                        pool.tensor_tensor(wl[:, j % RING, 0:width[i]], k.w[:, (q0 + i) % 2, c, 0:width[i]],
                                           wh[:, j % RING, 0:width[i]].bitcast(F32), ALU.subtract).then_inc(lo_ready, 1)

            @block.tensor
            def _(pe):
                for i in range(n):
                    for c in range(kd):
                        j = i * kd + c
                        pe.wait_ge(lo_ready, j + 1)
                        for tt in range(TT):
                            u = i * TT + tt
                            if c == 0 and u >= NBANK:
                                pe.wait_ge(free, u - NBANK + 1)
                            ins = three_passes(pe, banks[u % NBANK][:, 0:width[i]], lhsT(tt, c),
                                               (wh[:, j % RING, 0:width[i]], wl[:, j % RING, 0:width[i]]),
                                               c == 0, c == kd - 1)
                            if c < kd - 1 and tt == TT - 1:
                                ins.then_inc(piece_done, 1)
                            elif c == kd - 1 and tt < TT - 1:
                                ins.then_inc(done, 1)
                        if c == kd - 1:
                            ins.then_inc(piece_done, 1)
                        for b in turned_after(j):
                            pe.wait_ge(finished, i)
                            if b >= 2:
                                pe.wait_ge(turn_out, b - 1)
                            for tt in range(TT):
                                a = turn_src(b // 4, tt, b % 4)
                                ins = pe.transpose(tbanks[b % 2][0:a.shape[1], tt * P:(tt + 1) * P], a, k.c("ident"))
                            ins.then_inc(turned, 1)

            @block.vector
            def _(dve):
                step = Chain(dve, step_d)
                if aside:
                    aside(dve, step)
                for i in range(n):
                    for tt in range(TT):
                        if tt < TT - 1:
                            dve.wait_ge(done, i * (TT - 1) + tt + 1)
                        else:
                            dve.wait_ge(piece_done, kd * (i + 1))
                        evac(dve, step, i, tt, banks[(i * TT + tt) % NBANK]).then_inc(free, 1)
                        dve.wait_ge(free, i * TT + tt + 1)
                    if i < afters:
                        if first:
                            first(dve, step, i).then_inc(first_done, 1)
                        else:
                            dve.sem_inc(first_done, 1)
                        dve.wait_ge(middle_done, i + 1)
                        last(dve, step, i)
                        dve.sem_inc(finished, 1)


def expert_weights(k, name, ctx):
    w1 = [k.sb(ctx, f"{name}_w1_{i}", [P, KD * 2 * FF]) for i in range(W_SLOTS)]
    w2 = [k.sb(ctx, f"{name}_w2_{i}", [P, 2 * DM]) for i in range(W_SLOTS)]
    w1_in, w2_in = ([k.sem(f"{name}_{n}{i}") for i in range(W_SLOTS)] for n in ("w1", "w2"))
    return w1, w2, w1_in, w2_in


def router_weights(k, name, W, ctx):
    return k.sb(ctx, f"{name}_wr", [P, KD, W]), k.sb(ctx, f"{name}_bv", [P, W]), k.sem(f"{name}_in")


def first_loads(sp, router, weights, logits_w, bias, w_gu, w_dn):
    wr, bv, in_ready = router
    w1, w2, w1_in, w2_in = weights
    sp.dma_start(wr[:], logits_w).then_inc(in_ready, 16)
    sp.dma_start(bv[:], bias).then_inc(in_ready, 16)
    for e in range(W_SLOTS):
        sp.dma_start(w1[e][:], w_gu[e]).then_inc(w1_in[e], 16)
        sp.dma_start(w2[e][:], w_dn[e]).then_inc(w2_in[e], 16)


def route(k, name, E, G, S, router, ctx, rows, x_store):
    nc = k.nc
    PG, NT, W = E // G, most_tiles(E, S), G + E
    k.gate = k.sb(ctx, f"{name}_gate", [P, 2, TT])
    k.slot = k.sb(ctx, f"{name}_slot", [P, 2, TT], U32)
    k.tok_of = k.sb(ctx, f"{name}_tok_of", [S, NT], U32)
    k.exp_of = k.sb(ctx, f"{name}_exp_of", [1, NT - E], I32)
    k.used = k.sb(ctx, f"{name}_used", [1, 1], I32)
    k.rows_stored = k.sem(f"{name}_rows_stored")
    with ExitStack() as s:
        wr, bv, in_ready = router
        wrh, wrl = (k.sb(s, f"{name}_wr{x}", [P, KD, W], F32R) for x in ("hi", "lo"))
        wr_ready = k.sem(f"{name}_wr_ready")
        lg = k.sb(s, f"{name}_lg", [P, TT, W])
        (group_max, group_sum, group_p, first_max, second_max, gap, gap_exp, pair_sum, share, key_max) = (
            k.sb(s, f"{name}_{n}", [P, TT]) for n in ("gmax", "gsum", "gp", "max1", "max2", "gap", "gapexp", "psum",
                                                      "share", "keymax"))
        g_diff, g_exp, g_key, g_hot = (k.sb(s, f"{name}_g{i}", [P, TT, G]) for i in range(4))
        mine, key, hot1, rest, hot2 = (k.sb(s, f"{name}_e{i}", [P, TT, PG]) for i in range(5))
        wide = k.sb(s, f"{name}_wide", [P, TT, G, PG])
        OH = k.sb(s, f"{name}_oh", [P, 2, TT, G, PG])
        picked = k.sb(s, f"{name}_picked", [P, 2, TT, E])
        M = k.sb(s, f"{name}_m", [P, TT, E])
        extra, cum, base, zero, counts = (k.sb(s, f"{name}_{n}", [P, E]) for n in ("extra", "cum", "base", "zero",
                                                                                  "counts"))
        rank = k.sb(s, f"{name}_rank", [P, TT, E])
        cmp = k.sb(s, f"{name}_cmp", [1, NT - E, E])
        tef = k.sb(s, f"{name}_tef", [1, NT - E])
        pos, q, over, tile, own, r, slotf = (k.sb(s, f"{name}_{n}", [P, 2, TT]) for n in ("pos", "q", "over", "tile",
                                                                                         "own", "r", "slotf"))
        ohr = k.sb(s, f"{name}_ohr", [P, 2, TT, S])
        ohj = k.sb(s, f"{name}_ohj", [P, 2, TT, NT])
        lT = k.sb(s, f"{name}_lT", [W, SEQ])
        lT_ready = k.sem(f"{name}_lT_ready")
        lbank, nbank, rbank, totals, tbank = (k.ps(s, f"{name}_{n}") for n in ("lbank", "nbank", "rbank", "totals",
                                                                              "tbank"))
        (logits_done, step_d, diff_ready, exp_ready, m_ready, rank_done, oh_ready, tok_done) = (
            k.sem(f"{name}_{n}") for n in ("logits", "step", "diff", "exp", "mready", "rank", "oh", "tok"))
        with nc.Block() as block:
            @block.sync
            def _(sp):
                for tt in range(TT):
                    sp.dma_start(rows[tt * P:(tt + 1) * P, :], x_store(tt)).then_inc(k.rows_stored, 16)
                sp.wait_ge(k.rows_stored, 16 * TT)

            @block.tensor
            def _(pe):
                pe.wait_ge(in_ready, 32)
                pe.wait_ge(wr_ready, 2)
                for c in range(KD):
                    ins = three_passes(pe, lbank[0:W, :], (wrh[:, c, :], wrl[:, c, :]), (k.xh[:, c, :], k.xl[:, c, :]),
                                       c == 0, c == KD - 1)
                ins.then_inc(logits_done, 1)
                pe.wait_ge(lT_ready, 1)
                for tt in range(TT):
                    ins = pe.matmul(nbank[:, tt * W:(tt + 1) * W], lT[:, tt * P:(tt + 1) * P],
                                    k.c("ident")[0:W, 0:W], start=True, stop=True)
                ins.then_inc(logits_done, 1)
                pe.wait_ge(m_ready, 1)
                flat = M[:].rearrange("p t e -> p (t e)")
                pe.matmul(totals[:, 0:TT * E], k.c("ones"), flat, start=True, stop=True)
                pe.matmul(rbank[:, 0:TT * E], k.c("before"), flat, start=True, stop=True).then_inc(rank_done, 1)
                pe.wait_ge(oh_ready, 1)
                for j in range(2 * TT):
                    i, tt = divmod(j, TT)
                    ins = pe.matmul(tbank[0:S, 0:NT], ohr[:, i, tt, :], ohj[:, i, tt, :], start=(j == 0),
                                    stop=(j == 2 * TT - 1))
                ins.then_inc(tok_done, 1)

            @block.gpsimd
            def _(pool):
                pool.wait_ge(in_ready, 32)
                pool.tensor_copy(wrh[:], wr[:]).then_inc(wr_ready, 1)
                pool.wait_ge(wr_ready, 1)
                pool.tensor_tensor(wrl[:], wr[:], wrh[:].bitcast(F32), ALU.subtract).then_inc(wr_ready, 1)

            @block.scalar
            def _(act):
                act.wait_ge(logits_done, 1)
                act.activation(lT[:], lbank[0:W, :], ACT.Copy).then_inc(lT_ready, 1)
                act.wait_ge(diff_ready, 1)
                act.activation(g_exp[:], g_diff[:], ACT.Exp).then_inc(exp_ready, 1)
                act.wait_ge(diff_ready, 2)
                act.activation(gap_exp[:], gap[:], ACT.Exp).then_inc(exp_ready, 1)

            @block.vector
            def _(dve):
                step = Chain(dve, step_d)

                def first_best(x, best, down, key, onehot, n):
                    step(dve.reduce_max(best[:], x, AX))
                    step(dve.tensor_tensor(key, x, bc(best[:], 2, n), ALU.is_equal))
                    step(dve.tensor_tensor(key, key, down, ALU.mult))
                    step(dve.reduce_max(key_max[:], key, AX))
                    step(dve.tensor_tensor(onehot, key, bc(key_max[:], 2, n), ALU.is_equal))

                def down(n):
                    return bc(k.c("down")[:, P - n:P], 1, TT)

                def choose(i, hot):
                    step(dve.tensor_tensor(OH[:, i], bc(g_hot[:], 3, PG), bc(hot[:], 2, G), ALU.mult))

                step(dve.memset(zero[:], 0.0))
                dve.wait_ge(in_ready, 32)
                dve.wait_ge(logits_done, 2)
                step(dve.tensor_tensor(lg[:], nbank[:, 0:TT * W].rearrange("p (t w) -> p t w", t=TT), bc(bv[:], 1, TT),
                                       ALU.add))
                gl = lg[:, :, 0:G]
                first_best(gl, group_max, down(G), g_key[:], g_hot[:], G)
                dve.tensor_tensor(g_diff[:], gl, bc(group_max[:], 2, G), ALU.subtract).then_inc(diff_ready, 1)
                step(dve.tensor_tensor(wide[:], lg[:, :, G:W].rearrange("p t (g e) -> p t g e", g=G),
                                       bc(g_hot[:], 3, PG), ALU.mult))
                step(dve.reduce_sum(mine[:], wide[:].rearrange("p t g e -> p t e g"), AX))
                first_best(mine[:], first_max, down(PG), key[:], hot1[:], PG)
                step(dve.scalar_tensor_tensor(rest[:], hot1[:], NEG, mine[:], ALU.mult, ALU.add))
                first_best(rest[:], second_max, down(PG), key[:], hot2[:], PG)
                choose(0, hot1)
                choose(1, hot2)
                flat = OH[:].rearrange("p i t g e -> p i t (g e)")
                dve.tensor_tensor(M[:], flat[:, 0], flat[:, 1], ALU.add).then_inc(m_ready, 1)
                dve.tensor_tensor(gap[:], second_max[:], first_max[:], ALU.subtract).then_inc(diff_ready, 1)
                for i in range(2):
                    step(dve.tensor_tensor(picked[:, i], flat[:, i], bc(k.c("iota")[:, 0:E], 1, TT), ALU.mult))
                step(dve.reduce_sum(own[:], picked[:], AX))
                dve.wait_ge(exp_ready, 2)
                step(dve.reduce_sum(group_sum[:], g_exp[:], AX))
                step(dve.reciprocal(group_p[:], group_sum[:]))
                step(dve.tensor_scalar(pair_sum[:], gap_exp[:], 1.0, None, ALU.add))
                step(dve.reciprocal(share[:], pair_sum[:]))
                step(dve.tensor_tensor(k.gate[:, 0, :], share[:], group_p[:], ALU.mult))
                step(dve.tensor_tensor(k.gate[:, 1, :], k.gate[:, 0, :], gap_exp[:], ALU.mult))
                dve.wait_ge(rank_done, 1)
                total = totals[:, 0:TT * E].rearrange("p (t e) -> p t e", t=TT)
                step(dve.tensor_copy(rank[:, 0], zero[:]))
                for tt in range(1, TT):
                    step(dve.tensor_tensor(rank[:, tt], rank[:, tt - 1], total[:, tt - 1], ALU.add))
                step(dve.tensor_tensor(counts[:], rank[:, TT - 1], total[:, TT - 1], ALU.add))
                step(dve.tensor_tensor(rank[:], rank[:], rbank[:, 0:TT * E].rearrange("p (t e) -> p t e", t=TT), ALU.add))
                step(dve.tensor_scalar(extra[:], counts[:], S + 0.5, None, ALU.is_gt))
                for j in range(2, -(-SEQ // S)):
                    step(dve.scalar_tensor_tensor(extra[:], counts[:], j * S + 0.5, extra[:], ALU.is_gt, ALU.add))
                step(dve.tensor_tensor_scan(cum[:], extra[:], zero[:], 0.0, ALU.add, ALU.add))
                step(dve.scalar_tensor_tensor(base[:], cum[:], E - 1.0, extra[:], ALU.add, ALU.subtract))
                for i in range(2):
                    step(dve.tensor_tensor(picked[:, i], flat[:, i], rank[:], ALU.mult))
                step(dve.reduce_sum(pos[:], picked[:], AX))
                for i in range(2):
                    step(dve.tensor_tensor(picked[:, i], flat[:, i], bc(base[:], 1, TT), ALU.mult))
                step(dve.reduce_sum(tile[:], picked[:], AX))
                step(dve.tensor_scalar(over[:], pos[:], S - 0.5, None, ALU.is_gt))
                q_now = over
                for j in range(2, -(-SEQ // S)):
                    step(dve.scalar_tensor_tensor(q[:], pos[:], j * S - 0.5, q_now[:], ALU.is_gt, ALU.add))
                    q_now = q
                step(dve.tensor_tensor(tile[:], tile[:], own[:], ALU.subtract))
                step(dve.tensor_tensor(tile[:], tile[:], over[:], ALU.mult))
                step(dve.tensor_tensor(tile[:], tile[:], own[:], ALU.add))
                step(dve.tensor_tensor(tile[:], tile[:], q[:], ALU.add))
                step(dve.scalar_tensor_tensor(r[:], q[:], -float(S), pos[:], ALU.mult, ALU.add))
                for i in range(2):
                    step(dve.tensor_tensor(ohr[:, i], bc(k.c("iota")[:, 0:S], 1, TT), bc(r[:, i], 2, S), ALU.is_equal))
                    step(dve.tensor_tensor(ohj[:, i], bc(k.c("iota")[:, 0:NT], 1, TT), bc(tile[:, i], 2, NT),
                                           ALU.is_equal))
                    ins = dve.tensor_tensor(ohj[:, i], ohj[:, i], bc(k.c("tok"), 2, NT), ALU.mult)
                    if i == 0:
                        step(ins)
                ins.then_inc(oh_ready, 1)
                step(dve.scalar_tensor_tensor(slotf[:], tile[:], float(S), r[:], ALU.mult, ALU.add))
                step(dve.tensor_copy(k.slot[:], slotf[:]))
                step(dve.tensor_tensor(cmp[:], bc(k.c("iota")[0:1, 0:NT - E], 2, E), bc(cum[0:1, :], 1, NT - E),
                                       ALU.is_ge))
                step(dve.reduce_sum(tef[:], cmp[:], AX))
                step(dve.tensor_copy(k.exp_of[:], tef[:]))
                step(dve.tensor_scalar(k.used[:], cum[0:1, E - 1:E], float(E), None, ALU.add))
                dve.wait_ge(tok_done, 1)
                step(dve.tensor_copy(k.tok_of[:], tbank[0:S, 0:NT]))


class Perhaps:

    def __init__(self, eng, used):
        self.eng, self.used = eng, used

    def __call__(self, t):
        return self.eng.If(self.used > t)


def experts(k, name, E, S, x_in, rows, w_gu, w_dn, out_rows, weights):
    nc = k.nc
    NT, R = most_tiles(E, S), W_SLOTS
    w1, w2, w1_in, w2_in = weights
    with ExitStack() as s:
        xg = [k.sb(s, f"{name}_xg{i}", [S, DM]) for i in range(2)]
        idx = [k.sb(s, f"{name}_idx{i}", [S, 1], U32) for i in range(2)]
        xT = [k.sb(s, f"{name}_xT{i}", [P, KD * S]) for i in range(2)]
        sg = k.sb(s, f"{name}_sg", [P, 2 * S])
        prod = k.sb(s, f"{name}_prod", [P, 2 * S])
        hTh, hTl = ([k.sb(s, f"{name}_hT_{x}{i}", [P, 2 * S], F32R) for i in range(2)] for x in ("hi", "lo"))
        y = [k.sb(s, f"{name}_y{i}", [S, DM]) for i in range(2)]
        xbank = [k.ps(s, f"{name}_xbank{i}") for i in range(2)]
        gbank, ubank = ([k.ps(s, f"{name}_{n}{i}") for i in range(2)] for n in ("gate", "up"))
        ybank = k.ps(s, f"{name}_ybank", (P, 1024))
        XH = KD * S // 2
        y_out = [k.sem(f"{name}_yout{b}") for b in range(2)]
        (idx_ready, idx_seen, x_seen, x_turned, xT_v, xT_s, gate_done, gu_done, silu_ready, hT_ready, y_done, y_v, y_s,
         w2_hi, w2_lo, step_d) = (
            k.sem(f"{name}_{n}") for n in ("idx", "idx_seen", "x_seen", "x_turned", "xT_v", "xT_s", "gate", "gu", "silu",
                                           "hT", "y_done", "y_v", "y_s", "w2_hi", "w2_lo", "step"))

        def every_tile(eng, used, tile, empty=None):
            surely, perhaps = lambda t: nullcontext(), Perhaps(eng, used)
            for b in range(R):
                tile(0, b, surely)
            with eng.Fori(1, E // R) as i:
                for b in range(R):
                    tile(i, b, surely if b < R - 1 else perhaps)

            def extra(i, b):
                with eng.If(used > R * i + b):
                    tile(i, b, perhaps)
                if empty:
                    with eng.If(used < R * i + (b + 1)):
                        empty(b)

            with eng.Fori(E // R, NT // R) as i:
                for b in range(R):
                    extra(i, b)
            for b in range(NT % R):
                extra(NT // R, b)

        def w2_part(x, b, c, m=None):
            at = 4 * (b % 2) + 2 * c
            return x[:, at:at + 4, :] if m is None else x[:, at + m, :]

        def before(i, b):
            return (i, b - 1) if b else (i - 1, R - 1)

        def pair(i, b):
            return R // 2 * i + b // 2

        with nc.Block() as block:
            @block.sync
            def _(sp):
                used = sp.value_load(k.used[0:1, 0:1], min_val=E, max_val=NT)

                def load(e, i, b):
                    t = R * i + b
                    sp.wait_ge(gu_done, t - (R - 1))
                    sp.dma_start(w1[b][:], w_gu[bass.ds(e, 1)].rearrange("a p n -> (a p) n")).then_inc(w1_in[b], 16)
                    sp.wait_ge(w2_lo, t - (R - 1))
                    sp.dma_start(w2[b][:], w_dn[bass.ds(e, 1)].rearrange("a p n -> (a p) n")).then_inc(w2_in[b], 16)

                def extra(i, b):
                    with sp.If(used > R * i + b):
                        e = sp.value_load(k.exp_of[0:1, bass.ds(R * i + b - E, 1)], min_val=0, max_val=E - 1)
                        load(e, i, b)

                with sp.Fori(1, E // R) as i:
                    for b in range(R):
                        load(R * i + b, i, b)
                with sp.Fori(E // R, NT // R) as i:
                    for b in range(R):
                        extra(i, b)
                for b in range(NT % R):
                    extra(NT // R, b)
                sp.wait_ge(y_out[0], 16 * ((NT + 1) // 2))
                sp.wait_ge(y_out[1], 16 * (NT // 2))

            @block.gpsimd
            def _(pool):
                used = pool.value_load(k.used[0:1, 0:1], min_val=E, max_val=NT)
                pool.wait_ge(k.rows_stored, 16 * TT)

                def tile(i, b, more):
                    t = R * i + b
                    if not isinstance(t, int) or t >= 2:
                        pool.wait_ge(x_turned, t - 1)
                    pool.tensor_copy(idx[b % 2][:], k.tok_of[:, bass.ds(t, 1)]).then_inc(idx_ready, 1)
                    pool.wait_ge(idx_ready, t + 1)
                    pool.sem_inc(idx_seen, 1)
                    pool.indirect_dma_start(xg[b % 2][:], None, rows, bass.IndirectOffsetOnAxis(
                        ap=idx[b % 2][:], axis=0)).then_inc(x_in[b % 2], 16)

                every_tile(pool, used, tile)

            @block.tensor
            def _(pe):
                used = pe.value_load(k.used[0:1, 0:1], min_val=E, max_val=NT)

                def turn_x(t, b, n):
                    pe.wait_ge(x_in[b % 2], 16 * n + 16)
                    pe.wait_ge(xT_v, t)
                    pe.wait_ge(xT_s, t)
                    pe.sem_inc(x_seen, 1)
                    for c in range(KD):
                        ins = pe.transpose(xbank[c * 2 // KD][:, c * S % XH:c * S % XH + S],
                                           xg[b % 2][:, c * P:(c + 1) * P], k.c("ident")[0:S, 0:S])
                    ins.then_inc(x_turned, 1)

                def half(t, b, bank, n, signal):
                    for m in range(FF // P):
                        for c in range(KD):
                            w = c * 2 * FF + (n + m) * P
                            ins = pe.matmul(bank[b % 2][:, m * S:(m + 1) * S], w1[b][:, w:w + P],
                                            xT[b % 2][:, c * S:(c + 1) * S], start=(c == 0), stop=(c == KD - 1))
                    ins.then_inc(signal, 1)

                def down(t, b):
                    pe.wait_ge(w2_lo, t + 1)
                    pe.wait_ge(hT_ready, t + 1)
                    pe.wait_ge(y_v, t)
                    pe.wait_ge(y_s, t)
                    for m in range(2):
                        for c in range(2):
                            h = slice(c * S, (c + 1) * S)
                            ins = three_passes(pe, ybank[0:S, m * 512:(m + 1) * 512], (hTh[b % 2][:, h], hTl[b % 2][:, h]),
                                               (w2_part(k.xh, b, c, m), w2_part(k.xl, b, c, m)), c == 0, c == 1)
                    ins.then_inc(y_done, 1)

                def tile(i, b, more):
                    t = R * i + b
                    pe.wait_ge(w1_in[b], 16 * i + 16)
                    pe.wait_ge(xT_v, t + 1)
                    pe.wait_ge(xT_s, t + 1)
                    if not isinstance(t, int) or t >= 2:
                        pe.wait_ge(hT_ready, t - 1)
                    half(t, b, gbank, 0, gate_done)
                    with more(t + 1):
                        turn_x(t + 1, b + 1, pair(i, b + 1))
                    if not isinstance(t, int) or t >= 1:
                        down(t - 1, b - 1)
                    half(t, b, ubank, FF // P, gu_done)
                    if isinstance(more, Perhaps):
                        with pe.If(used < t + 2):
                            down(t, b)

                turn_x(0, 0, 0)
                every_tile(pe, used, tile)

            @block.vector
            def _(dve):
                used = dve.value_load(k.used[0:1, 0:1], min_val=E, max_val=NT)

                def one_by_one(t):
                    return Chain(dve, step_d, 2 * t)

                def copy_x(t, b):
                    dve.wait_ge(x_turned, t + 1)
                    if not isinstance(t, int) or t >= 2:
                        dve.wait_ge(gu_done, t - 1)
                    dve.tensor_copy(xT[b % 2][:, 0:XH], xbank[0][:, 0:XH]).then_inc(xT_v, 1)

                def take_y(i, b):
                    dve.wait_ge(y_done, R * i + b + 1)
                    if not isinstance(i, int) or R * i + b >= 2:
                        dve.wait_ge(y_out[b % 2], 16 * pair(i, b))
                    dve.tensor_copy(y[b % 2][:, 0:512], ybank[0:S, 0:512]).then_inc(y_v, 1)

                def tile(i, b, more):
                    t = R * i + b
                    step = one_by_one(t)
                    with more(t + 1):
                        copy_x(t + 1, b + 1)
                    dve.wait_ge(w2_hi, t + 1)
                    dve.tensor_tensor(w2_part(k.xl, b, 0), w2[b][:].rearrange("p (q n) -> p q n", q=4),
                                      w2_part(k.xh, b, 0).bitcast(F32), ALU.subtract).then_inc(w2_lo, 1)
                    if not isinstance(t, int) or t >= 1:
                        take_y(*before(i, b))
                    dve.wait_ge(silu_ready, t + 1)
                    dve.wait_ge(gu_done, t + 1)
                    step(dve.tensor_tensor(prod[:], sg[:], ubank[b % 2][:, 0:2 * S], ALU.mult))
                    if not isinstance(t, int) or t >= 2:
                        dve.wait_ge(y_done, t - 1)
                    step(dve.tensor_copy(hTh[b % 2][:], prod[:]))
                    dve.tensor_tensor(hTl[b % 2][:], prod[:], hTh[b % 2][:].bitcast(F32),
                                      ALU.subtract).then_inc(hT_ready, 1)
                    if isinstance(more, Perhaps):
                        with dve.If(used < t + 2):
                            take_y(i, b)

                copy_x(0, 0)
                every_tile(dve, used, tile)

            @block.scalar
            def _(act):
                used = act.value_load(k.used[0:1, 0:1], min_val=E, max_val=NT)

                def copy_x(t, b):
                    act.wait_ge(x_turned, t + 1)
                    if not isinstance(t, int) or t >= 2:
                        act.wait_ge(gu_done, t - 1)
                    act.activation(xT[b % 2][:, XH:2 * XH], xbank[1][:, 0:XH], ACT.Copy).then_inc(xT_s, 1)

                def take_y(i, b):
                    t = R * i + b
                    act.wait_ge(y_done, t + 1)
                    if not isinstance(t, int) or t >= 2:
                        act.wait_ge(y_out[b % 2], 16 * pair(i, b))
                    act.activation(y[b % 2][:, 512:1024], ybank[0:S, 512:1024], ACT.Copy).then_inc(y_s, 1)
                    act.wait_ge(y_s, t + 1)
                    act.wait_ge(y_v, t + 1)
                    act.dma_start(out_rows[bass.ds(t * S, S), :], y[b % 2][:]).then_inc(y_out[b % 2], 16)

                def tile(i, b, more):
                    t = R * i + b
                    act.wait_ge(gate_done, t + 1)
                    if not isinstance(t, int) or t >= 1:
                        act.wait_ge(hT_ready, t)
                    act.activation(sg[:], gbank[b % 2][:, 0:2 * S], ACT.Silu).then_inc(silu_ready, 1)
                    with more(t + 1):
                        copy_x(t + 1, b + 1)
                    act.wait_ge(w2_in[b], 16 * i + 16)
                    if not isinstance(t, int) or t >= 2:
                        act.wait_ge(y_done, t - 1)
                    act.activation(w2_part(k.xh, b, 0), w2[b][:].rearrange("p (q n) -> p q n", q=4),
                                   ACT.Copy).then_inc(w2_hi, 1)
                    if not isinstance(t, int) or t >= 1:
                        take_y(*before(i, b))
                    if isinstance(more, Perhaps):
                        with act.If(used < t + 2):
                            take_y(i, b)

                def empty(b):
                    act.sem_inc(y_out[b % 2], 16)

                copy_x(0, 0)
                every_tile(act, used, tile, empty)


def combine(k, name, out_rows, x, scale, out=None, stats=None):
    nc = k.nc
    with ExitStack() as s:
        yr = [k.sb(s, f"{name}_row{i}", [P, DM]) for i in range(2 * TT)]
        row_in, row_base = k.gather_sems[4:], list(k.gathered[4:])
        scaled, used, step_d, out_done = (k.sem(f"{name}_{n}") for n in ("scaled", "used", "step", "outd"))
        with nc.Block() as block:
            @block.gpsimd
            def _(pool):
                for j in range(2 * TT):
                    tt, i = divmod(j, 2)
                    pool.indirect_dma_start(yr[j][:], None, out_rows, bass.IndirectOffsetOnAxis(
                        ap=k.slot[:, i, tt:tt + 1], axis=0)).then_inc(row_in[j], 16)

            if scale != 1.0:
                @block.scalar
                def _(act):
                    for tt in range(TT):
                        act.activation(x[:, tt, :], x[:, tt, :], ACT.Copy, scale=scale).then_inc(scaled, 1)

            @block.vector
            def _(dve):
                step = Chain(dve, step_d)
                for tt in range(TT):
                    if scale != 1.0:
                        dve.wait_ge(scaled, tt + 1)
                    for i in range(2):
                        j = 2 * tt + i
                        dve.wait_ge(row_in[j], row_base[j] + 16)
                        dve.scalar_tensor_tensor(x[:, tt, :], yr[j][:], k.gate[:, i, tt:tt + 1], x[:, tt, :],
                                                 ALU.mult, ALU.add).then_inc(used, 1)
                        dve.wait_ge(used, j + 1)
                    if stats is not None:
                        for half in range(2):
                            step(row_stats(dve, stats[:, tt], x[:, tt, :], half))

            if out is not None:
                @block.sync
                def _(sp):
                    for tt in range(TT):
                        sp.wait_ge(used, 2 * tt + 2)
                        sp.dma_start(out[tt * P:(tt + 1) * P, :], x[:, tt, :]).then_inc(out_done, 16)
                    sp.wait_ge(out_done, 16 * TT)
    for j in range(2 * TT):
        k.gathered[4 + j] += 16


def head_norms(k, name, items, then, eps=EPS):
    nc = k.nc
    n = len(items)
    with ExitStack() as s:
        H, D = items[0][0].shape[2:]
        sq = k.sb(s, f"{name}_sq", [P, 2, H, D])
        m = k.sb(s, f"{name}_m", [P, n, 4, TT, H])
        summed, squared, ms_ready, sd_ready, step_d = (k.sem(f"{name}_{x}") for x in ("sum", "sq", "ms", "sd", "step"))
        with nc.Block() as block:
            @block.scalar
            def _(act):
                for j in range(n * TT):
                    i, tt = divmod(j, TT)
                    if j >= 2:
                        act.wait_ge(summed, j - 1)
                    act.activation(sq[:, j % 2], items[i][0][:, tt], ACT.Square).then_inc(squared, 1)
                for i in range(n):
                    act.wait_ge(ms_ready, i + 1)
                    act.activation(m[:, i, 2], m[:, i, 1], ACT.Sqrt).then_inc(sd_ready, 1)

            @block.vector
            def _(dve):
                step = Chain(dve, step_d)
                for j in range(n * TT):
                    i, tt = divmod(j, TT)
                    dve.wait_ge(squared, j + 1)
                    dve.reduce_sum(m[:, i, 0, tt], sq[:, j % 2], AX).then_inc(summed, 1)
                for i, (x, gain, scale) in enumerate(items):
                    dve.wait_ge(summed, (i + 1) * TT)
                    dve.tensor_scalar(m[:, i, 1], m[:, i, 0], 1.0 / D / scale ** 2, eps / scale ** 2, ALU.mult,
                                      ALU.add).then_inc(ms_ready, 1)
                for i, (x, gain, scale) in enumerate(items):
                    dve.wait_ge(sd_ready, i + 1)
                    step(dve.reciprocal(m[:, i, 3], m[:, i, 2]))
                    for tt in range(TT):
                        step(dve.tensor_tensor(x[:, tt], x[:, tt], bc(m[:, i, 3, tt], 2, D), ALU.mult))
                        step(dve.tensor_tensor(x[:, tt], x[:, tt], bc(gain, 1, H), ALU.mult))
                then(dve, step)


def copy_evac(dst):
    def evac(dve, step, i, tt, bank):
        o = dst(i, tt)
        return dve.tensor_copy(o, bank[:, 0:o.shape[-1]])
    return evac


def rope_tables(k, cos, sin):
    nc, d = k.nc, k.d
    two_pi = [6.28125, 0.0019340515136718750, 1.2554228305816650e-06]
    two_pi.append(float(2 * np.pi - np.sum(np.array(two_pi, np.float64))))
    MAGIC = 12582912.0
    EDGE = 3.1415925
    with ExitStack() as s:
        pi32 = k.sb(s, "pos_i", [P, TT], I32)
        pos = k.sb(s, "pos_f", [P, TT])
        ang, turns, r, c, over = (k.sb(s, f"ang{i}", [P, TT, 16]) for i in range(5))
        pos_in, red, done, step_d = k.sem("pos_in"), k.sem("angle_red"), k.sem("angle_done"), k.sem("angle_step")
        with nc.Block() as block:
            @block.sync
            def _(sp):
                sp.dma_start(pi32[:], d["positions"]).then_inc(pos_in, 16)

            @block.vector
            def _(dve):
                step = Chain(dve, step_d)
                dve.wait_ge(pos_in, 16)
                step(dve.tensor_copy(pos[:], pi32[:]))
                step(dve.tensor_tensor(ang[:], bc(pos[:], 2, 16), bc(k.c("freq"), 1, TT), ALU.mult))
                step(dve.tensor_scalar(turns[:], ang[:], 1.0 / (2 * np.pi), MAGIC, ALU.mult, ALU.add))
                step(dve.tensor_scalar(turns[:], turns[:], -MAGIC, None, ALU.add))
                for i, part in enumerate(two_pi):
                    step(dve.scalar_tensor_tensor(r[:], turns[:], -part, r[:] if i else ang[:], ALU.mult, ALU.add))
                step(dve.tensor_scalar(c[:], r[:], float(np.pi / 2), None, ALU.add))
                step(dve.tensor_scalar(over[:], c[:], float(np.pi), -2 * float(np.pi), ALU.is_gt, ALU.mult))
                step(dve.tensor_tensor(c[:], c[:], over[:], ALU.add))
                step(dve.tensor_scalar(c[:], c[:], EDGE, -EDGE, ALU.min, ALU.max))
                dve.tensor_scalar(r[:], r[:], EDGE, -EDGE, ALU.min, ALU.max).then_inc(red, 1)

            @block.scalar
            def _(act):
                act.wait_ge(red, 1)
                act.activation(cos[:], c[:], ACT.Sin).then_inc(done, 1)
                act.activation(sin[:], r[:], ACT.Sin).then_inc(done, 1)


def latent_attention(k, ctx):
    nc, d = k.nc, k.d
    k.o_mla = k.sb(ctx, "o_mla", [P, TT, 512])
    with ExitStack() as s:
        kv = k.sb(s, "kv", [P, TT, 1024])
        qT, kT = (k.sb(s, n, [MLA_D, 8, SEQ]) for n in ("mla_qT", "mla_kT"))
        with ExitStack() as s1:
            nat = k.sb(s1, "mla_nat", [P, TT, MLA_COLS])
            cos, sin = k.sb(s1, "cos2", [P, TT, 16]), k.sb(s1, "sin2", [P, TT, 16])
            gains = k.sb(s1, "mla_gains", [P, 2 * MLA_D])
            gains_in = k.sem("gains_in")
            with nc.Block() as block:
                @block.sync
                def _(sp):
                    a = VEC_AT["q_norm_mla"][0]
                    sp.dma_start(gains[:], k.d["vecs"][:, a:a + 2 * MLA_D]).then_inc(gains_in, 16)
                    sp.wait_ge(gains_in, 16)
            rope_tables(k, cos, sin)
            q4 = nat[:, :, 0:768].rearrange("p t (h e) -> p t h e", h=8)

            def rotate(dve, step, x, t):
                n = x.shape[2]
                C, S = bc(cos[:], 2, n), bc(sin[:], 2, n)
                a, b = x[:, :, :, 64:80], x[:, :, :, 80:96]
                for o, v, w in zip(t, (a, b, b, a), (C, S, C, S)):
                    step(dve.tensor_tensor(o[:], v, w, ALU.mult))
                step(dve.tensor_tensor(a, t[0][:], t[1][:], ALU.subtract))
                step(dve.tensor_tensor(b, t[2][:], t[3][:], ALU.add))

            with ExitStack() as s2:
                tq = [k.sb(s2, f"rope_tq{i}", [P, TT, 4, 16]) for i in range(4)]
                q_heads = lambda i: (nat[:, :, 384 * i:384 * (i + 1)].rearrange("p t (h e) -> p t h e", h=4))
                project(k, "mla", k.xs_lhs, columns(d["w_mla"], 384),
                        copy_evac(lambda i, tt: nat[:, tt, 384 * i:min(384 * i + 384, MLA_COLS)]), ahead=2,
                        then=columns(d["w_ukv"], 512),
                        after=head_rms(k, s2, "mlaq", 2, lambda i: (q_heads(i), gains[:, 0:MLA_D], MLA_D ** -0.5),
                                       lambda dve, step, i: rotate(dve, step, q_heads(i), tq)),
                        turn=(2, lambda i, tt, b: q4[:, tt, 4 * i + b, :], lambda i, b: qT[:, 4 * i + b, :]))
            ckv = lambda tt: nat[:, tt, 768:1024]
            rms_rows(k, "ckv", ckv, ckv, "norm_ckv", 256)
            with ExitStack() as s2:
                ckvT = [k.sb(s2, f"ckvT_{x}", [P, 2, SEQ], F32R) for x in ("hi", "lo")]
                transpose_split(k, "ckvT", lambda tt, b: nat[:, tt, 768 + b * P:768 + (b + 1) * P],
                                lambda b: tuple(x[:, b, :] for x in ckvT), 2)
                project(k, "ukv", lambda tt, c: tuple(x[:, c, tt * P:(tt + 1) * P] for x in ckvT),
                        columns(d["w_ukv"], 512), copy_evac(lambda i, tt: kv[:, tt, i * 512:(i + 1) * 512]), ahead=2,
                        then=dil_chunks(d, 0)[0:2])
            kf = k.sb(s1, "mla_k", [P, TT, 8, MLA_D])
            tk = [k.sb(s1, f"rope_tk{i}", [P, TT, 4, 16]) for i in range(4)]
            kv4 = kv[:].rearrange("p t (h e) -> p t h e", h=8)
            built = k.sem("k_built")
            with nc.Block() as block:
                @block.vector
                def _(dve):
                    for tt in range(TT):
                        dve.tensor_copy(kf[:, tt, :, 0:64], kv4[:, tt, :, 0:64]).then_inc(built, 1)
                        dve.tensor_copy(kf[:, tt, :, 64:96], bc(nat[:, tt, 1024:1056], 1, 8)).then_inc(built, 1)
                    dve.wait_ge(built, 2 * TT)
            head_norms(k, "mlanorm", [(kf[:], gains[:, MLA_D:], 1.0)],
                       lambda dve, step: [rotate(dve, step, kf[:, :, h:h + 4], tk) for h in (0, 4)])
            transpose_tiles(k, "mlaT", lambda tt, b: kf[:, tt, b, :], lambda b: kT[:, b, :], 8)
        units = []
        for tt in range(TT):
            w = (tt + 1) * P
            for h in range(8):
                units.append(dict(q=qT[:, h, tt * P:w], keys=kT[:, h, 0:w],
                                  masks=[(k.cb("ident_b"), k.cb("causal_b"), tt * P, w)],
                                  values=[kv[:, b, h * P + HD:(h + 1) * P] for b in range(tt + 1)]))
        attention(k, "mlaatt", units, lambda g: k.o_mla[:, g, :].rearrange("p (h d) -> p h d", h=8))


DIL_ORDER = (1, 2, 0)
FOLD = 4


def dil_chunks(d, turn):
    if turn == len(DIL):
        return columns(d["w_o_mla"], 512)
    return [columns(d["w_dil"], 512)[3 * i + DIL_ORDER[turn]] for i in range(3)]


def dilated_attention(k, ctx):
    nc, d = k.nc, k.d
    k.o_dil = k.sb(ctx, "o_dil", [P, TT, 512])
    NG = len(DIL)
    with ExitStack() as s:
        o_raw = k.sb(s, "o_raw", [P, NG, TT, 528])
        folded_out, folded_in = k.sem("folded_out"), k.sem("folded_in")
        gains = k.sb(s, "dil_gains", [P, 2 * NG * HD])
        gains_in = k.sem("dil_gains_in")
        with nc.Block() as block:
            @block.sync
            def _(sp):
                a = VEC_AT["q_norm_dil"][0]
                sp.dma_start(gains[:], k.d["vecs"][:, a:a + 2 * NG * HD]).then_inc(gains_in, 16)
                sp.wait_ge(gains_in, 16)
        dlo = k.cb("delta_b")
        dfold = k.cb("dfold_b").rearrange("p (g x) -> p g x", g=2)
        slope, slope4 = (k.cb(n).rearrange("p (h q) -> p h q", h=8) for n in ("slope_b", "slope4_b"))
        for turn, g in enumerate(DIL_ORDER):
            fold = DIL[g][1] > 1
            with ExitStack() as s1:
                nat = k.sb(s1, f"dil_nat{g}", [P, 3, TT, 512])
                qkT = k.sb(s1, f"dil_qkT{g}", [P, 8, SEQ])
                if fold:
                    lhs = lambda tt, c: tuple(x[:, c, tt::FOLD] for x in (k.xh, k.xl))
                else:
                    lhs = k.xs_lhs

                def head(i):
                    return (nat[:, i].rearrange("p t (h e) -> p t h e", h=8),
                            gains[:, (i * NG + g) * HD:(i * NG + g + 1) * HD], HD ** -0.5 if i == 0 else 1.0)

                project(k, f"dil{g}", lhs, dil_chunks(d, turn), copy_evac(lambda i, tt: nat[:, i, tt, :]), ahead=2,
                        then=dil_chunks(d, turn + 1)[0:2], after=head_rms(k, s1, f"dilnorm{g}", 2, head),
                        turn=(2, lambda i, tt, b: nat[:, i, tt, b * P:(b + 1) * P], lambda i, b: qkT[:, 4 * i + b, :]))
                units = []
                for tt in range(TT):
                    lo = tt if fold else max(0, tt - 1)
                    for h in range(8):
                        r = slice(HD * (h % 2), HD * (h % 2) + HD)
                        if fold:
                            masks = [(slope4[:, h, :], dfold[:, g - 1, :], 0, P)]
                        else:
                            masks = [(slope[:, h, :], dlo[:, 2 * P - (tt + 1 - lo) * P:], 0, (tt + 1 - lo) * P)]
                        units.append(dict(q=qkT[r, h // 2, tt * P:(tt + 1) * P],
                                          keys=qkT[r, 4 + h // 2, lo * P:(tt + 1) * P], masks=masks,
                                          values=[nat[:, 2, b, h * HD:(h + 1) * HD] for b in range(lo, tt + 1)]))

                def store(sp, out_free, g=g):
                    rows = d["folded"][g - 1].rearrange("(l j) n -> l j n", j=FOLD)
                    for j in range(TT):
                        sp.wait_ge(out_free, j + 1)
                        sp.dma_start(rows[:, j, :], o_raw[:, g, j, :]).then_inc(folded_out, 16)

                def load_back(sp, out_free):
                    sp.wait_ge(folded_out, 2 * TT * 16)
                    for f in (1, 2):
                        sp.dma_start(o_raw[:, f], d["folded"][f - 1].rearrange("(t p) n -> p t n", p=P)).then_inc(
                            folded_in, 16)

                attention(k, f"dilatt{g}", units, lambda t: o_raw[:, g, t, 0:512].rearrange("p (h d) -> p h d", h=8),
                          stats=[lambda j, a=a: o_raw[:, g, j // 8, a + j % 8:a + j % 8 + 1] for a in (512, 520)],
                          sync=store if fold else load_back)
        nmax, den = (o_raw[:, :, :, a:a + 8] for a in (512, 520))
        with ExitStack() as s1:
            diff, e, part = (k.sb(s1, f"merge_{n}", [P, NG, TT, 8]) for n in ("diff", "e", "part"))
            least, total, inv = (k.sb(s1, f"merge_{n}", [P, TT, 8]) for n in ("least", "total", "inv"))
            tmp = k.sb(s1, "merge_tmp", [P, 512])
            diff_ready, e_ready, step_d = k.sem("merge_diff"), k.sem("merge_e"), k.sem("merge_step")
            with nc.Block() as block:
                @block.scalar
                def _(act):
                    act.wait_ge(diff_ready, 1)
                    act.activation(e[:], diff[:], ACT.Exp).then_inc(e_ready, 1)

                @block.vector
                def _(dve):
                    step = Chain(dve, step_d)
                    dve.wait_ge(folded_in, 2 * 16)
                    step(dve.tensor_tensor(least[:], nmax[:, 0], nmax[:, 1], ALU.min))
                    step(dve.tensor_tensor(least[:], least[:], nmax[:, 2], ALU.min))
                    for g in range(NG):
                        ins = dve.tensor_tensor(diff[:, g], least[:], nmax[:, g], ALU.subtract)
                        if g < NG - 1:
                            step(ins)
                    ins.then_inc(diff_ready, 1)
                    dve.wait_ge(e_ready, 1)
                    for g in range(NG):
                        step(dve.tensor_tensor(part[:, g], e[:, g], den[:, g], ALU.mult))
                    step(dve.reduce_sum(total[:], part[:].rearrange("p g t h -> p t h g"), AX))
                    step(dve.reciprocal(inv[:], total[:]))
                    for g in range(NG):
                        step(dve.tensor_tensor(e[:, g], e[:, g], inv[:], ALU.mult))
                    for tt in range(TT):
                        o = k.o_dil[:, tt, :].rearrange("p (h d) -> p h d", h=8)
                        t3 = tmp[:].rearrange("p (h d) -> p h d", h=8)
                        for g in range(NG):
                            w = bc(e[:, g, tt, :], 2, HD)
                            x = o_raw[:, g, tt, 0:512].rearrange("p (h d) -> p h d", h=8)
                            step(dve.tensor_tensor(t3 if g else o, x, w, ALU.mult))
                            if g:
                                step(dve.tensor_tensor(o, o, t3, ALU.add))


def second_block(k):
    nc, d = k.nc, k.d
    k.recycle_semaphores()
    x = lambda tt: k.x1[:, tt, :]
    stage = ExitStack()
    k.weight_buffers(stage, "block2")
    with ExitStack() as s:
        h_nat = k.sb(s, "h_nat", [P, TT, DM])
        rms_rows(k, "rms1", x, lambda tt: h_nat[:, tt, :], "norm_attn", then=columns(d["w_mla"], 384, 2))
        transpose_split(k, "hT", lambda tt, b: h_nat[:, tt, b * P:(b + 1) * P], lambda b: (k.xh[:, b, :], k.xl[:, b, :]), KD)
    with ExitStack() as s:
        latent_attention(k, s)
        k.recycle_semaphores()
        dilated_attention(k, s)
        k.recycle_semaphores()
        a = k.sb(s, "branches", [P, 2, TT, DM])
        with ExitStack() as s1:
            oT = [k.sb(s1, f"oT_{x}", [P, 8, SEQ], F32R) for x in ("hi", "lo")]
            transpose_split(k, "oT", lambda tt, b: (k.o_mla if b < 4 else k.o_dil)[:, tt, (b % 4) * P:(b % 4 + 1) * P],
                            lambda b: tuple(x[:, b, :] for x in oT), 8)
            follow = [columns(d["w_o_dil"], 512), columns(d["w_gates"], 512)[0:2]]
            for i, n in enumerate(("w_o_mla", "w_o_dil")):
                project(k, n, lambda tt, c: tuple(x[:, 4 * i + c, tt * P:(tt + 1) * P] for x in oT), columns(d[n], 512),
                        copy_evac(lambda j, tt: a[:, i, tt, j * 512:(j + 1) * 512]), ahead=2, then=follow[i])
        with ExitStack() as s1:
            pre = k.sb(s1, "gate_pre", [P, 2, TT, 512])
            bg = k.sb(s1, "gate_bias", [P, 2 * DM])
            bg_in = k.sem("gate_bias_in")
            with nc.Block() as block:
                @block.sync
                def _(sp):
                    sp.dma_start(bg[:], k.vec("b_gate")).then_inc(bg_in, 16)
                    sp.wait_ge(bg_in, 16)

            def add_bias(dve, step, i, tt, bank):
                return dve.tensor_tensor(pre[:, i % 2, tt, :], bank[:], bg[:, i * 512:(i + 1) * 512], ALU.add)

            def sigmoid(act, i):
                return act.activation(pre[:, i % 2], pre[:, i % 2], ACT.Sigmoid)

            def gate(dve, step, i):
                branch, half = divmod(i, 2)
                x, y = (a[:, j, :, half * 512:(half + 1) * 512] for j in (branch, 0))
                step(dve.tensor_tensor(x, x, pre[:, i % 2], ALU.mult))
                if branch:
                    step(dve.tensor_tensor(y, y, x, ALU.add))

            project(k, "gates", k.xs_lhs, columns(d["w_gates"], 512), add_bias, ahead=2,
                    then=columns(d["w_out2"], 512), after=(4, None, sigmoid, gate))
        transpose_split(k, "merT", lambda tt, b: a[:, 0, tt, b * P:(b + 1) * P], lambda b: (k.xh[:, b, :], k.xl[:, b, :]), KD)

        def add_out(dve, step, i, tt, bank):
            o = k.x1[:, tt, i * 512:(i + 1) * 512]
            return dve.tensor_tensor(o, o, bank[:], ALU.add)

        project(k, "out2", k.xs_lhs, columns(d["w_out2"], 512), add_out, ahead=2)
    stage.close()
    k.recycle_semaphores()
    with ExitStack() as s:
        h2 = k.sb(s, "h2_nat", [P, TT, DM])
        weights, router = expert_weights(k, "e2", s), router_weights(k, "r2", G2 + E2, s)
        rms_rows(k, "rms2", x, lambda tt: h2[:, tt, :], "norm_ffn",
                 prefetch=lambda sp: first_loads(sp, router, weights, d["w_route2"], k.vec("b2"), d["gu2"], d["dn2"]))
        transpose_split(k, "h2T", lambda tt, b: h2[:, tt, b * P:(b + 1) * P], lambda b: (k.xh[:, b, :], k.xl[:, b, :]), KD)
        route(k, "r2", E2, G2, S2, router, s, d["rows"], lambda tt: h2[:, tt, :])
        experts(k, "e2", E2, S2, k.gather_sems[2:4], d["rows"], d["gu2"], d["dn2"], d["slots"][0:SLOTS2, :], weights)
        combine(k, "c2", d["slots"][0:SLOTS2, :], k.x1, 1.0, out=d["out"])


def first_block(k):
    nc, d = k.nc, k.d
    with ExitStack() as s:
        place_block1(k, s)
        stats = k.row_stats
        k.weight_buffers(s, "block1")
        project1(k, s)
        select_keys(k, s)
        state_space(k, s)
        att = k.sb(s, "att1", [P, TT, 512])
        units = []
        bias_step, bias_ready = k.sem("bias_step"), k.sem("bias_ready")
        for tt in range(TT):
            w = (tt + 1) * P
            for h in range(H1):
                r = slice(HD * (h % 2), HD * (h % 2) + HD)
                units.append(dict(q=k.ropeT[r, h // 2, tt * P:w], keys=k.ropeT[r, 4, 0:w],
                                  masks=[(k.cb("ident_b"), k.key_bias[:, tt, 0:w], 0, w)],
                                  values=[k.v[:, b, 0:HD] for b in range(tt + 1)]))
        units[(TT - 1) * H1]["wait"] = (bias_ready, 1)

        def best_of_last(dve, st):
            if st < k.best_rounds:
                k.best_round(dve, Chain(dve, bias_step, 2 * st))
            if st == k.best_rounds - 1:
                k.last_biases(dve).then_inc(bias_ready, 1)

        blank_out = k.sem("blank_out")

        def blank_slots(sp, out_free):
            first = min(E1 * S1, E2 * S2)
            spare = d["slots"][first:, :].rearrange("(n p) (a f) -> n p a f", p=P, f=256)
            for i in range(spare.shape[0]):
                sp.dma_start(spare[i], bc(k.blank[:], 1, DM // 256)).then_inc(blank_out, 16)
            sp.wait_ge(blank_out, 16 * spare.shape[0])

        attention(k, "dsa", units, lambda g: att[:, g, :].rearrange("p (h d) -> p h d", h=8), sync=blank_slots,
                  aside=best_of_last)
        cat = lambda tt, b: att[:, tt, b * P:(b + 1) * P] if b < 4 else k.y[:, tt, (b - 4) * P:(b - 3) * P]
        transpose_split(k, "mix1", cat, lambda b: (k.xh[:, b, :], k.xl[:, b, :]), KD)

        def add_mixed(dve, step, i, tt, bank):
            x = k.x1[:, tt, i * 512:(i + 1) * 512]
            step(dve.scalar_tensor_tensor(x, x, ALPHA, bank[:], ALU.mult, ALU.add))
            return row_stats(dve, stats[:, tt], k.x1[:, tt, :], i)

        project(k, "out1", k.xs_lhs, columns(d["w_out"], 512), add_mixed, ahead=2)
    k.recycle_semaphores()
    s = ExitStack()
    weights, router = expert_weights(k, "e1", s), router_weights(k, "r1", G1 + E1, s)
    layer_norm(k, "ln1", k.x1, "ln1_g", "ln1_b", stats, 
               lambda sp: first_loads(sp, router, weights, d["w_route1"], k.vec("b1"), d["gu1"], d["dn1"]))
    transpose_split(k, "x1T", lambda tt, b: k.x1[:, tt, b * P:(b + 1) * P], lambda b: (k.xh[:, b, :], k.xl[:, b, :]), KD)
    with s:
        route(k, "r1", E1, G1, S1, router, s, d["rows"], lambda tt: k.x1[:, tt, :])
        experts(k, "e1", E1, S1, k.gather_sems[0:2], d["rows"], d["gu1"], d["dn1"], d["slots"][0:SLOTS1, :], weights)
        combine(k, "c1", d["slots"][0:SLOTS1, :], k.x1, ALPHA, stats=stats)
    layer_norm(k, "ln2", k.x1, "ln2_g", "ln2_b", stats)


def program(nc, d):
    with ExitStack() as ctx:
        k = Core(nc, ctx, d)
        first_block(k)
        second_block(k)


def lay_out(a):
    f = np.float32
    A = {n: np.asarray(v) for n, v in a.items()}
    L = {n: (v[0] if v.ndim > 1 else v) for n, v in A.items() if n not in ("x", "positions_2")}
    o = {}
    x = A["x"][0]
    o["x_nat"] = x.reshape(TT, P, DM).transpose(1, 0, 2)
    o["xT"] = x.T.reshape(KD, P, SEQ).transpose(1, 0, 2)
    w = L["w_in"]
    rows = lambda m: m.reshape(-1, P, m.shape[1]).transpose(1, 0, 2)
    q, kk, vv, iq, ik, iw, z, xbc, dt = np.split(w, np.cumsum([512, 64, 64, 256, 64, 4, 512, 768]), axis=1)
    spare = np.zeros((DM, P - FEW), f)
    cols = np.concatenate([q, kk, kk, iq, ik, ik, xbc, vv, iw, dt, spare], axis=1)
    o["w_in_t"] = cols.reshape(KD, P, -1, P).transpose(2, 1, 0, 3).reshape(-1, P, KD * P)
    o["w_z"] = rows(z)
    cw = np.concatenate([L["conv_w"], L["conv_b"][None]], 0)
    o["convw"] = cw.reshape(5, 6, P).transpose(2, 1, 0)
    o["w_out"] = rows(L["w_out"])
    o["w_route1"] = rows(np.concatenate([L["w_route_group"], L["w_route_expert"]], 1))

    def expert(wg, wu, wd):
        E = wg.shape[0]
        gu = np.concatenate([wg, wu], 2).reshape(E, KD, P, 2 * FF).transpose(0, 2, 1, 3).reshape(E, P, -1)
        return gu, wd.reshape(E, 2, P, DM).transpose(0, 2, 1, 3).reshape(E, P, -1)

    o["gu1"], o["dn1"] = expert(L["w_gate"], L["w_up"], L["w_down"])
    o["gu2"], o["dn2"] = expert(L["w_gate_2"], L["w_up_2"], L["w_down_2"])
    v = {"b1": np.concatenate([L["b_route_group"], L["b_route_expert"]]),
         "b2": np.concatenate([L["b_router_group_2"], L["b_router_expert_2"]])}
    for n, width in VECS:
        if n not in v:
            v[n] = L[n] if n in L else L[n + "_2"]
    flat = np.concatenate([np.asarray(v[n]).reshape(-1) for n, _ in VECS])
    o["vecs"] = np.broadcast_to(flat[None], (P, NVEC))
    w2 = L["w_in_2"]
    o["w_mla"] = rows(w2[:, 0:MLA_COLS])
    o["w_dil"] = rows(w2[:, MLA_COLS:MLA_COLS + 9 * 512])
    o["w_gates"] = rows(w2[:, MLA_COLS + 9 * 512:])
    o["w_ukv"] = rows(L["w_ukv_2"])
    o["w_o_mla"], o["w_o_dil"], o["w_out2"] = rows(L["w_o_mla_2"]), rows(L["w_o_dil_2"]), rows(L["w_out_2"])
    o["w_route2"] = rows(np.concatenate([L["w_router_group_2"], L["w_router_expert_2"]], 1))
    o["positions"] = A["positions_2"][0].reshape(TT, P).T.astype(np.int32)
    o["consts"], o["consts_b"] = constants()
    return {n: np.ascontiguousarray(m) for n, m in o.items()}


def kernel(**inputs):
    import concourse.bacc as bacc
    from concourse.bass_utils import run_bass_kernel_spmd
    nc = bacc.Bacc("TRN2", target_bir_lowering=False, num_devices=1)
    arrays = {f"in_{n}": m for n, m in lay_out(inputs).items()}
    d = {n[3:]: nc.dram_tensor(n, m.shape, mybir.dt.from_np(m.dtype), kind="ExternalInput").ap()
         for n, m in arrays.items()}
    d["consts_b"] = d["consts_b"].bitcast(BF16)
    d["rows"] = nc.dram_tensor("token_rows", (SEQ, DM), F32, kind="Internal").ap()
    d["slots"] = nc.dram_tensor("slot_rows", (max(SLOTS1, SLOTS2), DM), F32, kind="Internal").ap()
    d["folded"] = nc.dram_tensor("folded_rows", (2, SEQ, 528), F32, kind="Internal").ap()
    d["out"] = nc.dram_tensor("out", (SEQ, DM), F32, kind="ExternalOutput").ap()
    program(nc, d)
    r = run_bass_kernel_spmd(nc, [arrays], core_ids=[0])
    return r.results[0]["out"].reshape(1, SEQ, DM)
```
